# Optimizing a Trainium2 kernel written in Bass

```python
import jax, jax.numpy as jnp
from jax import lax
import numpy as np

D_MODEL = 2048
BATCH = 1
SEQ = 512
DEPTH = 1
DEC_BATCH = 8
DEC_SEQ = 4
PAST_LEN = 2048
PAGE_SIZE = 128

HEAD_DIM = 64
N_Q_HEADS = 16
N_KV_HEADS = 4
GQA_GROUP = N_Q_HEADS // N_KV_HEADS
ATTN_WIDTH = N_Q_HEADS * HEAD_DIM
KV_WIDTH = N_KV_HEADS * HEAD_DIM
WINDOW = 128
BLOCK = WINDOW
POOL_WINDOWS = (2, 4, 8, 16)
N_POOL_GROUPS = len(POOL_WINDOWS)
POOL_GROUP_WIDTH = 256
POOL_WIDTH = N_POOL_GROUPS * POOL_GROUP_WIDTH
POOL_STATE = max(POOL_WINDOWS) - 1
MIX_WIDTH = ATTN_WIDTH + POOL_WIDTH
IN_WIDTH = ATTN_WIDTH + 2 * KV_WIDTH + POOL_WIDTH
D_FF = 4 * D_MODEL
EPS = 1e-6

kernel_name = 'hymba_pool_swa_sink_decoder'

def rmsnorm(x, g):
    xf = x.astype(jnp.float32)
    y = xf * lax.rsqrt(jnp.mean(xf * xf, axis=-1, keepdims=True) + EPS)
    return (y * g.astype(jnp.float32)).astype(x.dtype)

def alibi_slopes():
    h = jnp.arange(1, N_Q_HEADS + 1, dtype=jnp.float32)
    return jnp.exp2(-8.0 * h / N_Q_HEADS).reshape(N_KV_HEADS, GQA_GROUP)

def window_attention(q, k, v, qpos, kpos, sinks):
    lead = q.shape[:-2]
    qf = q.astype(jnp.float32).reshape(lead + (N_KV_HEADS, GQA_GROUP, HEAD_DIM))
    s = jnp.einsum('...qkgd,...skd->...kgqs', qf, k.astype(jnp.float32)) * (HEAD_DIM ** -0.5)
    dist = qpos[..., :, None] - kpos[..., None, :]
    valid = (dist >= 0) & (dist < WINDOW) & (kpos[..., None, :] >= 0)
    bias = -alibi_slopes()[:, :, None, None] * dist.astype(jnp.float32)[..., None, None, :, :]
    s = jnp.where(valid[..., None, None, :, :], s + bias, -jnp.inf)
    sink = sinks.astype(jnp.float32).reshape(N_KV_HEADS, GQA_GROUP)[:, :, None, None]
    m = jnp.maximum(jnp.max(s, axis=-1, keepdims=True), sink)
    p = jnp.exp(s - m)
    denom = jnp.sum(p, axis=-1, keepdims=True) + jnp.exp(sink - m)
    o = jnp.einsum('...kgqs,...skd->...qkgd', p / denom, v.astype(jnp.float32))
    return o.reshape(lead + (ATTN_WIDTH,)).astype(q.dtype)

def shift_blocks(b):
    return jnp.pad(b, ((0, 0), (1, 0), (0, 0), (0, 0), (0, 0)))[:, :-1]

def pool_mix(u, buf, pos0, w_pool, scale):
    n, t, _ = u.shape
    p = jnp.concatenate([buf, u], axis=1)
    pf = p.astype(jnp.float32)
    cs0 = jnp.pad(jnp.cumsum(pf, axis=1), ((0, 0), (1, 0), (0, 0)))
    uf = pf[:, POOL_STATE:]
    pos = pos0 + jnp.arange(t)
    groups = []
    for gi, w in enumerate(POOL_WINDOWS):
        lo, hi = gi * POOL_GROUP_WIDTH, (gi + 1) * POOL_GROUP_WIDTH
        upper = cs0[:, POOL_STATE + 1:POOL_STATE + 1 + t, lo:hi]
        lower = cs0[:, POOL_STATE + 1 - w:POOL_STATE + 1 - w + t, lo:hi]
        cnt = jnp.minimum(pos + 1, w).astype(jnp.float32)[:, None]
        groups.append((upper - lower) / cnt - uf[..., lo:hi])
    z = jnp.stack(groups, axis=2)
    z = jnp.einsum('ntgc,gcd->ntgd', z, w_pool.astype(jnp.float32))
    out = z.reshape(n, t, POOL_WIDTH) * scale.astype(jnp.float32)
    return out.astype(u.dtype), p[:, -POOL_STATE:]

def mixer_sublayer(x, k_buf, v_buf, pool_buf, pos0, w_in, w_out, w_pool, pool_scale, sinks, g_pre, g_post):
    n, t, _ = x.shape
    h = rmsnorm(x, g_pre)
    proj = jnp.einsum('ntd,de->nte', h, w_in)
    q = proj[..., :ATTN_WIDTH].reshape(n, t, N_Q_HEADS, HEAD_DIM)
    k = proj[..., ATTN_WIDTH:ATTN_WIDTH + KV_WIDTH].reshape(n, t, N_KV_HEADS, HEAD_DIM)
    v = proj[..., ATTN_WIDTH + KV_WIDTH:ATTN_WIDTH + 2 * KV_WIDTH].reshape(n, t, N_KV_HEADS, HEAD_DIM)
    u = proj[..., ATTN_WIDTH + 2 * KV_WIDTH:]
    if k_buf is None:
        nb = t // BLOCK
        qb = q.reshape(n, nb, BLOCK, N_Q_HEADS, HEAD_DIM)
        kb = k.reshape(n, nb, BLOCK, N_KV_HEADS, HEAD_DIM)
        vb = v.reshape(n, nb, BLOCK, N_KV_HEADS, HEAD_DIM)
        kk = jnp.concatenate([shift_blocks(kb), kb], axis=2)
        vv = jnp.concatenate([shift_blocks(vb), vb], axis=2)
        qpos = (pos0 + jnp.arange(t)).reshape(nb, BLOCK)
        kpos = qpos[:, :1] - BLOCK + jnp.arange(2 * BLOCK)[None, :]
        a = window_attention(qb, kk, vv, qpos, kpos, sinks).reshape(n, t, ATTN_WIDTH)
        new_k, new_v = k[:, -WINDOW:], v[:, -WINDOW:]
        pool_buf = jnp.zeros((n, POOL_STATE, POOL_WIDTH), u.dtype)
    else:
        kk = jnp.concatenate([k_buf.astype(k.dtype), k], axis=1)
        vv = jnp.concatenate([v_buf.astype(v.dtype), v], axis=1)
        qpos = pos0 + jnp.arange(t)
        kpos = pos0 - WINDOW + jnp.arange(WINDOW + t)
        a = window_attention(q, kk, vv, qpos, kpos, sinks)
        new_k, new_v = kk[:, -WINDOW:], vv[:, -WINDOW:]
    pl, new_pool = pool_mix(u, pool_buf.astype(u.dtype), pos0, w_pool, pool_scale)
    out = jnp.einsum('nte,ed->ntd', jnp.concatenate([a, pl], axis=-1), w_out)
    return x + rmsnorm(out, g_post), new_k, new_v, new_pool

def ffn_sublayer(x, w_up, w_down, g_pre, g_post):
    h = rmsnorm(x, g_pre)
    a = jnp.square(jax.nn.relu(jnp.einsum('ntd,df->ntf', h, w_up)))
    return x + rmsnorm(jnp.einsum('ntf,fd->ntd', a, w_down), g_post)

def setup_inputs(seed: int = 0) -> dict:
    key = jax.random.key(seed)
    ks = jax.random.split(key, 16)
    f32 = jnp.float32
    nrm = lambda k, s: jax.random.normal(k, s, f32)
    return {
        'x_prompt': nrm(ks[0], (BATCH, SEQ, D_MODEL)),
        'x_sample': nrm(ks[1], (DEC_BATCH, DEC_SEQ, D_MODEL)),
        'cache_k': nrm(ks[2], (DEPTH, DEC_BATCH, WINDOW, N_KV_HEADS, HEAD_DIM)),
        'cache_v': nrm(ks[3], (DEPTH, DEC_BATCH, WINDOW, N_KV_HEADS, HEAD_DIM)),
        'state_pool': nrm(ks[4], (DEPTH, DEC_BATCH, POOL_STATE, POOL_WIDTH)),
        'w_in': nrm(ks[5], (DEPTH, D_MODEL, IN_WIDTH)) * D_MODEL ** -0.5,
        'w_out': nrm(ks[6], (DEPTH, MIX_WIDTH, D_MODEL)) * MIX_WIDTH ** -0.5,
        'w_pool': nrm(ks[7], (DEPTH, N_POOL_GROUPS, POOL_GROUP_WIDTH, POOL_GROUP_WIDTH)) * POOL_GROUP_WIDTH ** -0.5,
        'pool_scale': 1.0 + 0.1 * nrm(ks[8], (DEPTH, POOL_WIDTH)),
        'attn_sinks': 0.5 * nrm(ks[9], (DEPTH, N_Q_HEADS)),
        'g_pre_mix': 1.0 + 0.05 * nrm(ks[10], (DEPTH, D_MODEL)),
        'g_post_mix': 1.0 + 0.05 * nrm(ks[11], (DEPTH, D_MODEL)),
        'g_pre_ffn': 1.0 + 0.05 * nrm(ks[12], (DEPTH, D_MODEL)),
        'g_post_ffn': 1.0 + 0.05 * nrm(ks[13], (DEPTH, D_MODEL)),
        'w_up': nrm(ks[14], (DEPTH, D_MODEL, D_FF)) * D_MODEL ** -0.5,
        'w_down': nrm(ks[15], (DEPTH, D_FF, D_MODEL)) * D_FF ** -0.5,
    }

def reference(x_prompt, x_sample, cache_k, cache_v, state_pool, w_in, w_out, w_pool, pool_scale, attn_sinks,
              g_pre_mix, g_post_mix, g_pre_ffn, g_post_ffn, w_up, w_down):
    xp, xs = x_prompt, x_sample
    kp_l, vp_l, pp_l, ks_l, vs_l, ps_l = [], [], [], [], [], []
    for l in range(DEPTH):
        xp, kp, vp, pp = mixer_sublayer(xp, None, None, None, 0, w_in[l], w_out[l], w_pool[l], pool_scale[l],
                                        attn_sinks[l], g_pre_mix[l], g_post_mix[l])
        xs, kn, vn, pn = mixer_sublayer(xs, cache_k[l], cache_v[l], state_pool[l], PAST_LEN, w_in[l], w_out[l],
                                        w_pool[l], pool_scale[l], attn_sinks[l], g_pre_mix[l], g_post_mix[l])
        xp = ffn_sublayer(xp, w_up[l], w_down[l], g_pre_ffn[l], g_post_ffn[l])
        xs = ffn_sublayer(xs, w_up[l], w_down[l], g_pre_ffn[l], g_post_ffn[l])
        kp_l.append(kp); vp_l.append(vp); pp_l.append(pp)
        ks_l.append(kn); vs_l.append(vn); ps_l.append(pn)
    k_prompt = jnp.stack(kp_l); v_prompt = jnp.stack(vp_l); pool_prompt = jnp.stack(pp_l)
    k_sample = jnp.stack(ks_l); v_sample = jnp.stack(vs_l); pool_sample = jnp.stack(ps_l)
    return (xp, xs, k_prompt, v_prompt, pool_prompt, k_sample, v_sample, pool_sample)


_drawn_inputs = setup_inputs


def setup_inputs(seed=0):
    import zlib

    import numpy as np

    out = dict(_drawn_inputs(seed))
    spreads = {}
    factors = {'attn_sinks': 3.278}
    for name, (base, spread) in spreads.items():
        noise = np.random.default_rng([zlib.crc32(name.encode()), seed]).standard_normal(out[name].shape)
        drawn = base * np.exp(spread * noise) if base else spread * noise
        out[name] = __import__('jax').numpy.asarray(drawn.astype(out[name].dtype))
    for name, factor in factors.items():
        out[name] = (out[name] * factor).astype(out[name].dtype)
    return out
```

```python
from contextlib import ExitStack

import concourse.bass as bass
from concourse import mybir

F32 = mybir.dt.float32
F32R = mybir.dt.float32r
I32 = mybir.dt.int32
ALU = mybir.AluOpType
ACT = mybir.ActivationFunctionType
AX = mybir.AxisListType

P = 128
EPS = 1e-6
MASKED = -1e38
RAW_SLOTS = 4
SPLIT_SLOTS = 2
UNIT_KT = 4
UNIT_N = 256
POOL_WINDOWS = (2, 4, 8, 16)


def hybrid_decoder(nc, x_prompt, x_sample, cache_k, cache_v, state_pool, w_in, w_out, w_pool, pool_scale,
                   attn_sinks, g_pre_mix, g_post_mix, g_pre_ffn, g_post_ffn, w_up, w_down,
                   y_prompt, y_sample, k_prompt, v_prompt, pool_prompt, k_sample, v_sample, pool_sample):
    _, SEQ, D = x_prompt.shape
    DEC_B, DEC_T, _ = x_sample.shape
    _, _, WINDOW, KV_HEADS, HD = cache_k.shape
    STATE = state_pool.shape[2]
    HEADS = attn_sinks.shape[1]
    GQA = HEADS // KV_HEADS
    F = w_up.shape[2]
    ND = DEC_B * DEC_T
    T = SEQ + ND
    H = T // 2
    KT = D // P
    TOK = SEQ // P + 1
    QW = HEADS * HD
    KVW = KV_HEADS * HD
    PW = w_pool.shape[1] * w_pool.shape[2]
    PAIRS = KV_HEADS // 2
    QT = QW // P
    UT = PW // P
    NKEY = WINDOW + ND
    LAST = STATE + DEC_T
    assert D == w_out.shape[1] and WINDOW == P and HD * 2 == P and T % 2 == 0 and QT + UT == KT
    assert tuple(w_in.shape[1:]) == (D, QW + 2 * KVW + PW) and PAIRS == 2 and GQA == 4 and TOK == 5

    IN_PAIRS = w_in.shape[2] // UNIT_N
    K_UNITS = KT // UNIT_KT
    IN_UNITS = IN_PAIRS * K_UNITS
    POOL_UNITS = PW // (UNIT_KT * P)
    POOL_PAIRS = len(POOL_WINDOWS)
    OUT_PAIRS = D // UNIT_N
    CHUNK = UNIT_KT * P
    CHUNKS = F // CHUNK
    UP_PAIRS = CHUNK // UNIT_N
    CHUNK_UNITS = UP_PAIRS * K_UNITS + OUT_PAIRS
    CHUNK_PAIRS = UP_PAIRS + OUT_PAIRS
    CHUNK_TILES = 2 * CHUNK_PAIRS
    U_POOL = IN_UNITS
    U_OUT = U_POOL + POOL_UNITS
    U_FFN = U_OUT + OUT_PAIRS * K_UNITS
    P_POOL = IN_PAIRS
    P_OUT = P_POOL + POOL_PAIRS
    P_FFN = P_OUT + OUT_PAIRS
    N_UNITS = U_FFN + CHUNKS * CHUNK_UNITS

    tok_rows = [min(P, T - c * P) for c in range(TOK)]

    def units_of(w):
        return w.rearrange("(u k p) n -> u p k n", k=UNIT_KT, p=P)

    w_in_v, w_out_v, w_up_v, w_down_v = units_of(w_in[0]), units_of(w_out[0]), units_of(w_up[0]), units_of(w_down[0])
    w_pool_v = units_of(w_pool[0].rearrange("g c d -> (g c) d"))

    with ExitStack() as ctx:
        def sb(name, shape, dt=F32, scope=ctx):
            return scope.enter_context(nc.sbuf_tensor(name, shape, dt))

        def sem(name):
            return ctx.enter_context(nc.semaphore(name))

        acts_hi = sb("acts_hi", [P, KT, T], F32R)
        acts_lo = sb("acts_lo", [P, KT, T], F32R)
        w_raw = sb("w_raw", [P, RAW_SLOTS, UNIT_KT * UNIT_N])
        w_hi = sb("w_hi", [P, SPLIT_SLOTS, UNIT_KT * UNIT_N], F32R)
        w_lo = sb("w_lo", [P, SPLIT_SLOTS, UNIT_KT * UNIT_N], F32R)
        gemm_scale = sb("gemm_scale", [P, T])
        norm_scale = sb("norm_scale", [P, T])
        sq_sum = sb("sq_sum", [P, T])
        sq_tmp = sb("sq_tmp", [P, 2 * T])
        diag = sq_tmp[:, 0:TOK * P].rearrange("p (c m) -> p c m", c=TOK)
        vecs = sb("vecs", [P, 4 * KT + UT])
        ident = sb("ident", [P, P])
        ones = sb("ones", [P, P])
        sink_all = sb("sink_all", [P, HEADS])
        neg_sink = sb("neg_sink", [P, HEADS])
        dec_consts = sb("dec_consts", [P, 2 * PAIRS])
        neg_dec_sink = sb("neg_dec_sink", [P, 2, PAIRS])
        dec_sink = sb("dec_sink", [P, 2, PAIRS])
        dec_slope = dec_consts[:, PAIRS:2 * PAIRS]
        row_i = sb("row_i", [P, 3], I32)
        row_t = sb("row_t", [P, 2])
        ss = sb("ss", [P, TOK])
        var = sb("var", [P, TOK])
        inv = sb("inv", [P, TOK])
        root = sb("root", [P, TOK])
        newton = sb("newton", [P, TOK])
        rstd = sb("rstd", [P, TOK])
        g_pre, g_post = vecs[:, 0:KT], vecs[:, KT:2 * KT]
        g_ffn, g_last = vecs[:, 2 * KT:3 * KT], vecs[:, 3 * KT:4 * KT]
        p_scale = vecs[:, 4 * KT:4 * KT + UT]

        banks = ctx.enter_context(nc.psum_tensor("banks", [P, 8, 512], F32))

        def slot(s):
            return banks[:, 2 * s:2 * s + 2, 0:H]

        def flat(b, n):
            return banks[:, b:b + (n + 511) // 512, :].rearrange("p b n -> p (b n)")[:, 0:n]

        mixer = ExitStack()
        qT = sb("qT", [P, QT, T], F32, mixer)
        kT = sb("kT", [P, PAIRS, T], F32, mixer)
        vT = sb("vT", [P, PAIRS, T], F32, mixer)
        pooling = ExitStack()
        uT = sb("uT", [P, UT, T], F32, pooling)
        start = ExitStack()
        x_tok = sb("x_tok", [P, TOK, D], F32, start)
        vec_rows = sb("vec_rows", [4 * KT + UT, P], F32, start)
        sink_row = sb("sink_row", [1, HEADS], F32, start)
        sink_hh = sb("sink_hh", [2 * GQA, PAIRS], F32, start)
        head_rows = sb("head_rows", [2 * GQA, P], F32, start)
        slope_row = sb("slope_row", [1, P], F32, start)
        slope_pair = sb("slope_pair", [1, PAIRS], F32, start)
        start.close()
        u_ext = sb("u_ext", [P, UT, DEC_B, LAST], F32, pooling)
        run_a = sb("run_a", [P, UT, SEQ], F32, pooling)
        run_b = sb("run_b", [P, UT - 2, SEQ], F32, pooling)
        z_dec = sb("z_dec", [P, UT, ND], F32, pooling)
        edge = sb("edge", [P, len(POOL_WINDOWS), 16], F32, pooling)
        u_tok = sb("u_tok", [ND, 2, PW], F32, pooling)
        pooling.close()
        bias = sb("bias", [P, 2 * WINDOW], F32, mixer)
        dec_bias = sb("dec_bias", [P, 2, NKEY], F32, mixer)
        dec_pen = sb("dec_pen", [P, 2, NKEY], F32, mixer)
        probs = sb("probs", [P, 2, GQA, 2 * WINDOW], F32, mixer)
        probs_T = sb("probs_T", [P, 2, GQA * 2, P], F32, mixer)
        v_tok = sb("v_tok", [P, TOK - 1, KVW], F32, mixer)
        kv_dec = sb("kv_dec", [ND, 2, KVW], F32, mixer)
        k_tok = sb("k_tok", [P, KVW], F32, mixer)
        attn_tok = sb("attn_tok", [P, QW], F32, mixer)
        old_k = sb("old_k", [P, DEC_B, KVW], F32, mixer)
        old_v = sb("old_v", [P, DEC_B, KVW], F32, mixer)
        old_kT = sb("old_kT", [P, DEC_B * PAIRS, P], F32, mixer)
        q_blocks = sb("q_blocks", [P, DEC_B * PAIRS, 2 * GQA * DEC_T], F32, mixer)
        dec_probs = sb("dec_probs", [P, 4, NKEY], F32, mixer)
        dec_PT = sb("dec_PT", [P, 4, P], F32, mixer)
        dec_PT_new = sb("dec_PT_new", [ND, 4, P], F32, mixer)
        stats = sb("stats", [P, 2, 8, GQA], F32, mixer)
        dec_stats = sb("dec_stats", [P, 8, 4], F32, mixer)
        mixer.close()
        x1T = sb("x1T", [P, KT, T])
        relu_buf = sb("relu_buf", [P, T])
        again = ExitStack()
        x_tok2 = sb("x_tok2", [P, TOK, D], F32, again)
        again.close()
        y_sum = sb("y_sum", [P, KT, T])
        mlp_hi = sb("mlp_hi", [P, UNIT_KT, T], F32R)
        mlp_lo = sb("mlp_lo", [P, UNIT_KT, T], F32R)

        vec_landed = [sem(f"vec_landed{i}") for i in range(7)]
        x_landed = [sem(f"x_landed{i}") for i in range(TOK)]
        x2_landed = [sem(f"x2_landed{i}") for i in range(TOK)]
        w_landed = [sem(f"w_landed{i}") for i in range(RAW_SLOTS)]
        state_landed = sem("state_landed")
        cache_landed = [sem(f"cache_landed{i}") for i in range(2)]
        hi_split = sem("hi_split")
        lo_split = sem("lo_split")
        unit_used = sem("unit_used")
        first_done = sem("first_done")
        even_group_done = sem("even_group_done")
        tile_read = sem("tile_read")
        consts = sem("consts")
        vecs_turned = sem("vecs_turned")
        vecs_ready = sem("vecs_ready")
        small = sem("small")
        squares = sem("squares")
        x_turned = sem("x_turned")
        h_hi = sem("h_hi")
        h_lo = sem("h_lo")
        inv_ready = sem("inv_ready")
        root_ready = sem("root_ready")
        diag_ready = sem("diag_ready")
        spread = sem("spread")
        scale_ready = sem("scale_ready")
        sums_turned = sem("sums_turned")
        sq_ready = sem("sq_ready")
        sq_added = sem("sq_added")
        sum_clear = sem("sum_clear")
        state_turned = sem("state_turned")
        u_turned = sem("u_turned")
        u_copied = sem("u_copied")
        state_copied = sem("state_copied")
        z_ready = sem("z_ready")
        z_hi = sem("z_hi")
        z_lo = sem("z_lo")
        mix_hi = sem("mix_hi")
        edge_ready = sem("edge_ready")
        bias_ready = sem("bias_ready")
        kv_turned = sem("kv_turned")
        kv_copied = sem("kv_copied")
        scores = sem("scores")
        scores_read = sem("scores_read")
        shift_ready = sem("shift_ready")
        exps = sem("exps")
        probs_turned = sem("probs_turned")
        probs_copied = sem("probs_copied")
        mixed = sem("mixed")
        mixed_read = sem("mixed_read")
        rows_turned = sem("rows_turned")
        rows_hi = sem("rows_hi")
        rows_lo = sem("rows_lo")
        old_k_turned = sem("old_k_turned")
        old_k_act = sem("old_k_act")
        old_k_dve = sem("old_k_dve")
        q_ready = sem("q_ready")
        dec_scores = sem("dec_scores")
        dec_shift = sem("dec_shift")
        dec_exps = sem("dec_exps")
        dec_norm = sem("dec_norm")
        dec_turned = sem("dec_turned")
        dec_copied = sem("dec_copied")
        dec_mixed = sem("dec_mixed")
        dec_hi = sem("dec_hi")
        dec_lo = sem("dec_lo")
        x1_ready = sem("x1_ready")
        y_clear = sem("y_clear")
        relu_sq = sem("relu_sq")
        mlp_hi_ready = sem("mlp_hi_ready")
        mlp_lo_ready = sem("mlp_lo_ready")
        y_ready = sem("y_ready")
        y_turned = sem("y_turned")
        y_copied = [sem("y_copied_act"), sem("y_copied_dve")]
        y_stored = [sem(f"y_stored{i}") for i in range(8)]
        kept = sem("kept")
        u_stored = sem("u_stored")
        stored = sem("stored")

        N_STORED = 4

        def num(k, v, per=1):
            return k + v * per if not isinstance(v, int) or v else k

        def dec_out(half, h):
            w = 2 * GQA * DEC_T
            src = banks[half * HD:(half + 1) * HD, 5, :].rearrange("d (b pair c) -> d pair b c", b=DEC_B, pair=PAIRS)[
                :, :, :, half * GQA * DEC_T + h * DEC_T:half * GQA * DEC_T + (h + 1) * DEC_T]
            r = slice((h % 2) * HD, (h % 2 + 1) * HD)
            e = half * 2 + h // 2

            def dst(t):
                return t[r, 0:QT, SEQ:T].rearrange("d (pair e) (b t) -> d e pair b t", pair=PAIRS, t=DEC_T)[:, e]
            return src, dst(acts_hi), dst(acts_lo)

        def pool_z(dve, step, run, g):
            w, e0 = POOL_WINDOWS[g], 2 * g
            step(nc.vector.tensor_tensor(run(g)(e0, e0 + 2, 0, 16), run(g)(e0, e0 + 2, 0, 16),
                                         edge[:, g:g + 1, :].broadcast_to([P, 2, 16]), ALU.mult))
            nc.vector.scalar_tensor_tensor(out=run(g)(e0, e0 + 2, 0, SEQ), in0=run(g)(e0, e0 + 2, 0, SEQ), scalar=1.0 / w,
                                           in1=uT[:, e0:e0 + 2, 0:SEQ], op0=ALU.mult, op1=ALU.subtract).then_inc(z_ready, 1)

        block = ctx.enter_context(nc.Block())

        @block.sync
        def _(sp):
            rows = [(g_pre_mix, 0, KT), (g_post_mix, KT, KT), (g_pre_ffn, 2 * KT, KT), (g_post_ffn, 3 * KT, KT),
                    (pool_scale, 4 * KT, UT)]
            for i, (vec, at, n) in enumerate(rows):
                sp.dma_start(vec_rows[at:at + n, :], vec[0].rearrange("(k p) -> k p", p=P)).then_inc(vec_landed[i], 16)
            sp.dma_start(sink_row[:], attn_sinks).then_inc(vec_landed[5], 16)
            with nc.allow_non_contiguous_dma("16 sinks, by head within a pair of groups"):
                sp.dma_start(sink_hh[:], attn_sinks[0].rearrange("(pair hh) -> hh pair", pair=PAIRS)).then_inc(vec_landed[6], 16)
            for c in range(TOK - 1):
                sp.dma_start(x_tok[:, c, :], x_prompt[0, c * P:(c + 1) * P, :]).then_inc(x_landed[c], 16)
            sp.dma_start(x_tok[0:ND, TOK - 1, :], x_sample.rearrange("b t d -> (b t) d")).then_inc(x_landed[TOK - 1], 16)

            def load(k, v, src):
                if k >= RAW_SLOTS or not isinstance(v, int):
                    sp.wait_ge(lo_split, num(k - RAW_SLOTS + 1, v, 4))
                s = k % RAW_SLOTS
                sp.dma_start(w_raw[:, s, :].rearrange("p (k n) -> p k n", k=UNIT_KT), src).then_inc(w_landed[s], 16)

            for kq in range(K_UNITS):
                load(kq, 0, w_in_v[kq, :, :, 0:UNIT_N])
            with sp.Fori(1, IN_PAIRS) as pair:
                for kq in range(K_UNITS):
                    load(kq, pair, w_in_v[kq, :, :, bass.ts(pair, UNIT_N)])
            for j in range(POOL_UNITS):
                load(U_POOL + j, 0, w_pool_v[j])
            with sp.Fori(0, OUT_PAIRS) as pair:
                for kq in range(K_UNITS):
                    load(U_OUT + kq, pair, w_out_v[kq, :, :, bass.ts(pair, UNIT_N)])
            with sp.Fori(0, CHUNKS) as c:
                for b in range(UP_PAIRS):
                    for kq in range(K_UNITS):
                        load(U_FFN + b * K_UNITS + kq, c * (CHUNK_UNITS // 4),
                             w_up_v[kq, :, :, bass.ds(c * CHUNK + b * UNIT_N, UNIT_N)])
                for n in range(OUT_PAIRS):
                    load(U_FFN + UP_PAIRS * K_UNITS + n, c * (CHUNK_UNITS // 4),
                         w_down_v[bass.ds(c, 1), :, :, n * UNIT_N:(n + 1) * UNIT_N].rearrange("o p k n -> (o p) k n"))

            for kg in range(KT // 4):
                for c in range(TOK):
                    o = kg * TOK + c
                    sp.wait_ge(y_copied[o % 2], o // 2 + 1)
                    dst = (y_prompt[0, c * P:(c + 1) * P, :] if c < TOK - 1 else y_sample.rearrange("b t d -> (b t) d"))
                    sp.dma_start(dst[:, kg * 512:(kg + 1) * 512],
                                 w_raw[0:tok_rows[c], :, :].rearrange("p s n -> p (s n)")[:, (o % 8) * 512:(o % 8 + 1) * 512]
                                 ).then_inc(y_stored[o % 8], 16)
            for i in range(8):
                sp.wait_ge(y_stored[i], 16 * len(range(i, TOK * KT // 4, 8)))
            sp.wait_ge(kept, 16 * 3)
            sp.wait_ge(u_stored, 16 * 2)
            sp.wait_ge(stored, 16 * N_STORED)

        @block.gpsimd
        def _(gp):
            nc.gpsimd.memset(ident[:], 0.0).then_inc(consts, 1)
            nc.gpsimd.memset(ones[:], 1.0).then_inc(consts, 1)
            nc.gpsimd.memset(ss[:], 1.0).then_inc(consts, 1)
            nc.gpsimd.memset(head_rows[:], 1.0).then_inc(consts, 1)
            for hh in range(2 * GQA):
                nc.gpsimd.memset(slope_row[:].rearrange("o (b hh t) -> o b hh t", b=4, t=DEC_T)[:, :, hh, :],
                                 2.0 ** (-8.0 * (hh + 1) / HEADS)).then_inc(consts, 1)
            for pair in range(PAIRS):
                nc.gpsimd.memset(slope_pair[:, pair:pair + 1], 2.0 ** (-8.0 * 2 * GQA * pair / HEADS)).then_inc(consts, 1)
            nc.gpsimd.iota(row_i[:, 0:1], pattern=[[0, 1]], base=0, channel_multiplier=1).then_inc(consts, 1)
            n = 5 + 2 * GQA + PAIRS
            gp.wait_ge(consts, n)
            nc.gpsimd.affine_select(out=ident[:], in_=ident[:], compare_op=ALU.not_equal, fill=1.0, base=0,
                                    pattern=[[-1, P]], channel_multiplier=1).then_inc(consts, 1)
            hr = head_rows[:].rearrange("h (b hh t) -> h b hh t", b=4, t=DEC_T)
            nc.gpsimd.affine_select(out=hr, in_=hr, compare_op=ALU.is_equal, fill=0.0, base=0,
                                    pattern=[[0, 4], [1, 2 * GQA], [0, DEC_T]], channel_multiplier=-1).then_inc(consts, 1)

            gp.wait_ge(x_turned, KT)
            nc.gpsimd.memset(edge[:], 1.0).then_inc(edge_ready, 1)
            gp.wait_ge(edge_ready, 1)
            n_edge = 1
            for g, w in enumerate(POOL_WINDOWS):
                for t in range(w - 1):
                    nc.gpsimd.memset(edge[:, g, t:t + 1], float(w) / (t + 1)).then_inc(edge_ready, 1)
                    n_edge += 1

            gp.wait_ge(z_lo, len(POOL_WINDOWS) + 1)
            gp.wait_ge(z_hi, len(POOL_WINDOWS) + 1)
            gp.wait_ge(u_stored, 32)
            nc.gpsimd.iota(bias[:], pattern=[[1, 2 * WINDOW]], base=-WINDOW, channel_multiplier=-1,
                           allow_small_or_imprecise_dtypes=True).then_inc(bias_ready, 1)
            gp.wait_ge(bias_ready, 1)
            nc.gpsimd.affine_select(out=bias[:], in_=bias[:], compare_op=ALU.is_ge, fill=MASKED, base=WINDOW,
                                    pattern=[[-1, 2 * WINDOW]], channel_multiplier=1).then_inc(bias_ready, 1)
            gp.wait_ge(bias_ready, 2)
            nc.gpsimd.affine_select(out=bias[:], in_=bias[:], compare_op=ALU.is_gt, fill=MASKED, base=0,
                                    pattern=[[1, 2 * WINDOW]], channel_multiplier=-1).then_inc(bias_ready, 1)
            nc.gpsimd.iota(dec_bias[:, 0, 0:WINDOW], pattern=[[1, WINDOW]], base=-WINDOW, channel_multiplier=0,
                           allow_small_or_imprecise_dtypes=True).then_inc(bias_ready, 1)
            nc.gpsimd.iota(dec_bias[:, 0, WINDOW:NKEY], pattern=[[0, DEC_B], [1, DEC_T]], base=0, channel_multiplier=0,
                           allow_small_or_imprecise_dtypes=True).then_inc(bias_ready, 1)
            nc.gpsimd.iota(dec_pen[:, 0, WINDOW:NKEY], pattern=[[1, DEC_B], [0, DEC_T]], base=0, channel_multiplier=0,
                           allow_small_or_imprecise_dtypes=True).then_inc(bias_ready, 1)

            nc.gpsimd.memset(q_blocks[:], 0.0).then_inc(q_ready, 1)
            gp.wait_ge(q_ready, 1)
            gp.wait_ge(tile_read, 2 * IN_PAIRS)
            for pair in range(PAIRS):
                for half in range(2):
                    r = slice(half * HD, (half + 1) * HD)
                    w = GQA * DEC_T
                    dst = q_blocks[r, :, half * w:(half + 1) * w].rearrange(
                        "d (b pair) (h t) -> d pair h b t", pair=PAIRS, t=DEC_T)[:, pair]
                    src = qT[r, pair * GQA:(pair + 1) * GQA, SEQ:T].rearrange("d h (b t) -> d h b t", t=DEC_T)
                    nc.gpsimd.tensor_copy(dst, src).then_inc(q_ready, 1)
                    gp.wait_ge(q_ready, 2 + pair * 2 + half)

            def clear_sum(n):
                if n > 0:
                    gp.wait_ge(sums_turned, n)
                nc.gpsimd.memset(sq_sum[:], 0.0).then_inc(sum_clear, 1)
                gp.wait_ge(sum_clear, n + 1)

            def add(count, par):
                gp.wait_ge(sq_ready, count + 1)
                gp.wait_ge(sq_added, count) if not isinstance(count, int) or count else None
                nc.gpsimd.tensor_tensor(sq_sum[:], sq_sum[:], sq_tmp[:, par * T:(par + 1) * T], ALU.add).then_inc(sq_added, 1)

            clear_sum(0)
            for m in range(4):
                add(m, m % 2)
            with gp.Fori(1, KT // 4) as i:
                for m in range(4):
                    add(i * 4 + m, m % 2)
            clear_sum(1)
            for kt in range(KT):
                add(KT + kt, kt % 2)
            gp.wait_ge(x_turned, 2 * KT)
            nc.gpsimd.memset(y_sum[:], 0.0).then_inc(y_clear, 1)
            clear_sum(2)
            for n in range(KT):
                add(2 * KT + n, n % 2)

        @block.scalar
        def _(act):
            def split(k, v=0):
                act.wait_ge(w_landed[k % RAW_SLOTS], num(16 * (k // RAW_SLOTS + 1), v, 16))
                if k >= SPLIT_SLOTS or not isinstance(v, int):
                    act.wait_ge(unit_used, num(k - SPLIT_SLOTS + 1, v, 4))
                nc.scalar.activation(w_hi[:, k % SPLIT_SLOTS, :], w_raw[:, k % RAW_SLOTS, :], ACT.Copy).then_inc(hi_split, 1)

            def take_root(n):
                act.wait_ge(inv_ready, n + 1)
                nc.scalar.activation(root[:], inv[:], ACT.Sqrt).then_inc(root_ready, 1)

            for c in range(TOK):
                r = tok_rows[c]
                act.wait_ge(x_landed[c], 16)
                if c == 0:
                    act.wait_ge(consts, 3)
                else:
                    act.wait_ge(squares, c)
                nc.scalar.activation(acts_lo[0:r, 0:4, 0:512], x_tok[0:r, c, :].rearrange("p (a b) -> p a b", a=4), ACT.Square,
                                     accum_out=ss[0:r, c:c + 1]).then_inc(squares, 1)
            act.wait_ge(vecs_ready, 1)
            take_root(0)
            for kt in range(KT):
                act.wait_ge(x_turned, kt + 1)
                nc.scalar.activation(acts_hi[:, kt, :], flat(2 * (kt % 4), T), ACT.Copy, scale=g_pre[:, kt:kt + 1]).then_inc(h_hi, 1)
                if kt in (2, 6):
                    split(kt // 4)
            act.wait_ge(x_turned, KT)
            act.wait_ge(vecs_turned, 1)
            act.dma_start(run_a[0:DEC_B * STATE, 0:2, :].rearrange("p a n -> p (a n)"),
                          state_pool[0].rearrange("b s c -> (b s) c")).then_inc(state_landed, 16)
            act.dma_start(k_sample[0, :, 0:WINDOW - DEC_T].rearrange("b w h d -> b (w h d)"),
                          cache_k[0, :, DEC_T:WINDOW].rearrange("b w h d -> b (w h d)")).then_inc(kept, 16)
            act.dma_start(v_sample[0, :, 0:WINDOW - DEC_T].rearrange("b w h d -> b (w h d)"),
                          cache_v[0, :, DEC_T:WINDOW].rearrange("b w h d -> b (w h d)")).then_inc(kept, 16)
            act.dma_start(pool_sample[0, :, 0:STATE - DEC_T].rearrange("b s c -> b (s c)"),
                          state_pool[0, :, DEC_T:STATE].rearrange("b s c -> b (s c)")).then_inc(kept, 16)
            for u in range(2, 8):
                split(u)
            with act.Fori(1, IN_UNITS // 8) as i:
                for k in range(8):
                    split(k, i * 2)
            split(U_POOL)

            act.wait_ge(u_turned, 1)
            nc.scalar.activation(u_tok[0:STATE, 0, :], flat(2, PW)[0:STATE], ACT.Copy).then_inc(u_copied, 1)
            nc.scalar.activation(u_tok[0:ND, 1, :], flat(4, PW)[0:ND], ACT.Copy).then_inc(u_copied, 1)
            act.wait_ge(u_copied, 2)
            act.dma_start(pool_prompt[0, 0], u_tok[0:STATE, 0, :]).then_inc(u_stored, 16)
            act.dma_start(pool_sample[0, :, STATE - DEC_T:STATE],
                          u_tok[0:ND, 1, :]).then_inc(u_stored, 16)
            act.wait_ge(z_ready, 1)
            nc.scalar.activation(acts_hi[:, 0:UT, SEQ:T], z_dec[:], ACT.Copy).then_inc(z_hi, 1)
            for g in range(len(POOL_WINDOWS)):
                act.wait_ge(z_ready, g + 2)
                z = (run_a[:, 2 * g:2 * g + 2, :] if g % 2 == 0 else run_b[:, 2 * g - 2:2 * g, :])
                nc.scalar.activation(acts_hi[:, 2 * g:2 * g + 2, 0:SEQ], z, ACT.Copy).then_inc(z_hi, 1)
            act.wait_ge(z_lo, len(POOL_WINDOWS) + 1)
            act.wait_ge(u_stored, 32)
            act.dma_start(old_k[:], cache_k[0].rearrange("b w h d -> w b (h d)")).then_inc(cache_landed[0], 16)
            act.dma_start(old_v[:], cache_v[0].rearrange("b w h d -> w b (h d)")).then_inc(cache_landed[1], 16)
            for g in range(POOL_PAIRS):
                if g % 2 == 0:
                    split(U_POOL + g // 2 + 1)
                for nt in range(2):
                    m = 2 * g + nt
                    if nt == 0:
                        act.wait_ge(first_done, P_POOL + g + 1)
                    elif g % 2 == 0:
                        act.wait_ge(even_group_done, g // 2 + 1)
                    else:
                        act.wait_ge(unit_used, U_POOL + g // 2 + 1)
                    out = acts_hi[:, QT + m, :].rearrange("p (h t) -> p h t", h=2)
                    nc.scalar.activation(out, slot((g % 2) * 2 + nt), ACT.Copy, scale=p_scale[:, m:m + 1]).then_inc(mix_hi, 1)

            act.wait_ge(kv_turned, 1)
            nc.scalar.activation(v_tok[:].rearrange("p b n -> p (b n)"), flat(0, (TOK - 1) * KVW), ACT.Copy).then_inc(kv_copied, 1)
            act.wait_ge(kv_copied, 3)
            act.dma_start(k_prompt[0, 0].rearrange("w h d -> w (h d)"), k_tok[:]).then_inc(stored, 16)
            for i, dst in enumerate((k_sample, v_sample)):
                act.dma_start(dst[0, :, WINDOW - DEC_T:WINDOW].rearrange("b t h d -> b t (h d)"), kv_dec[:, i, :]).then_inc(stored, 16)
            act.dma_start(v_prompt[0, 0].rearrange("w h d -> w (h d)"), v_tok[:, TOK - 2, :]).then_inc(stored, 16)

            def exponentials(s):
                blk, g = divmod(s, KV_HEADS)
                lo = WINDOW if blk == 0 else 0
                act.wait_ge(shift_ready, s + 1)
                for h in range(GQA):
                    nc.scalar.activation(probs[:, s % 2, h, lo:], probs[:, s % 2, h, lo:], ACT.Exp,
                                         bias=stats[:, s % 2, 0, h:h + 1], accum_out=stats[:, s % 2, 2, h:h + 1]).then_inc(exps, 1)
                nc.scalar.activation(stats[:, s % 2, 3, :], stats[:, s % 2, 1, :], ACT.Exp).then_inc(exps, 1)

            def rows_high(qb, r, n):
                act.wait_ge(rows_turned, n + 1)
                nc.scalar.activation(acts_hi[:, 4 * r:4 * r + 4, qb * P:(qb + 1) * P],
                                     banks[:, 7, :].rearrange("p (a q) -> p a q", a=4), ACT.Copy).then_inc(rows_hi, 1)

            steps = (TOK - 1) * KV_HEADS
            exponentials(0)
            for s in range(steps):
                blk = s // KV_HEADS
                if s + 1 < steps:
                    exponentials(s + 1)
                act.wait_ge(probs_turned, s + 1)
                if s >= 2:
                    act.wait_ge(mixed, s - 1)
                halves = 1 if blk == 0 else 2
                nc.scalar.activation(probs_T[:, s % 2, 0:GQA * halves, :].rearrange("p a q -> p (a q)"),
                                     flat(4, GQA * halves * P), ACT.Copy).then_inc(probs_copied, 1)
                if s % KV_HEADS == 0 and s > 0:
                    rows_high(blk - 1, 0, 2 * (blk - 1))
                    rows_high(blk - 1, 1, 2 * (blk - 1) + 1)
            rows_high(TOK - 2, 0, 2 * (TOK - 2))
            rows_high(TOK - 2, 1, 2 * (TOK - 2) + 1)

            for r in range(2):
                act.wait_ge(old_k_turned, r + 1)
                nc.scalar.activation(old_kT[:, 4 * r:4 * r + 4, :].rearrange("p a k -> p (a k)"), banks[:, r, :],
                                     ACT.Copy).then_inc(old_k_act, 1)
            act.wait_ge(dec_shift, 1)
            for ck in range(4):
                nc.scalar.activation(dec_probs[:, ck, :], dec_probs[:, ck, :], ACT.Exp, bias=dec_stats[:, 0, ck:ck + 1],
                                     accum_out=dec_stats[:, 2, ck:ck + 1]).then_inc(dec_exps, 1)
            nc.scalar.activation(dec_stats[:, 3, :], dec_stats[:, 1, :], ACT.Exp).then_inc(dec_exps, 1)
            act.wait_ge(dec_turned, 1)
            nc.scalar.activation(dec_PT[:].rearrange("p a r -> p (a r)"), banks[:, 6, :], ACT.Copy).then_inc(dec_copied, 1)
            act.wait_ge(dec_mixed, 1)
            for half in range(2):
                for h in range(GQA):
                    src, dst_hi, _ = dec_out(half, h)
                    nc.scalar.activation(dst_hi, src, ACT.Copy).then_inc(dec_hi, 1)
            act.wait_ge(dec_lo, 2 * GQA)
            act.wait_ge(mixed_read, steps)
            act.wait_ge(stored, 16 * N_STORED)
            for c in range(TOK - 1):
                act.dma_start(x_tok2[:, c, :], x_prompt[0, c * P:(c + 1) * P, :]).then_inc(x2_landed[c], 16)
            act.dma_start(x_tok2[0:ND, TOK - 1, :], x_sample.rearrange("b t d -> (b t) d")).then_inc(x2_landed[TOK - 1], 16)

            def square(src, count, par):
                if not isinstance(count, int) or count >= 2:
                    act.wait_ge(sq_added, count - 1)
                nc.scalar.activation(sq_tmp[:, par * T:(par + 1) * T].rearrange("p (h t) -> p h t", h=2), src,
                                     ACT.Square).then_inc(sq_ready, 1)

            def out_pair(k, v, pair_k, pair_v, count):
                for kq in range(K_UNITS):
                    split(k + kq + 1, v)
                for nt in range(2):
                    if nt == 0:
                        act.wait_ge(first_done, num(pair_k + 1, pair_v))
                    else:
                        act.wait_ge(unit_used, num(k + K_UNITS, v, 4))
                    square(slot((pair_k % 2) * 2 + nt), count + nt, nt)

            for b in range(2):
                out_pair(U_OUT + b * K_UNITS, 0, P_OUT + b, 0, 2 * b)
            with act.Fori(1, OUT_PAIRS // 2) as i:
                for b in range(2):
                    out_pair(U_OUT + b * K_UNITS, i * 2, P_OUT + b, i * 2, i * 4 + 2 * b)

            take_root(1)
            act.wait_ge(spread, 2)
            for kt in range(KT):
                act.wait_ge(x1_ready, kt + 1)
                nc.scalar.activation(acts_hi[:, kt, :], x1T[:, kt, :], ACT.Copy, scale=g_ffn[:, kt:kt + 1]).then_inc(h_hi, 1)
                square(x1T[:, kt, :].rearrange("p (h t) -> p h t", h=2), KT + kt, kt % 2)
            take_root(2)

            def chunk(c, last=False):
                v = c * (CHUNK_UNITS // 4)
                for b in range(UP_PAIRS):
                    for kq in range(K_UNITS):
                        split(U_FFN + b * K_UNITS + kq + 1, v)
                    for nt in range(2):
                        j = 2 * b + nt
                        act.wait_ge(tile_read, num(2 * P_FFN + j + 1, c, CHUNK_TILES))
                        nc.scalar.activation(mlp_hi[:, j, :], relu_buf[:], ACT.Square).then_inc(mlp_hi_ready, 1)
                for n in range(OUT_PAIRS):
                    k = U_FFN + UP_PAIRS * K_UNITS + n + 1
                    if not last or n + 1 < OUT_PAIRS:
                        split(k, v)
                    if last:
                        for nt in range(2):
                            m = 2 * n + nt
                            act.wait_ge(tile_read, num(2 * P_FFN + 2 * UP_PAIRS + m + 1, c, CHUNK_TILES))
                            square(y_sum[:, m, :].rearrange("p (h t) -> p h t", h=2), 2 * KT + m, m % 2)

            with act.Fori(0, CHUNKS - 1) as c:
                chunk(c)
            chunk(CHUNKS - 1, last=True)
            take_root(3)
            for kg in range(KT // 4):
                for c in range(TOK):
                    o = kg * TOK + c
                    if o % 2 == 0:
                        act.wait_ge(y_turned, o + 1)
                        if o >= 8:
                            act.wait_ge(y_stored[o % 8], 16 * (o // 8))
                        r = tok_rows[c]
                        nc.scalar.activation(w_raw[0:r].rearrange("p s n -> p (s n)")[:, (o % 8) * 512:(o % 8 + 1) * 512],
                                             banks[0:r, o % 8, :], ACT.Copy).then_inc(y_copied[0], 1)

        @block.vector
        def _(dve):
            chained = [0]

            def step(ins):
                ins.then_inc(small, 1)
                chained[0] += 1
                dve.wait_ge(small, chained[0])

            def split(k, v=0):
                dve.wait_ge(hi_split, num(k + 1, v, 4))
                nc.vector.tensor_tensor(w_lo[:, k % SPLIT_SLOTS, :], w_raw[:, k % RAW_SLOTS, :],
                                        w_hi[:, k % SPLIT_SLOTS, :].bitcast(F32), ALU.subtract).then_inc(lo_split, 1)

            def row_scales(n, target):
                if n == 0:
                    dve.wait_ge(squares, TOK)
                else:
                    dve.wait_ge(sums_turned, n)
                    nc.vector.tensor_copy(ss[:, 0:TOK - 1], banks[:, 6, 0:TOK - 1])
                    step(nc.vector.tensor_copy(ss[0:ND, TOK - 1:TOK], banks[0:ND, 6, TOK - 1:TOK]))
                step(nc.vector.tensor_scalar(var[:], ss[:], 1.0 / D, EPS, ALU.mult, ALU.add))
                nc.vector.reciprocal(inv[:], var[:]).then_inc(inv_ready, 1)
                dve.wait_ge(root_ready, n + 1)
                step(nc.vector.tensor_tensor(newton[:], root[:], root[:], ALU.mult))
                step(nc.vector.tensor_tensor(newton[:], newton[:], var[:], ALU.mult))
                step(nc.vector.tensor_scalar(newton[:], newton[:], -0.5, 1.5, ALU.mult, ALU.add))
                step(nc.vector.tensor_tensor(rstd[:], root[:], newton[:], ALU.mult))
                nc.vector.tensor_tensor(diag, ident[:].unsqueeze(1).broadcast_to([P, TOK, P]),
                                        rstd[:].unsqueeze(2).broadcast_to([P, TOK, P]), ALU.mult).then_inc(diag_ready, 1)
                dve.wait_ge(spread, n + 1)
                nc.vector.tensor_copy(target[:], flat(6, T)).then_inc(scale_ready, 1)

            dve.wait_ge(vecs_turned, 1)
            step(nc.vector.tensor_copy(sink_all[:], banks[:, 1, 0:HEADS]))
            step(nc.vector.tensor_scalar(neg_sink[:], sink_all[:], -1.0, None, ALU.mult))
            step(nc.vector.tensor_copy(dec_consts[:], banks[:, 1, HEADS:HEADS + 2 * PAIRS]))
            for bg in range(2):
                step(nc.vector.tensor_copy(dec_sink[:, bg, :], dec_consts[:, 0:PAIRS]))
            step(nc.vector.tensor_scalar(neg_dec_sink[:], dec_sink[:], -1.0, None, ALU.mult))
            dve.wait_ge(consts, 5 + 2 * GQA + PAIRS)
            step(nc.vector.tensor_scalar(row_i[:, 1:2], row_i[:, 0:1], DEC_T - 1, None, ALU.bitwise_and))
            step(nc.vector.tensor_scalar(row_i[:, 2:3], row_i[:, 0:1], 5, None, ALU.logical_shift_right))
            step(nc.vector.tensor_copy(row_t[:], row_i[:, 1:3]))
            nc.vector.tensor_copy(vecs[:], banks[:, 0, 0:4 * KT + UT]).then_inc(vecs_ready, 1)

            def first_low(kt):
                dve.wait_ge(h_hi, kt + 1)
                nc.vector.scalar_tensor_tensor(out=acts_lo[:, kt, :], in0=flat(2 * (kt % 4), T), scalar=g_pre[:, kt:kt + 1],
                                               in1=acts_hi[:, kt, :].bitcast(F32), op0=ALU.mult, op1=ALU.subtract).then_inc(h_lo, 1)

            dve.wait_ge(squares, TOK)
            step(nc.vector.tensor_scalar(var[:], ss[:], 1.0 / D, EPS, ALU.mult, ALU.add))
            nc.vector.reciprocal(inv[:], var[:]).then_inc(inv_ready, 1)
            dve.wait_ge(vecs_ready, 1)
            for kt in range(KT):
                first_low(kt)
                if kt in (2, 6):
                    split(kt // 4)
            dve.wait_ge(root_ready, 1)
            step(nc.vector.tensor_tensor(newton[:], root[:], root[:], ALU.mult))
            step(nc.vector.tensor_tensor(newton[:], newton[:], var[:], ALU.mult))
            step(nc.vector.tensor_scalar(newton[:], newton[:], -0.5, 1.5, ALU.mult, ALU.add))
            step(nc.vector.tensor_tensor(rstd[:], root[:], newton[:], ALU.mult))
            nc.vector.tensor_tensor(diag, ident[:].unsqueeze(1).broadcast_to([P, TOK, P]),
                                    rstd[:].unsqueeze(2).broadcast_to([P, TOK, P]), ALU.mult).then_inc(diag_ready, 1)
            dve.wait_ge(spread, 1)
            nc.vector.tensor_copy(gemm_scale[:], flat(6, T)).then_inc(scale_ready, 1)

            def halves(ap):
                return ap.rearrange("p o (h t) -> p (o h) t", h=2)

            def pair_ready(nt, k, v, pair_k, pair_v):
                if nt == 0:
                    dve.wait_ge(first_done, num(pair_k + 1, pair_v))
                else:
                    dve.wait_ge(unit_used, num(k + K_UNITS, v, 4))

            scale2 = gemm_scale[:].rearrange("p (h t) -> p h t", h=2)
            dve.wait_ge(scale_ready, 1)

            def tile_evacuated(ins):
                ins.then_inc(tile_read, 1)

            def in_pair(k, v, pair_k, pair_v, read_tile):
                for kq in range(K_UNITS):
                    if not isinstance(v, int) or k + kq > 0:
                        split(k + kq + 1, v)
                for nt in range(2):
                    pair_ready(nt, k, v, pair_k, pair_v)
                    read_tile(nt, slot((pair_k % 2) * 2 + nt)).then_inc(tile_read, 1)

            def read_q(pair):
                def read(nt, src):
                    j = 2 * pair + nt
                    for head in range(2):
                        rows = slice(head * HD, (head + 1) * HD)
                        g, h = divmod(2 * j + head, GQA)
                        base = HD * (g % 2)
                        ins = nc.vector.scalar_tensor_tensor(
                            out=qT[base:base + HD, (g // 2) * GQA + h, :].rearrange("p (h t) -> p h t", h=2),
                            in0=src[rows], scalar=HD ** -0.5, in1=scale2[rows], op0=ALU.mult, op1=ALU.mult)
                        if head == 0:
                            ins.then_inc(small, 1)
                            chained[0] += 1
                    return ins
                return read

            def read_scaled(dst):
                def read(nt, src):
                    return nc.vector.tensor_tensor(halves(dst(nt)), src, scale2, ALU.mult)
                return read

            for pair in range(QW // UNIT_N):
                in_pair(pair * K_UNITS, 0, pair, 0, read_q(pair))
            for i, dst in enumerate((kT, vT)):
                pair = QW // UNIT_N + i
                in_pair(pair * K_UNITS, 0, pair, 0, read_scaled(lambda nt: dst[:, nt:nt + 1, :]))
            U_PAIR0 = (QW + 2 * KVW) // UNIT_N
            with dve.Fori(0, PW // UNIT_N // 2) as i:
                for b in range(2):
                    pair = U_PAIR0 + b
                    in_pair(pair * K_UNITS, i * 2, pair, i * 2,
                            read_scaled(lambda nt: uT[:, bass.ds(i * 4 + 2 * b + nt, 1), :]))
            dve.wait_ge(tile_read, 2 * IN_PAIRS)

            dve.wait_ge(state_turned, 1)
            for r in range(2):
                ins = nc.vector.tensor_copy(
                    u_ext[:, 4 * r:4 * r + 4, :, 0:STATE],
                    banks[:, r, 0:4 * DEC_B * STATE].rearrange("p (e b s) -> p e b s", e=4, b=DEC_B))
                ins.then_inc(state_copied, 1)
            step(nc.vector.tensor_copy(u_ext[:, :, :, STATE:LAST],
                                       uT[:, :, SEQ:T].rearrange("p e (b t) -> p e b t", t=DEC_T)))
            dve.wait_ge(state_copied, 2)
            ext = u_ext[:].rearrange("p e b s -> p (e b) s")
            dec_a = run_a[:].rearrange("p e n -> p (e n)")[:, 0:UT * DEC_B * LAST].rearrange("p (e s) -> p e s", s=LAST)
            dec_b = run_b[:].rearrange("p e n -> p (e n)")[:, 0:UT * DEC_B * LAST].rearrange("p (e s) -> p e s", s=LAST)
            src, dst, first = ext, dec_a, 0
            for g, w in enumerate(POOL_WINDOWS):
                e = slice(2 * g * DEC_B, UT * DEC_B)
                half = w // 2
                step(nc.vector.tensor_tensor(dst[:, e, first + half:LAST], src[:, e, first + half:LAST],
                                             src[:, e, first:LAST - half], ALU.add))
                own = slice(2 * g * DEC_B, (2 * g + 2) * DEC_B)
                ins = nc.vector.scalar_tensor_tensor(
                    out=z_dec[:, 2 * g:2 * g + 2, :].rearrange("p e (b t) -> p (e b) t", t=DEC_T),
                    in0=dst[:, own, STATE:LAST], scalar=1.0 / w, in1=ext[:, own, STATE:LAST],
                    op0=ALU.mult, op1=ALU.subtract)
                if g == len(POOL_WINDOWS) - 1:
                    ins.then_inc(z_ready, 1)
                else:
                    step(ins)
                first += half
                src, dst = dst, (dec_b if dst is dec_a else dec_a)
            dve.wait_ge(z_ready, 1)
            dve.wait_ge(edge_ready, 1 + sum(w - 1 for w in POOL_WINDOWS))

            def run(g):
                return (lambda e0, e1, t0, t1: run_a[:, e0:e1, t0:t1]) if g % 2 == 0 else (
                    lambda e0, e1, t0, t1: run_b[:, e0 - 2:e1 - 2, t0:t1])

            before = lambda e0, e1, t0, t1: uT[:, e0:e1, t0:t1]
            for g, w in enumerate(POOL_WINDOWS):
                half, e0 = w // 2, 2 * g
                step(nc.vector.tensor_tensor(run(g)(e0, UT, half, SEQ), before(e0, UT, half, SEQ),
                                             before(e0, UT, 0, SEQ - half), ALU.add))
                step(nc.vector.tensor_copy(run(g)(e0, UT, 0, half), before(e0, UT, 0, half)))
                before = run(g)
                if g > 0:
                    finish = g - 1
                    pool_z(dve, step, run, finish)
            pool_z(dve, step, run, len(POOL_WINDOWS) - 1)
            dve.wait_ge(z_hi, 1)
            nc.vector.tensor_tensor(acts_lo[:, 0:UT, SEQ:T], z_dec[:], acts_hi[:, 0:UT, SEQ:T].bitcast(F32),
                                    ALU.subtract).then_inc(z_lo, 1)
            for g in range(len(POOL_WINDOWS)):
                dve.wait_ge(z_hi, g + 2)
                nc.vector.tensor_tensor(acts_lo[:, 2 * g:2 * g + 2, 0:SEQ], run(g)(2 * g, 2 * g + 2, 0, SEQ),
                                        acts_hi[:, 2 * g:2 * g + 2, 0:SEQ].bitcast(F32), ALU.subtract).then_inc(z_lo, 1)
            for g in range(POOL_PAIRS):
                if g % 2 == 0:
                    split(U_POOL + g // 2 + 1)
                for nt in range(2):
                    m = 2 * g + nt
                    dve.wait_ge(mix_hi, m + 1)
                    shape = "p (h t) -> p h t"
                    nc.vector.scalar_tensor_tensor(
                        out=acts_lo[:, QT + m, :].rearrange(shape, h=2), in0=slot((g % 2) * 2 + nt),
                        scalar=p_scale[:, m:m + 1], in1=acts_hi[:, QT + m, :].bitcast(F32).rearrange(shape, h=2),
                        op0=ALU.mult, op1=ALU.subtract).then_inc(tile_read, 1)

            dve.wait_ge(kv_turned, 1)
            nc.vector.tensor_copy(kv_dec[:].rearrange("p b n -> p (b n)"), banks[0:ND, 2, :]).then_inc(kv_copied, 1)
            nc.vector.tensor_copy(k_tok[:], banks[:, 3, 0:KVW]).then_inc(kv_copied, 1)
            dve.wait_ge(bias_ready, 6)

            def shift_scores(s):
                blk, g = divmod(s, KV_HEADS)
                par = s % 2
                lo = WINDOW if blk == 0 else 0
                dve.wait_ge(scores, s + 1)
                if s >= 2:
                    dve.wait_ge(probs_turned, s - 1)
                for h in range(GQA):
                    slope = 2.0 ** (-8.0 * (g * GQA + h + 1) / HEADS)
                    nc.vector.scalar_tensor_tensor(
                        out=probs[:, par, h, lo:], in0=bias[:, lo:], scalar=slope,
                        in1=banks[:, 2 * par + h // 2, (h % 2) * 256 + lo:(h % 2) * 256 + 256],
                        op0=ALU.mult, op1=ALU.add).then_inc(scores_read, 1)
                dve.wait_ge(scores_read, GQA * (s + 1))
                step(nc.vector.tensor_reduce(stats[:, par, 4, :], probs[:, par, :, lo:], AX.X, ALU.max, negate=True))
                step(nc.vector.tensor_tensor(stats[:, par, 0, :], stats[:, par, 4, :],
                                             neg_sink[:, g * GQA:(g + 1) * GQA], ALU.min))
                nc.vector.tensor_tensor(stats[:, par, 1, :], sink_all[:, g * GQA:(g + 1) * GQA], stats[:, par, 0, :],
                                        ALU.add).then_inc(shift_ready, 1)

            def normalise(s):
                g, par = s % KV_HEADS, s % 2
                dve.wait_ge(exps, (GQA + 1) * (s + 1))
                step(nc.vector.tensor_tensor(stats[:, par, 5, :], stats[:, par, 2, :], stats[:, par, 3, :], ALU.add))
                step(nc.vector.reciprocal(stats[:, par, 6, :], stats[:, par, 5, :]))
                dve.wait_ge(mixed, s + 1)
                nc.vector.tensor_tensor(attn_tok[:, g * GQA * HD:(g + 1) * GQA * HD].rearrange("p (h d) -> p h d", h=GQA),
                                        banks[:, 6, 0:GQA * HD].rearrange("p (h d) -> p h d", h=GQA),
                                        stats[:, par, 6, :].unsqueeze(2).broadcast_to([P, GQA, HD]),
                                        ALU.mult).then_inc(mixed_read, 1)

            def rows_low(qb, r, n):
                dve.wait_ge(rows_hi, n + 1)
                dst = slice(qb * P, (qb + 1) * P)
                nc.vector.tensor_tensor(acts_lo[:, 4 * r:4 * r + 4, dst],
                                        banks[:, 7, :].rearrange("p (a q) -> p a q", a=4),
                                        acts_hi[:, 4 * r:4 * r + 4, dst].bitcast(F32), ALU.subtract).then_inc(rows_lo, 1)

            steps = (TOK - 1) * KV_HEADS
            shift_scores(0)
            for s in range(steps):
                blk = s // KV_HEADS
                turn = s % KV_HEADS == 0 and s > 0
                if s + 1 < steps:
                    shift_scores(s + 1)
                if turn:
                    rows_low(blk - 1, 0, 2 * (blk - 1))
                normalise(s)
                if turn:
                    rows_low(blk - 1, 1, 2 * (blk - 1) + 1)
            rows_low(TOK - 2, 0, 2 * (TOK - 2))
            rows_low(TOK - 2, 1, 2 * (TOK - 2) + 1)

            new = slice(WINDOW, NKEY)
            for bg in (1, 0):
                step(nc.vector.tensor_scalar(dec_pen[:, bg, new], dec_pen[:, 0, new], row_t[:, 1:2], 4.0 * bg,
                                             ALU.subtract, ALU.not_equal))
                step(nc.vector.tensor_scalar(dec_pen[:, bg, new], dec_pen[:, bg, new], MASKED, None, ALU.mult))
                step(nc.vector.tensor_scalar(dec_bias[:, bg, :], dec_bias[:, 0, :], row_t[:, 0:1], None, ALU.subtract))
                step(nc.vector.tensor_scalar(dec_pen[:, bg, 0:WINDOW], dec_bias[:, bg, 0:WINDOW], -float(WINDOW), MASKED,
                                             ALU.is_le, ALU.mult))
                step(nc.vector.tensor_tensor(dec_pen[:, bg, :], dec_pen[:, bg, :], dec_bias[:, bg, :], ALU.add))
                step(nc.vector.tensor_scalar(dec_bias[:, bg, new], dec_bias[:, bg, new], 0.0, MASKED, ALU.is_gt, ALU.mult))
                step(nc.vector.tensor_tensor(dec_pen[:, bg, new], dec_pen[:, bg, new], dec_bias[:, bg, new], ALU.add))
            for r in range(2, 4):
                dve.wait_ge(old_k_turned, r + 1)
                nc.vector.tensor_copy(old_kT[:, 4 * r:4 * r + 4, :].rearrange("p a k -> p (a k)"),
                                      banks[:, r, :]).then_inc(old_k_dve, 1)
            dve.wait_ge(dec_scores, 1)
            for bg in range(2):
                for pair in range(PAIRS):
                    step(nc.vector.scalar_tensor_tensor(
                        out=dec_probs[:, bg * PAIRS + pair, :], in0=dec_pen[:, bg, :], scalar=dec_slope[:, pair:pair + 1],
                        in1=banks[:, 4 + bg, pair * NKEY:(pair + 1) * NKEY], op0=ALU.mult, op1=ALU.add))
            step(nc.vector.tensor_reduce(dec_stats[:, 4, :], dec_probs[:], AX.X, ALU.max, negate=True))
            step(nc.vector.tensor_tensor(dec_stats[:, 0, :], dec_stats[:, 4, :],
                                         neg_dec_sink[:].rearrange("p b c -> p (b c)"), ALU.min))
            nc.vector.tensor_tensor(dec_stats[:, 1, :], dec_sink[:].rearrange("p b c -> p (b c)"), dec_stats[:, 0, :],
                                    ALU.add).then_inc(dec_shift, 1)
            dve.wait_ge(dec_exps, 5)
            step(nc.vector.tensor_tensor(dec_stats[:, 5, :], dec_stats[:, 2, :], dec_stats[:, 3, :], ALU.add))
            step(nc.vector.reciprocal(dec_stats[:, 6, :], dec_stats[:, 5, :]))
            nc.vector.tensor_tensor(dec_probs[:], dec_probs[:], dec_stats[:, 6, :].unsqueeze(2).broadcast_to([P, 4, NKEY]),
                                    ALU.mult).then_inc(dec_norm, 1)
            dve.wait_ge(dec_turned, 1)
            nc.vector.tensor_copy(dec_PT_new[:].rearrange("p a r -> p (a r)"), banks[0:ND, 7, :]).then_inc(dec_copied, 1)
            dve.wait_ge(dec_hi, 2 * GQA)
            for half in range(2):
                for h in range(GQA):
                    src, dst_hi, dst_lo = dec_out(half, h)
                    nc.vector.tensor_tensor(dst_lo, src, dst_hi.bitcast(F32), ALU.subtract).then_inc(dec_lo, 1)

            def out_pair(k, v, pair_k, pair_v, tile, count):
                for kq in range(K_UNITS):
                    split(k + kq + 1, v)
                for nt in range(2):
                    dve.wait_ge(sq_ready, count + nt + 1)
                    nc.vector.tensor_scalar(halves(x1T[:, tile(nt), :]), slot((pair_k % 2) * 2 + nt), 1.0, None,
                                            ALU.mult).then_inc(tile_read, 1)

            with dve.Fori(0, OUT_PAIRS // 2) as i:
                for b in range(2):
                    out_pair(U_OUT + b * K_UNITS, i * 2, P_OUT + b, i * 2,
                             lambda nt: bass.ds(i * 4 + 2 * b + nt, 1), i * 4 + 2 * b)

            row_scales(1, norm_scale)
            dve.wait_ge(scale_ready, 2)

            def second_low(kt):
                dve.wait_ge(h_hi, KT + kt + 1)
                nc.vector.scalar_tensor_tensor(out=acts_lo[:, kt, :], in0=x1T[:, kt, :], scalar=g_ffn[:, kt:kt + 1],
                                               in1=acts_hi[:, kt, :].bitcast(F32), op0=ALU.mult, op1=ALU.subtract).then_inc(h_lo, 1)

            for kt in range(KT):
                step(nc.vector.tensor_tensor(x1T[:, kt, :], x1T[:, kt, :], norm_scale[:], ALU.mult))
                dve.wait_ge(x_turned, KT + kt + 1)
                nc.vector.scalar_tensor_tensor(out=x1T[:, kt, :], in0=x1T[:, kt, :], scalar=g_post[:, kt:kt + 1],
                                               in1=flat(2 * (kt % 4), T), op0=ALU.mult, op1=ALU.add).then_inc(x1_ready, 1)
                if kt > 0:
                    second_low(kt - 1)
            second_low(KT - 1)
            row_scales(2, gemm_scale)
            dve.wait_ge(scale_ready, 3)

            dve.wait_ge(y_clear, 1)

            def chunk(c, last=False):
                v = c * (CHUNK_UNITS // 4)
                for b in range(UP_PAIRS):
                    k = U_FFN + b * K_UNITS
                    for kq in range(K_UNITS):
                        split(k + kq + 1, v)
                    for nt in range(2):
                        j = 2 * b + nt
                        pair_ready(nt, k, v, P_FFN + b, c * CHUNK_PAIRS)
                        nc.vector.scalar_tensor_tensor(
                            out=relu_buf[:].rearrange("p (h t) -> p h t", h=2), in0=slot(((P_FFN + b) % 2) * 2 + nt),
                            scalar=0.0, in1=scale2, op0=ALU.max, op1=ALU.mult).then_inc(tile_read, 1)
                        dve.wait_ge(tile_read, num(2 * P_FFN + j + 1, c, CHUNK_TILES))
                        nc.vector.tensor_tensor(sq_tmp[:, 0:T], relu_buf[:], relu_buf[:], ALU.mult).then_inc(relu_sq, 1)
                        dve.wait_ge(mlp_hi_ready, num(j + 1, c, 2 * UP_PAIRS))
                        dve.wait_ge(relu_sq, num(j + 1, c, 2 * UP_PAIRS))
                        nc.vector.tensor_tensor(mlp_lo[:, j, :], sq_tmp[:, 0:T], mlp_hi[:, j, :].bitcast(F32),
                                                ALU.subtract).then_inc(mlp_lo_ready, 1)
                for n in range(OUT_PAIRS):
                    k = U_FFN + UP_PAIRS * K_UNITS + n
                    if not last or n + 1 < OUT_PAIRS:
                        split(k + 1, v)
                    for nt in range(2):
                        m = 2 * n + nt
                        if nt == 0:
                            dve.wait_ge(first_done, num(P_FFN + UP_PAIRS + n + 1, c, CHUNK_PAIRS))
                        else:
                            dve.wait_ge(unit_used, num(k + 1, v, 4))
                        acc = y_sum[:, m, :].rearrange("p (h t) -> p h t", h=2)
                        nc.vector.tensor_tensor(acc, acc, slot(((P_FFN + UP_PAIRS + n) % 2) * 2 + nt),
                                                ALU.add).then_inc(tile_read, 1)

            with dve.Fori(0, CHUNKS - 1) as c:
                chunk(c)
            chunk(CHUNKS - 1, last=True)

            row_scales(3, norm_scale)
            dve.wait_ge(scale_ready, 4)
            o = 0
            for kg in range(KT // 4):
                for kt in range(4 * kg, 4 * kg + 4):
                    step(nc.vector.tensor_tensor(y_sum[:, kt, :], y_sum[:, kt, :], norm_scale[:], ALU.mult))
                    nc.vector.scalar_tensor_tensor(out=x1T[:, kt, :], in0=y_sum[:, kt, :], scalar=g_last[:, kt:kt + 1],
                                                   in1=x1T[:, kt, :], op0=ALU.mult, op1=ALU.add).then_inc(y_ready, 1)
                for c in range(TOK):
                    o = kg * TOK + c
                    if o % 2 == 1:
                        dve.wait_ge(y_turned, o + 1)
                        if o >= 8:
                            dve.wait_ge(y_stored[o % 8], 16 * (o // 8))
                        r = tok_rows[c]
                        nc.vector.tensor_copy(w_raw[0:r].rearrange("p s n -> p (s n)")[:, (o % 8) * 512:(o % 8 + 1) * 512],
                                              banks[0:r, o % 8, :]).then_inc(y_copied[1], 1)

        @block.tensor
        def _(pe):
            def turn_x(tok, kt, s):
                for c in range(TOK):
                    r = tok_rows[c]
                    ins = nc.tensor.transpose(flat(2 * s, T)[:, c * P:c * P + r], tok[0:r, c, kt * P:(kt + 1) * P],
                                              ident[0:r, 0:r])
                ins.then_inc(x_turned, 1)

            def spread_scales(n):
                pe.wait_ge(diag_ready, n + 1)
                for c in range(TOK):
                    r = tok_rows[c]
                    ins = nc.tensor.matmul(flat(6, T)[:, c * P:c * P + r], ones[0:r, :], diag[0:r, c, 0:r], start=True, stop=True)
                ins.then_inc(spread, 1)

            def turn_sums(n):
                pe.wait_ge(sq_added, n * KT)
                for c in range(TOK):
                    r = tok_rows[c]
                    ins = nc.tensor.matmul(banks[0:r, 6, c:c + 1], sq_sum[:, c * P:c * P + r], ones[:, 0:1], start=True, stop=True)
                ins.then_inc(sums_turned, 1)

            def product(out, s, kk, nt, hi, lo, start, stop):
                cols = slice(kk * UNIT_N + nt * P, kk * UNIT_N + (nt + 1) * P)
                wh, wl = w_hi[:, s, cols], w_lo[:, s, cols]
                terms = [(wh, hi, start, False), (wh, lo, False, False), (wl, hi, False, stop)]
                for w, x, first, last in terms:
                    for h in range(2):
                        ins = nc.tensor.matmul(out[:, h, :], w, x[:, h * H:(h + 1) * H], start=first, stop=last)
                return ins

            def pair_tiles(k, v, pair_k, pair_v, units):
                for q in range(units):
                    u = k + q
                    pe.wait_ge(lo_split, num(u + 1, v, 4))
                    for nt in range(2):
                        if q == 0 and (pair_k >= 2 or not isinstance(pair_v, int)):
                            pe.wait_ge(tile_read, num(2 * pair_k - 3 + nt, pair_v, 2))
                        for kk in range(UNIT_KT):
                            kt = q * UNIT_KT + kk
                            ins = product(slot((pair_k % 2) * 2 + nt), u % SPLIT_SLOTS, kk, nt, acts_hi[:, kt, :],
                                          acts_lo[:, kt, :], kt == 0, kt == units * UNIT_KT - 1)
                        if q == units - 1 and nt == 0:
                            ins.then_inc(first_done, 1)
                    ins.then_inc(unit_used, 1)

            pe.wait_ge(consts, 7 + 2 * GQA + PAIRS)
            for i in range(7):
                pe.wait_ge(vec_landed[i], 16)
            n = 4 * KT + UT
            nc.tensor.transpose(banks[:, 0, 0:n], vec_rows[:], ident[0:n, 0:n])
            nc.tensor.matmul(banks[:, 1, 0:HEADS], ones[0:1, :], sink_row[:], start=True, stop=True)
            nc.tensor.matmul(banks[:, 1, HEADS:HEADS + PAIRS], head_rows[:], sink_hh[:], start=True, stop=True)
            nc.tensor.matmul(banks[:, 1, HEADS + PAIRS:HEADS + 2 * PAIRS], slope_row[:], slope_pair[:], start=True,
                             stop=True).then_inc(vecs_turned, 1)
            for c in range(TOK):
                pe.wait_ge(x_landed[c], 16)
            for kt in range(KT):
                if kt == 0:
                    pe.wait_ge(vecs_ready, 1)
                if kt >= 4:
                    pe.wait_ge(h_lo, kt - 3)
                turn_x(x_tok, kt, kt % 4)
            pe.wait_ge(h_lo, KT)
            spread_scales(0)
            pe.wait_ge(scale_ready, 1)

            for pair in range(2):
                pair_tiles(pair * K_UNITS, 0, pair, 0, K_UNITS)
            with pe.Fori(1, IN_PAIRS // 2) as i:
                for b in range(2):
                    pair_tiles(b * K_UNITS, i * 2, b, i * 2, K_UNITS)

            pe.wait_ge(tile_read, 2 * IN_PAIRS)
            pe.wait_ge(state_landed, 16)
            n = DEC_B * STATE
            for e in range(UT):
                ins = nc.tensor.transpose(banks[:, e // 4, (e % 4) * n:(e % 4 + 1) * n],
                                          run_a[0:n, 0:2, :].rearrange("p a n -> p (a n)")[:, e * P:(e + 1) * P], ident[0:n, 0:n])
            ins.then_inc(state_turned, 1)
            for e in range(UT):
                nc.tensor.transpose(flat(2, PW)[0:STATE, e * P:(e + 1) * P], uT[:, e, SEQ - STATE:SEQ], ident[:])
                ins = nc.tensor.transpose(flat(4, PW)[0:ND, e * P:(e + 1) * P], uT[:, e, SEQ:T], ident[:])
            ins.then_inc(u_turned, 1)
            pe.wait_ge(state_copied, 2)
            pe.wait_ge(u_copied, 2)
            for g in range(POOL_PAIRS):
                u = U_POOL + g // 2
                if g % 2 == 0:
                    pe.wait_ge(lo_split, u + 1)
                if g == 0:
                    pe.wait_ge(z_lo, 1 + POOL_PAIRS)
                for nt in range(2):
                    pe.wait_ge(tile_read, 2 * (P_POOL + g) - 3 + nt)
                    for kk in range(2):
                        e = 2 * g + kk
                        ins = product(slot((g % 2) * 2 + nt), u % SPLIT_SLOTS, (g % 2) * 2 + kk, nt, acts_hi[:, e, :],
                                      acts_lo[:, e, :], kk == 0, kk == 1)
                    if nt == 0:
                        ins.then_inc(first_done, 1)
                ins.then_inc(even_group_done if g % 2 == 0 else unit_used, 1)

            pe.wait_ge(tile_read, 2 * P_OUT)
            for blk in range(TOK - 1):
                for e in range(PAIRS):
                    nc.tensor.transpose(flat(0, 1024)[:, blk * KVW + e * P:blk * KVW + (e + 1) * P],
                                        vT[:, e, blk * P:(blk + 1) * P], ident[:])
            for i, src in enumerate((kT, vT)):
                for e in range(PAIRS):
                    nc.tensor.transpose(banks[0:ND, 2, i * KVW + e * P:i * KVW + (e + 1) * P], src[:, e, SEQ:T], ident[:])
            for e in range(PAIRS):
                ins = nc.tensor.transpose(banks[:, 3, e * P:(e + 1) * P], kT[:, e, SEQ - P:SEQ], ident[:])
            ins.then_inc(kv_turned, 1)
            pe.wait_ge(kv_copied, 3)

            def score(s):
                blk, g = divmod(s, KV_HEADS)
                rows = slice((g % 2) * HD, (g % 2 + 1) * HD)
                lo = WINDOW if blk == 0 else 0
                keys = slice(max(blk - 1, 0) * P, (blk + 1) * P)
                if s >= 2:
                    pe.wait_ge(scores_read, GQA * (s - 1))
                for h in range(GQA):
                    ins = nc.tensor.matmul(banks[:, 2 * (s % 2) + h // 2, (h % 2) * 256 + lo:(h % 2) * 256 + 256],
                                           qT[rows, (g // 2) * GQA + h, blk * P:(blk + 1) * P], kT[rows, g // 2, keys],
                                           start=True, stop=True)
                ins.then_inc(scores, 1)

            def turn_rows(r, n):
                if r == 0:
                    pe.wait_ge(mixed_read, (n // 2 + 1) * KV_HEADS)
                if n > 0:
                    pe.wait_ge(rows_lo, n)
                for a in range(4):
                    ins = nc.tensor.transpose(banks[:, 7, a * P:(a + 1) * P], attn_tok[:, (4 * r + a) * P:(4 * r + a + 1) * P], ident[:])
                ins.then_inc(rows_turned, 1)

            steps = (TOK - 1) * KV_HEADS
            score(0)
            score(1)
            for s in range(steps):
                blk, g = divmod(s, KV_HEADS)
                parts = 1 if blk == 0 else 2
                pe.wait_ge(exps, (GQA + 1) * (s + 1))
                if s > 0:
                    pe.wait_ge(probs_copied, s)
                for h in range(GQA):
                    for half in range(parts):
                        at = (2 - parts + half) * WINDOW
                        ins = nc.tensor.transpose(flat(4, 1024)[:, (h * parts + half) * P:(h * parts + half + 1) * P],
                                                  probs[:, s % 2, h, at:at + P], ident[:])
                ins.then_inc(probs_turned, 1)
                turn = g == 0 and blk > 0
                if turn:
                    turn_rows(0, 2 * (blk - 1))
                if s + 2 < steps:
                    score(s + 2)
                pe.wait_ge(probs_copied, s + 1)
                if s > 0:
                    pe.wait_ge(mixed_read, s)
                for h in range(GQA):
                    for half in range(parts):
                        ins = nc.tensor.matmul(banks[:, 6, h * HD:(h + 1) * HD], probs_T[:, s % 2, h * parts + half, :],
                                               v_tok[:, blk - parts + 1 + half, g * HD:(g + 1) * HD],
                                               start=half == 0, stop=half == parts - 1)
                ins.then_inc(mixed, 1)
                if turn:
                    turn_rows(1, 2 * (blk - 1) + 1)
            turn_rows(0, 2 * (TOK - 2))
            turn_rows(1, 2 * (TOK - 2) + 1)

            for i in range(2):
                pe.wait_ge(cache_landed[i], 16)
            pe.wait_ge(scores_read, GQA * steps)
            for r in range(4):
                for a in range(4):
                    b, pair = divmod(4 * r + a, PAIRS)
                    ins = nc.tensor.transpose(banks[:, r, a * P:(a + 1) * P], old_k[:, b, pair * P:(pair + 1) * P], ident[:])
                ins.then_inc(old_k_turned, 1)
            pe.wait_ge(q_ready, 1 + 2 * PAIRS)
            pe.wait_ge(old_k_act, 2)
            pe.wait_ge(old_k_dve, 2)
            pe.wait_ge(probs_copied, steps)
            for b in range(DEC_B):
                rows = slice(32 * (b % 4), 32 * (b % 4) + 32)
                for pair in range(PAIRS):
                    out = banks[rows, 4 + b // 4, pair * NKEY:(pair + 1) * NKEY]
                    i = b * PAIRS + pair
                    nc.tensor.matmul(out[:, 0:WINDOW], q_blocks[:, i, :], old_kT[:, i, :], start=True, stop=True)
                    ins = nc.tensor.matmul(out[:, WINDOW:NKEY], q_blocks[:, i, :], kT[:, pair, SEQ:T], start=True, stop=True)
            ins.then_inc(dec_scores, 1)
            pe.wait_ge(dec_norm, 1)
            pe.wait_ge(mixed_read, steps)
            pe.wait_ge(rows_lo, 2 * (TOK - 1))
            for ck in range(4):
                nc.tensor.transpose(banks[:, 6, ck * P:(ck + 1) * P], dec_probs[:, ck, 0:WINDOW], ident[:])
                ins = nc.tensor.transpose(banks[0:ND, 7, ck * P:(ck + 1) * P], dec_probs[:, ck, WINDOW:NKEY], ident[:])
            ins.then_inc(dec_turned, 1)
            pe.wait_ge(dec_copied, 2)
            for b in range(DEC_B):
                for pair in range(PAIRS):
                    ck = (b // 4) * PAIRS + pair
                    out = banks[:, 5, (b * PAIRS + pair) * 32:(b * PAIRS + pair + 1) * 32]
                    rows = slice(32 * (b % 4), 32 * (b % 4) + 32)
                    nc.tensor.matmul(out, old_v[:, b, pair * P:(pair + 1) * P], dec_PT[:, ck, rows], start=True, stop=False)
                    ins = nc.tensor.matmul(out, kv_dec[:, 1, pair * P:(pair + 1) * P], dec_PT_new[:, ck, rows], start=False, stop=True)
            ins.then_inc(dec_mixed, 1)
            pe.wait_ge(dec_lo, 2 * GQA)

            with pe.Fori(0, OUT_PAIRS // 2) as i:
                for b in range(2):
                    pair_tiles(U_OUT + b * K_UNITS, i * 2, P_OUT + b, i * 2, K_UNITS)

            pe.wait_ge(tile_read, 2 * P_FFN)
            turn_sums(1)
            spread_scales(1)
            for c in range(TOK):
                pe.wait_ge(x2_landed[c], 16)
            for kt in range(KT):
                if kt == 3:
                    pe.wait_ge(scale_ready, 2)
                if kt >= 4:
                    pe.wait_ge(x1_ready, kt - 3)
                turn_x(x_tok2, kt, kt % 4)
            pe.wait_ge(x1_ready, KT)
            turn_sums(2)
            spread_scales(2)
            pe.wait_ge(h_lo, 2 * KT)
            pe.wait_ge(scale_ready, 3)

            def chunk(c):
                v = c * (CHUNK_UNITS // 4)
                for b in range(UP_PAIRS):
                    pair_tiles(U_FFN + b * K_UNITS, v, P_FFN + b, c * CHUNK_PAIRS, K_UNITS)
                for n in range(OUT_PAIRS):
                    u = U_FFN + UP_PAIRS * K_UNITS + n
                    pair = P_FFN + UP_PAIRS + n
                    pe.wait_ge(lo_split, num(u + 1, v, 4))
                    for kk in range(UNIT_KT):
                        if n == 0:
                            pe.wait_ge(mlp_lo_ready, num(kk + 1, c, 2 * UP_PAIRS))
                        for nt in range(2):
                            if kk == 0:
                                pe.wait_ge(tile_read, num(2 * pair - 3 + nt, c, CHUNK_TILES))
                            ins = product(slot((pair % 2) * 2 + nt), u % SPLIT_SLOTS, kk, nt, mlp_hi[:, kk, :],
                                          mlp_lo[:, kk, :], kk == 0, kk == UNIT_KT - 1)
                            if kk == UNIT_KT - 1 and nt == 0:
                                ins.then_inc(first_done, 1)
                    ins.then_inc(unit_used, 1)

            with pe.Fori(0, CHUNKS) as c:
                chunk(c)

            pe.wait_ge(tile_read, 2 * (P_FFN + CHUNKS * CHUNK_PAIRS))
            turn_sums(3)
            spread_scales(3)
            pe.wait_ge(scale_ready, 4)
            for kg in range(KT // 4):
                pe.wait_ge(y_ready, 4 * kg + 4)
                for c in range(TOK):
                    o = kg * TOK + c
                    r = tok_rows[c]
                    if o >= 8:
                        pe.wait_ge(y_copied[o % 2], (o - 8) // 2 + 1)
                    for a in range(4):
                        ins = nc.tensor.transpose(banks[0:r, o % 8, a * P:(a + 1) * P], x1T[:, 4 * kg + a, c * P:c * P + r], ident[:])
                    ins.then_inc(y_turned, 1)


_INS = ['x_prompt', 'x_sample', 'cache_k', 'cache_v', 'state_pool', 'w_in', 'w_out', 'w_pool', 'pool_scale', 'attn_sinks',
        'g_pre_mix', 'g_post_mix', 'g_pre_ffn', 'g_post_ffn', 'w_up', 'w_down']


def kernel(**inputs):
    import numpy as np
    import concourse.bacc as bacc
    from concourse.bass_utils import run_bass_kernel_spmd

    nc = bacc.Bacc("TRN2", target_bir_lowering=False, num_devices=1)
    arrays, args = {}, []
    for name in _INS:
        a = np.ascontiguousarray(inputs[name])
        arrays[f"in_{name}"] = a
        args.append(nc.dram_tensor(f"in_{name}", a.shape, mybir.dt.from_np(a.dtype), kind="ExternalInput").ap())
    depth, dec_b, window, kv_heads, hd = inputs['cache_k'].shape
    _, _, state, pool_w = inputs['state_pool'].shape
    prompt = (depth, 1, window, kv_heads, hd)
    shapes = [inputs['x_prompt'].shape, inputs['x_sample'].shape, prompt, prompt, (depth, 1, state, pool_w),
              inputs['cache_k'].shape, inputs['cache_v'].shape, inputs['state_pool'].shape]
    for i, shape in enumerate(shapes):
        args.append(nc.dram_tensor(f"out_{i}", tuple(shape), F32, kind="ExternalOutput").ap())
    hybrid_decoder(nc, *args)
    r = run_bass_kernel_spmd(nc, [arrays], core_ids=[0])
    return tuple(r.results[0][f"out_{i}"] for i in range(len(shapes)))
```

```python
from contextlib import ExitStack

import concourse.bass as bass
from concourse import mybir

F32 = mybir.dt.float32
F32R = mybir.dt.float32r
I32 = mybir.dt.int32
ALU = mybir.AluOpType
ACT = mybir.ActivationFunctionType
AX = mybir.AxisListType

P = 128
EPS = 1e-6
MASKED = -1e38
RAW_SLOTS = 4
SPLIT_SLOTS = 2
UNIT_KT = 4
UNIT_N = 256
POOL_WINDOWS = (2, 4, 8, 16)


def hybrid_decoder(nc, x_prompt, x_sample, cache_k, cache_v, state_pool, w_in, w_out, w_pool, pool_scale,
                   attn_sinks, g_pre_mix, g_post_mix, g_pre_ffn, g_post_ffn, w_up, w_down,
                   y_prompt, y_sample, k_prompt, v_prompt, pool_prompt, k_sample, v_sample, pool_sample):
    _, SEQ, D = x_prompt.shape
    DEC_B, DEC_T, _ = x_sample.shape
    _, _, WINDOW, KV_HEADS, HD = cache_k.shape
    STATE = state_pool.shape[2]
    HEADS = attn_sinks.shape[1]
    GQA = HEADS // KV_HEADS
    F = w_up.shape[2]
    ND = DEC_B * DEC_T
    T = SEQ + ND
    H = T // 2
    KT = D // P
    TOK = SEQ // P + 1
    QW = HEADS * HD
    KVW = KV_HEADS * HD
    PW = w_pool.shape[1] * w_pool.shape[2]
    PAIRS = KV_HEADS // 2
    QT = QW // P
    UT = PW // P
    NKEY = WINDOW + ND
    LAST = STATE + DEC_T
    PAD = 16
    ROW = PAD + SEQ + DEC_B * LAST
    assert D == w_out.shape[1] and WINDOW == P and HD * 2 == P and T % 2 == 0 and QT + UT == KT
    assert QW // UNIT_N == KV_HEADS and KVW == UNIT_N and w_pool.shape[2] == UNIT_N and max(POOL_WINDOWS) <= PAD
    assert tuple(w_in.shape[1:]) == (D, QW + 2 * KVW + PW) and PAIRS == 2 and GQA == 4 and TOK == 5

    IN_PAIRS = w_in.shape[2] // UNIT_N
    Q_PAIR0, U_PAIR0 = 2, 2 + QW // UNIT_N
    K_UNITS = KT // UNIT_KT
    IN_UNITS = IN_PAIRS * K_UNITS
    POOL_UNITS = PW // (UNIT_KT * P)
    POOL_PAIRS = len(POOL_WINDOWS)
    OUT_PAIRS = D // UNIT_N
    CHUNK = UNIT_KT * P
    CHUNKS = F // CHUNK
    UP_PAIRS = CHUNK // UNIT_N
    CHUNK_UNITS = UP_PAIRS * K_UNITS + OUT_PAIRS
    CHUNK_PAIRS = UP_PAIRS + OUT_PAIRS
    CHUNK_TILES = 2 * CHUNK_PAIRS
    U_POOL = IN_UNITS
    U_OUT = U_POOL + POOL_UNITS
    U_FFN = U_OUT + OUT_PAIRS * K_UNITS
    P_POOL = IN_PAIRS
    P_OUT = P_POOL + POOL_PAIRS
    P_FFN = P_OUT + OUT_PAIRS
    N_UNITS = U_FFN + CHUNKS * CHUNK_UNITS

    tok_rows = [min(P, T - c * P) for c in range(TOK)]

    def units_of(w):
        return w.rearrange("(u k p) n -> u p k n", k=UNIT_KT, p=P)

    w_in_v, w_out_v, w_up_v, w_down_v = units_of(w_in[0]), units_of(w_out[0]), units_of(w_up[0]), units_of(w_down[0])
    w_pool_v = units_of(w_pool[0].rearrange("g c d -> (g c) d"))

    with ExitStack() as ctx:
        def sb(name, shape, dt=F32, scope=ctx):
            return scope.enter_context(nc.sbuf_tensor(name, shape, dt))

        def sem(name):
            return ctx.enter_context(nc.semaphore(name))

        acts_hi = sb("acts_hi", [P, KT, T], F32R)
        acts_lo = sb("acts_lo", [P, KT, T], F32R)
        w_raw = sb("w_raw", [P, RAW_SLOTS, UNIT_KT * UNIT_N])
        w_hi = sb("w_hi", [P, SPLIT_SLOTS, UNIT_KT * UNIT_N], F32R)
        w_lo = sb("w_lo", [P, SPLIT_SLOTS, UNIT_KT * UNIT_N], F32R)
        gemm_scale = sb("gemm_scale", [P, T])
        norm_scale = sb("norm_scale", [P, T])
        sq_sum = sb("sq_sum", [P, T])
        sq_tmp = sb("sq_tmp", [P, 2 * T])
        diag = sq_tmp[:, 0:TOK * P].rearrange("p (c m) -> p c m", c=TOK)
        vecs = sb("vecs", [P, 4 * KT + UT])
        ident = sb("ident", [P, P])
        ones = sb("ones", [P, P])
        sink_all = sb("sink_all", [P, HEADS])
        neg_sink = sb("neg_sink", [P, HEADS])
        dec_consts = sb("dec_consts", [P, 2 * PAIRS])
        neg_dec_sink = sb("neg_dec_sink", [P, 2, PAIRS])
        dec_sink = sb("dec_sink", [P, 2, PAIRS])
        dec_slope = dec_consts[:, PAIRS:2 * PAIRS]
        row_i = sb("row_i", [P, 3], I32)
        row_t = sb("row_t", [P, 2])
        ss = sb("ss", [P, TOK])
        var = sb("var", [P, TOK])
        inv = sb("inv", [P, TOK])
        root = sb("root", [P, TOK])
        newton = sb("newton", [P, TOK])
        rstd = sb("rstd", [P, TOK])
        g_pre, g_post = vecs[:, 0:KT], vecs[:, KT:2 * KT]
        g_ffn, g_last = vecs[:, 2 * KT:3 * KT], vecs[:, 3 * KT:4 * KT]
        p_scale = vecs[:, 4 * KT:4 * KT + UT]

        banks = ctx.enter_context(nc.psum_tensor("banks", [P, 8, 512], F32))

        def slot(s):
            return banks[:, 2 * s:2 * s + 2, 0:H]

        def flat(b, n):
            return banks[:, b:b + (n + 511) // 512, :].rearrange("p b n -> p (b n)")[:, 0:n]

        mixer = ExitStack()
        qT = sb("qT", [P, QT, T], F32, mixer)
        k_twice = sb("k_twice", [P, KV_HEADS, T], F32, mixer)
        uT = sb("uT", [P, UT, ROW], F32, mixer)
        start = ExitStack()
        x_tok = sb("x_tok", [P, TOK, D], F32, start)
        vec_rows = sb("vec_rows", [4 * KT + UT, P], F32, start)
        sink_row = sb("sink_row", [1, HEADS], F32, start)
        sink_hh = sb("sink_hh", [2 * GQA, PAIRS], F32, start)
        head_rows = sb("head_rows", [2 * GQA, P], F32, start)
        slope_row = sb("slope_row", [1, P], F32, start)
        slope_pair = sb("slope_pair", [1, PAIRS], F32, start)
        start.close()
        run_a = sb("run_a", [P, 2 * ROW], F32, mixer)
        old_k = sb("old_k", [P, DEC_B, KVW], F32, mixer)
        probs = sb("probs", [P, 2, GQA, 2 * WINDOW], F32, mixer)
        probs_T = sb("probs_T", [P, 2, 4 * P], F32, mixer)
        v_tok = sb("v_tok", [P, TOK - 1, KVW], F32, mixer)
        attn_tok = sb("attn_tok", [P, 2, GQA * HD], F32, mixer)
        kv_dec = sb("kv_dec", [ND, 2, KVW], F32, mixer)
        k_tok = sb("k_tok", [P, KVW], F32, mixer)
        k_new = sb("k_new", [P, PAIRS, ND], F32, mixer)
        q_blocks = sb("q_blocks", [P, DEC_B * PAIRS, 2 * GQA * DEC_T], F32, mixer)
        u_new = sb("u_new", [P, 2, 2, ND], F32, mixer)
        bias = sb("bias", [P, 2 * WINDOW], F32, mixer)
        dec_bias = sb("dec_bias", [P, 2, NKEY], F32, mixer)
        dec_pen = sb("dec_pen", [P, 2, NKEY], F32, mixer)
        edge = sb("edge", [P, len(POOL_WINDOWS), PAD], F32, mixer)
        stats = sb("stats", [P, 4, 7, GQA], F32, mixer)
        dec_stats = sb("dec_stats", [P, 7, 4], F32, mixer)
        vT = run_a[:, 0:PAIRS * T].rearrange("p (e t) -> p e t", e=PAIRS)
        old_k_flat = old_k[:].rearrange("p b n -> p (b n)")
        old_kT = old_k_flat.rearrange("p (i w) -> p i w", w=P)
        run_bufs = [run_a[:].rearrange("p (e n) -> p e n", e=2), old_k_flat[:, 0:2 * ROW].rearrange("p (e n) -> p e n", e=2)]
        probs_flat = probs[:].rearrange("p a h k -> p (a h k)")
        state_tok = probs_flat[0:DEC_B * STATE, 0:PW]
        old_v = probs_flat.rearrange("p (b n) -> p b n", b=DEC_B)
        u_tok = v_tok[:].rearrange("p c n -> p (c n)")
        dec_PT = probs_T[:, 0, :].rearrange("p (c r) -> p c r", c=4)
        dec_PT_new = probs_T[0:ND, 1, :].rearrange("p (c r) -> p c r", c=4)
        dec_probs = sq_tmp[:, 0:4 * NKEY].rearrange("p (c k) -> p c k", c=4)
        mixer.close()
        x1T = sb("x1T", [P, KT, T])
        relu_buf = sb("relu_buf", [P, T])
        again = ExitStack()
        x_tok2 = sb("x_tok2", [P, TOK, D], F32, again)
        again.close()
        y_sum = sb("y_sum", [P, KT, T])
        mlp_hi = sb("mlp_hi", [P, UNIT_KT, T], F32R)
        mlp_lo = sb("mlp_lo", [P, UNIT_KT, T], F32R)

        vec_landed = [sem(f"vec_landed{i}") for i in range(7)]
        x_landed = [sem(f"x_landed{i}") for i in range(TOK)]
        x2_landed = [sem(f"x2_landed{i}") for i in range(TOK)]
        w_landed = [sem(f"w_landed{i}") for i in range(RAW_SLOTS)]
        state_landed = sem("state_landed")
        pads_clear = sem("pads_clear")
        cache_landed = [sem(f"cache_landed{i}") for i in range(2)]
        hi_split = sem("hi_split")
        lo_split = sem("lo_split")
        unit_used = sem("unit_used")
        first_done = sem("first_done")
        even_group_done = sem("even_group_done")
        tile_read = sem("tile_read")
        consts = sem("consts")
        vecs_turned = sem("vecs_turned")
        vecs_ready = sem("vecs_ready")
        small = sem("small")
        squares = sem("squares")
        x_turned = sem("x_turned")
        h_hi = sem("h_hi")
        h_lo = sem("h_lo")
        inv_ready = sem("inv_ready")
        root_ready = sem("root_ready")
        diag_ready = sem("diag_ready")
        spread = sem("spread")
        scale_ready = sem("scale_ready")
        sums_turned = sem("sums_turned")
        sq_ready = sem("sq_ready")
        sq_added = sem("sq_added")
        sum_clear = sem("sum_clear")
        state_turned = sem("state_turned")
        u_turned = sem("u_turned")
        u_copied = sem("u_copied")
        state_copied = sem("state_copied")
        run_ready = sem("run_ready")
        z_ready = sem("z_ready")
        z_hi = sem("z_hi")
        z_lo = sem("z_lo")
        mix_hi = sem("mix_hi")
        edge_ready = sem("edge_ready")
        bias_ready = sem("bias_ready")
        kv_turned = sem("kv_turned")
        kv_copied = sem("kv_copied")
        scores = sem("scores")
        scores_read = sem("scores_read")
        shift_ready = sem("shift_ready")
        exps = sem("exps")
        probs_turned = sem("probs_turned")
        probs_copied = sem("probs_copied")
        mixed = sem("mixed")
        mixed_read = sem("mixed_read")
        rows_turned = sem("rows_turned")
        rows_read = sem("rows_read")
        attn_hi = sem("attn_hi")
        attn_lo = sem("attn_lo")
        old_k_turned = sem("old_k_turned")
        old_k_act = sem("old_k_act")
        old_k_dve = sem("old_k_dve")
        q_zero = sem("q_zero")
        q_ready = sem("q_ready")
        dec_scores = sem("dec_scores")
        dec_shift = sem("dec_shift")
        dec_exps = sem("dec_exps")
        dec_norm = sem("dec_norm")
        dec_turned = sem("dec_turned")
        dec_copied = sem("dec_copied")
        dec_mixed = sem("dec_mixed")
        dec_hi = sem("dec_hi")
        x1_ready = sem("x1_ready")
        y_clear = sem("y_clear")
        relu_sq = sem("relu_sq")
        mlp_hi_ready = sem("mlp_hi_ready")
        mlp_lo_ready = sem("mlp_lo_ready")
        y_ready = sem("y_ready")
        y_turned = sem("y_turned")
        y_copied = [sem("y_copied_act"), sem("y_copied_dve")]
        y_stored = [sem(f"y_stored{i}") for i in range(8)]
        kept = sem("kept")
        u_stored = sem("u_stored")
        stored = sem("stored")

        N_STORED = 4

        def num(k, v, per=1):
            return k + v * per if not isinstance(v, int) or v else k

        def dec_out(half, h):
            src = banks[half * HD:(half + 1) * HD, 4, :].rearrange("d (b pair c) -> d pair b c", b=DEC_B, pair=PAIRS)[
                :, :, :, half * GQA * DEC_T + h * DEC_T:half * GQA * DEC_T + (h + 1) * DEC_T]
            r = slice((h % 2) * HD, (h % 2 + 1) * HD)
            e = half * 2 + h // 2
            return src, qT[r, 0:QT, SEQ:T].rearrange("d (pair e) (b t) -> d e pair b t", pair=PAIRS, t=DEC_T)[:, e]

        pool_order = [3, 2, 1, 0]

        def decode_part(ap):
            return ap[:, :, PAD + SEQ:ROW].rearrange("p e (b s) -> p e b s", s=LAST)

        def z_parts(g):
            e = slice(2 * g, 2 * g + 2)
            out = slice(QT + 2 * g, QT + 2 * g + 2)

            def parts(t):
                return t[:, out, 0:SEQ], t[:, out, SEQ:T].rearrange("p e (b t) -> p e b t", t=DEC_T)
            return (uT[:, e, PAD:PAD + SEQ], decode_part(uT[:, e, :])[:, :, :, STATE:LAST]), parts(acts_hi), parts(acts_lo)

        steps = (TOK - 1) * KV_HEADS

        SCORE_AT = (Q_PAIR0 + 1) * K_UNITS
        TURN_AT = SCORE_AT + 1
        MIX_AT = TURN_AT + 1
        ROWS_AT = MIX_AT + 1
        DEC_SCORE_AT = ROWS_AT + steps - 1
        DEC_TURN_AT = DEC_SCORE_AT + 2
        DEC_MIX_AT = DEC_TURN_AT + 1
        U_TURN_AT = [DEC_SCORE_AT + 1, DEC_SCORE_AT + 3, IN_UNITS - 3]
        Z_AT = [DEC_TURN_AT + 1, IN_UNITS - 5, IN_UNITS - 2]

        block = ctx.enter_context(nc.Block())

        @block.sync
        def _(sp):
            rows = [(g_pre_mix, 0, KT), (g_post_mix, KT, KT), (g_pre_ffn, 2 * KT, KT), (g_post_ffn, 3 * KT, KT),
                    (pool_scale, 4 * KT, UT)]
            for i, (vec, at, n) in enumerate(rows):
                sp.dma_start(vec_rows[at:at + n, :], vec[0].rearrange("(k p) -> k p", p=P)).then_inc(vec_landed[i], 16)
            sp.dma_start(sink_row[:], attn_sinks).then_inc(vec_landed[5], 16)
            with nc.allow_non_contiguous_dma("16 sinks, by head within a pair of groups"):
                sp.dma_start(sink_hh[:], attn_sinks[0].rearrange("(pair hh) -> hh pair", pair=PAIRS)).then_inc(vec_landed[6], 16)
            for c in range(TOK - 1):
                sp.dma_start(x_tok[:, c, :], x_prompt[0, c * P:(c + 1) * P, :]).then_inc(x_landed[c], 16)
            sp.dma_start(x_tok[0:ND, TOK - 1, :], x_sample.rearrange("b t d -> (b t) d")).then_inc(x_landed[TOK - 1], 16)

            def load(k, v, src):
                if k >= RAW_SLOTS or not isinstance(v, int):
                    sp.wait_ge(lo_split, num(k - RAW_SLOTS + 1, v, 4))
                s = k % RAW_SLOTS
                sp.dma_start(w_raw[:, s, :].rearrange("p (k n) -> p k n", k=UNIT_KT), src).then_inc(w_landed[s], 16)

            columns = [QW, QW + KVW] + [g * UNIT_N for g in range(KV_HEADS)] + [QW + 2 * KVW + g * UNIT_N for g in pool_order]
            for pair, n0 in enumerate(columns):
                for kq in range(K_UNITS):
                    load(pair * K_UNITS + kq, 0, w_in_v[kq, :, :, n0:n0 + UNIT_N])
            for j in range(POOL_UNITS):
                load(U_POOL + j, 0, w_pool_v[pool_order[2 * j] // 2])
            with sp.Fori(0, OUT_PAIRS) as pair:
                for kq in range(K_UNITS):
                    load(U_OUT + kq, pair, w_out_v[kq, :, :, bass.ts(pair, UNIT_N)])
            with sp.Fori(0, CHUNKS) as c:
                for b in range(UP_PAIRS):
                    for kq in range(K_UNITS):
                        load(U_FFN + b * K_UNITS + kq, c * (CHUNK_UNITS // 4),
                             w_up_v[kq, :, :, bass.ds(c * CHUNK + b * UNIT_N, UNIT_N)])
                for n in range(OUT_PAIRS):
                    load(U_FFN + UP_PAIRS * K_UNITS + n, c * (CHUNK_UNITS // 4),
                         w_down_v[bass.ds(c, 1), :, :, n * UNIT_N:(n + 1) * UNIT_N].rearrange("o p k n -> (o p) k n"))

            for kg in range(KT // 4):
                for c in range(TOK):
                    o = kg * TOK + c
                    sp.wait_ge(y_copied[o % 2], o // 2 + 1)
                    dst = (y_prompt[0, c * P:(c + 1) * P, :] if c < TOK - 1 else y_sample.rearrange("b t d -> (b t) d"))
                    sp.dma_start(dst[:, kg * 512:(kg + 1) * 512],
                                 w_raw[0:tok_rows[c], :, :].rearrange("p s n -> p (s n)")[:, (o % 8) * 512:(o % 8 + 1) * 512]
                                 ).then_inc(y_stored[o % 8], 16)
            for i in range(8):
                sp.wait_ge(y_stored[i], 16 * len(range(i, TOK * KT // 4, 8)))
            sp.wait_ge(kept, 16 * 3)
            sp.wait_ge(u_stored, 16 * 2)
            sp.wait_ge(stored, 16 * N_STORED)

        @block.gpsimd
        def _(gp):
            nc.gpsimd.memset(ident[:], 0.0).then_inc(consts, 1)
            nc.gpsimd.memset(ones[:], 1.0).then_inc(consts, 1)
            nc.gpsimd.memset(ss[:], 1.0).then_inc(consts, 1)
            nc.gpsimd.memset(head_rows[:], 1.0).then_inc(consts, 1)
            for hh in range(2 * GQA):
                nc.gpsimd.memset(slope_row[:].rearrange("o (b hh t) -> o b hh t", b=4, t=DEC_T)[:, :, hh, :],
                                 2.0 ** (-8.0 * (hh + 1) / HEADS)).then_inc(consts, 1)
            for pair in range(PAIRS):
                nc.gpsimd.memset(slope_pair[:, pair:pair + 1], 2.0 ** (-8.0 * 2 * GQA * pair / HEADS)).then_inc(consts, 1)
            nc.gpsimd.iota(row_i[:, 0:1], pattern=[[0, 1]], base=0, channel_multiplier=1).then_inc(consts, 1)
            n = 5 + 2 * GQA + PAIRS
            gp.wait_ge(consts, n)
            nc.gpsimd.affine_select(out=ident[:], in_=ident[:], compare_op=ALU.not_equal, fill=1.0, base=0,
                                    pattern=[[-1, P]], channel_multiplier=1).then_inc(consts, 1)
            hr = head_rows[:].rearrange("h (b hh t) -> h b hh t", b=4, t=DEC_T)
            nc.gpsimd.affine_select(out=hr, in_=hr, compare_op=ALU.is_equal, fill=0.0, base=0,
                                    pattern=[[0, 4], [1, 2 * GQA], [0, DEC_T]], channel_multiplier=-1).then_inc(consts, 1)

            gp.wait_ge(x_turned, KT)
            nc.gpsimd.memset(uT[:, :, 0:PAD], 0.0).then_inc(pads_clear, 1)
            nc.gpsimd.memset(edge[:], 1.0).then_inc(edge_ready, 1)
            gp.wait_ge(edge_ready, 1)
            n_edge = 1
            for g, w in enumerate(POOL_WINDOWS):
                for t in range(w - 1):
                    nc.gpsimd.memset(edge[:, g, t:t + 1], float(w) / (t + 1)).then_inc(edge_ready, 1)
                    n_edge += 1

            nc.gpsimd.iota(bias[:], pattern=[[1, 2 * WINDOW]], base=-WINDOW, channel_multiplier=-1,
                           allow_small_or_imprecise_dtypes=True).then_inc(bias_ready, 1)
            gp.wait_ge(bias_ready, 1)
            nc.gpsimd.affine_select(out=bias[:], in_=bias[:], compare_op=ALU.is_ge, fill=MASKED, base=WINDOW,
                                    pattern=[[-1, 2 * WINDOW]], channel_multiplier=1).then_inc(bias_ready, 1)
            gp.wait_ge(bias_ready, 2)
            nc.gpsimd.affine_select(out=bias[:], in_=bias[:], compare_op=ALU.is_gt, fill=MASKED, base=0,
                                    pattern=[[1, 2 * WINDOW]], channel_multiplier=-1).then_inc(bias_ready, 1)
            nc.gpsimd.iota(dec_bias[:, 0, 0:WINDOW], pattern=[[1, WINDOW]], base=-WINDOW, channel_multiplier=0,
                           allow_small_or_imprecise_dtypes=True).then_inc(bias_ready, 1)
            nc.gpsimd.iota(dec_bias[:, 0, WINDOW:NKEY], pattern=[[0, DEC_B], [1, DEC_T]], base=0, channel_multiplier=0,
                           allow_small_or_imprecise_dtypes=True).then_inc(bias_ready, 1)
            nc.gpsimd.iota(dec_pen[:, 0, WINDOW:NKEY], pattern=[[1, DEC_B], [0, DEC_T]], base=0, channel_multiplier=0,
                           allow_small_or_imprecise_dtypes=True).then_inc(bias_ready, 1)
            nc.gpsimd.memset(q_blocks[:], 0.0).then_inc(q_zero, 1)

            gp.wait_ge(pads_clear, 1)
            gp.wait_ge(state_copied, 2)
            gp.wait_ge(kv_turned, 1)
            gp.wait_ge(dec_scores, 1)
            n_run = 0
            for p, g in enumerate(pool_order[:-1]):
                gp.wait_ge(tile_read, 2 * (U_PAIR0 + p) + 2)
                if p > 0:
                    gp.wait_ge(z_ready, p)
                src = uT[:, 2 * g:2 * g + 2, :]
                for level in range(g + 1):
                    half = 1 << level
                    dst = run_bufs[level % 2]
                    if level > 0:
                        gp.wait_ge(run_ready, n_run)
                    nc.gpsimd.tensor_tensor(dst[:, :, 2 * half - 1:ROW], src[:, :, 2 * half - 1:ROW],
                                            src[:, :, half - 1:ROW - half], ALU.add).then_inc(run_ready, 1)
                    n_run += 1
                    src = dst

            def clear_sum(n):
                if n > 0:
                    gp.wait_ge(sums_turned, n)
                nc.gpsimd.memset(sq_sum[:], 0.0).then_inc(sum_clear, 1)
                gp.wait_ge(sum_clear, n + 1)

            def add(count, par):
                gp.wait_ge(sq_ready, count + 1)
                gp.wait_ge(sq_added, count) if not isinstance(count, int) or count else None
                nc.gpsimd.tensor_tensor(sq_sum[:], sq_sum[:], sq_tmp[:, par * T:(par + 1) * T], ALU.add).then_inc(sq_added, 1)

            clear_sum(0)
            for m in range(4):
                add(m, m % 2)
            with gp.Fori(1, KT // 4) as i:
                for m in range(4):
                    add(i * 4 + m, m % 2)
            clear_sum(1)
            for kt in range(KT):
                add(KT + kt, kt % 2)
            gp.wait_ge(x_turned, 2 * KT)
            nc.gpsimd.memset(y_sum[:], 0.0).then_inc(y_clear, 1)
            clear_sum(2)
            for n in range(KT):
                add(2 * KT + n, n % 2)

        @block.scalar
        def _(act):
            def split(k, v=0):
                act.wait_ge(w_landed[k % RAW_SLOTS], num(16 * (k // RAW_SLOTS + 1), v, 16))
                if k >= SPLIT_SLOTS or not isinstance(v, int):
                    act.wait_ge(unit_used, num(k - SPLIT_SLOTS + 1, v, 4))
                nc.scalar.activation(w_hi[:, k % SPLIT_SLOTS, :], w_raw[:, k % RAW_SLOTS, :], ACT.Copy).then_inc(hi_split, 1)

            def take_root(n):
                act.wait_ge(inv_ready, n + 1)
                nc.scalar.activation(root[:], inv[:], ACT.Sqrt).then_inc(root_ready, 1)

            for c in range(TOK):
                r = tok_rows[c]
                act.wait_ge(x_landed[c], 16)
                if c == 0:
                    act.wait_ge(consts, 3)
                else:
                    act.wait_ge(squares, c)
                nc.scalar.activation(acts_lo[0:r, 0:4, 0:512], x_tok[0:r, c, :].rearrange("p (a b) -> p a b", a=4), ACT.Square,
                                     accum_out=ss[0:r, c:c + 1]).then_inc(squares, 1)
            act.wait_ge(vecs_ready, 1)
            take_root(0)
            for kt in range(KT):
                act.wait_ge(x_turned, kt + 1)
                nc.scalar.activation(acts_hi[:, kt, :], flat(2 * (kt % 4), T), ACT.Copy, scale=g_pre[:, kt:kt + 1]).then_inc(h_hi, 1)
                if kt in (2, 6):
                    split(kt // 4)
            act.wait_ge(x_turned, KT)
            act.wait_ge(vecs_turned, 1)
            act.dma_start(state_tok, state_pool[0].rearrange("b s c -> (b s) c")).then_inc(state_landed, 16)
            act.dma_start(k_sample[0, :, 0:WINDOW - DEC_T].rearrange("b w h d -> b (w h d)"),
                          cache_k[0, :, DEC_T:WINDOW].rearrange("b w h d -> b (w h d)")).then_inc(kept, 16)
            act.dma_start(v_sample[0, :, 0:WINDOW - DEC_T].rearrange("b w h d -> b (w h d)"),
                          cache_v[0, :, DEC_T:WINDOW].rearrange("b w h d -> b (w h d)")).then_inc(kept, 16)
            act.dma_start(pool_sample[0, :, 0:STATE - DEC_T].rearrange("b s c -> b (s c)"),
                          state_pool[0, :, DEC_T:STATE].rearrange("b s c -> b (s c)")).then_inc(kept, 16)
            act.dma_start(old_k[:], cache_k[0].rearrange("b w h d -> w b (h d)")).then_inc(cache_landed[0], 16)

            def exponentials(s):
                blk = s % (TOK - 1)
                lo = WINDOW if blk == 0 else 0
                act.wait_ge(shift_ready, s + 1)
                if s >= 4:
                    act.wait_ge(mixed_read, s - 3)
                for h in range(GQA):
                    nc.scalar.activation(probs[:, s % 2, h, lo:], probs[:, s % 2, h, lo:], ACT.Exp,
                                         bias=stats[:, s % 4, 0, h:h + 1], accum_out=stats[:, s % 4, 2, h:h + 1]).then_inc(exps, 1)
                nc.scalar.activation(stats[:, s % 4, 3, :], stats[:, s % 4, 1, :], ACT.Exp).then_inc(exps, 1)

            def copy_turned(s, r):
                n = 2 * P if s % (TOK - 1) == 0 else 4 * P
                act.wait_ge(probs_turned, 2 * s + r + 1)
                if s > 0:
                    act.wait_ge(mixed, s)
                nc.scalar.activation(probs_T[:, r, 0:n], banks[:, 6, 0:n], ACT.Copy).then_inc(probs_copied, 1)

            def new_rows(p):
                act.wait_ge(u_turned, p + 1)
                if p == 0:
                    act.wait_ge(mixed, steps)
                    act.wait_ge(stored, 16 * N_STORED)
                cols = slice(pool_order[p] * UNIT_N, (pool_order[p] + 1) * UNIT_N)
                nc.scalar.activation(u_tok[0:STATE, cols], banks[0:STATE, 5, 0:UNIT_N], ACT.Copy).then_inc(u_copied, 1)
                nc.scalar.activation(u_tok[ND:2 * ND, cols], banks[0:ND, 5, UNIT_N:2 * UNIT_N], ACT.Copy).then_inc(u_copied, 1)

            for j in range(IN_UNITS):
                if j + 2 <= U_POOL:
                    split(j + 2)
                if j == 2 * K_UNITS:
                    act.wait_ge(kv_turned, 1)
                    nc.scalar.activation(v_tok[:].rearrange("p b n -> p (b n)"), flat(4, (TOK - 1) * KVW), ACT.Copy).then_inc(kv_copied, 1)
                    act.wait_ge(kv_copied, 3)
                    act.dma_start(k_prompt[0, 0].rearrange("w h d -> w (h d)"), k_tok[:]).then_inc(stored, 16)
                    for i, dst in enumerate((k_sample, v_sample)):
                        act.dma_start(dst[0, :, WINDOW - DEC_T:WINDOW].rearrange("b t h d -> b t (h d)"), kv_dec[:, i, :]).then_inc(stored, 16)
                    act.dma_start(v_prompt[0, 0].rearrange("w h d -> w (h d)"), v_tok[:, TOK - 2, :]).then_inc(stored, 16)
                if j == 2 * K_UNITS + 1:
                    for r in range(2):
                        act.wait_ge(old_k_turned, r + 1)
                        nc.scalar.activation(old_kT[:, 4 * r:4 * r + 4, :].rearrange("p a k -> p (a k)"), banks[:, 4 + r, :],
                                             ACT.Copy).then_inc(old_k_act, 1)
                s = j - TURN_AT
                if 0 <= s < steps:
                    copy_turned(s, 0)
                if 0 <= s + 1 < steps:
                    exponentials(s + 1)
                if 0 <= s < steps:
                    copy_turned(s, 1)
                if s == steps:
                    act.wait_ge(probs_turned, 2 * steps)
                    act.dma_start(old_v, cache_v[0].rearrange("b w h d -> w b (h d)")).then_inc(cache_landed[1], 16)
                if j == DEC_SCORE_AT:
                    act.wait_ge(dec_shift, 1)
                    for ck in range(4):
                        nc.scalar.activation(dec_probs[:, ck, :], dec_probs[:, ck, :], ACT.Exp, bias=dec_stats[:, 0, ck:ck + 1],
                                             accum_out=dec_stats[:, 2, ck:ck + 1]).then_inc(dec_exps, 1)
                    nc.scalar.activation(dec_stats[:, 3, :], dec_stats[:, 1, :], ACT.Exp).then_inc(dec_exps, 1)
                if j == DEC_TURN_AT - 1:
                    act.wait_ge(dec_turned, 1)
                    nc.scalar.activation(dec_PT.rearrange("p a r -> p (a r)"), banks[:, 6, :], ACT.Copy).then_inc(dec_copied, 1)
                if j == DEC_MIX_AT:
                    act.wait_ge(dec_mixed, 1)
                    for half in range(2):
                        for h in range(GQA):
                            src, dst = dec_out(half, h)
                            nc.scalar.activation(dst, src, ACT.Copy).then_inc(dec_hi, 1)
                for p, at in enumerate(U_TURN_AT):
                    if j == at:
                        new_rows(p)
            new_rows(len(pool_order) - 1)
            act.wait_ge(u_copied, 2 * len(pool_order))
            act.dma_start(pool_prompt[0, 0], u_tok[0:STATE, :]).then_inc(u_stored, 16)
            act.dma_start(pool_sample[0, :, STATE - DEC_T:STATE], u_tok[ND:2 * ND, :]).then_inc(u_stored, 16)

            def z_high(p):
                act.wait_ge(z_ready, p + 1)
                src, hi, _ = z_parts(pool_order[p])
                for part in range(2):
                    nc.scalar.activation(hi[part], src[part], ACT.Copy).then_inc(z_hi, 1)

            def mix_high(p):
                if p % 2 == 0:
                    act.wait_ge(even_group_done, p // 2 + 1)
                else:
                    act.wait_ge(unit_used, U_POOL + p // 2 + 1)
                for nt in range(2):
                    m = 2 * pool_order[p] + nt
                    out = acts_hi[:, QT + m, :].rearrange("p (h t) -> p h t", h=2)
                    nc.scalar.activation(out, slot((p % 2) * 2 + nt), ACT.Copy, scale=p_scale[:, m:m + 1]).then_inc(mix_hi, 1)

            def attn_high(r):
                act.wait_ge(rows_read, steps)
                act.wait_ge(dec_hi, 2 * GQA)
                nc.scalar.activation(acts_hi[:, 4 * r:4 * r + 4, :], qT[:, 4 * r:4 * r + 4, :], ACT.Copy).then_inc(attn_hi, 1)

            act.wait_ge(unit_used, IN_UNITS)
            for p in range(3):
                z_high(p)
            split(U_POOL + 1)
            z_high(3)
            mix_high(0)
            attn_high(0)
            mix_high(1)
            split(U_OUT)
            attn_high(1)
            mix_high(2)
            mix_high(3)
            act.wait_ge(attn_lo, 2)
            act.wait_ge(z_lo, 2 * len(pool_order))
            act.wait_ge(stored, 16 * N_STORED)
            act.wait_ge(u_stored, 32)
            for c in range(TOK - 1):
                act.dma_start(x_tok2[:, c, :], x_prompt[0, c * P:(c + 1) * P, :]).then_inc(x2_landed[c], 16)
            act.dma_start(x_tok2[0:ND, TOK - 1, :], x_sample.rearrange("b t d -> (b t) d")).then_inc(x2_landed[TOK - 1], 16)

            def square(src, count, par):
                if not isinstance(count, int) or count >= 2:
                    act.wait_ge(sq_added, count - 1)
                nc.scalar.activation(sq_tmp[:, par * T:(par + 1) * T].rearrange("p (h t) -> p h t", h=2), src,
                                     ACT.Square).then_inc(sq_ready, 1)

            def out_pair(k, v, pair_k, pair_v, count):
                for kq in range(K_UNITS):
                    split(k + kq + 1, v)
                for nt in range(2):
                    if nt == 0:
                        act.wait_ge(first_done, num(pair_k + 1, pair_v))
                    else:
                        act.wait_ge(unit_used, num(k + K_UNITS, v, 4))
                    square(slot((pair_k % 2) * 2 + nt), count + nt, nt)

            for b in range(2):
                out_pair(U_OUT + b * K_UNITS, 0, P_OUT + b, 0, 2 * b)
            with act.Fori(1, OUT_PAIRS // 2) as i:
                for b in range(2):
                    out_pair(U_OUT + b * K_UNITS, i * 2, P_OUT + b, i * 2, i * 4 + 2 * b)

            take_root(1)
            act.wait_ge(spread, 2)
            for kt in range(KT):
                act.wait_ge(x1_ready, kt + 1)
                nc.scalar.activation(acts_hi[:, kt, :], x1T[:, kt, :], ACT.Copy, scale=g_ffn[:, kt:kt + 1]).then_inc(h_hi, 1)
                square(x1T[:, kt, :].rearrange("p (h t) -> p h t", h=2), KT + kt, kt % 2)
            take_root(2)

            def chunk(c, last=False):
                v = c * (CHUNK_UNITS // 4)
                for b in range(UP_PAIRS):
                    for kq in range(K_UNITS):
                        split(U_FFN + b * K_UNITS + kq + 1, v)
                    for nt in range(2):
                        j = 2 * b + nt
                        act.wait_ge(tile_read, num(2 * P_FFN + j + 1, c, CHUNK_TILES))
                        nc.scalar.activation(mlp_hi[:, j, :], relu_buf[:], ACT.Square).then_inc(mlp_hi_ready, 1)
                for n in range(OUT_PAIRS):
                    k = U_FFN + UP_PAIRS * K_UNITS + n + 1
                    if not last or n + 1 < OUT_PAIRS:
                        split(k, v)
                    if last:
                        for nt in range(2):
                            m = 2 * n + nt
                            act.wait_ge(tile_read, num(2 * P_FFN + 2 * UP_PAIRS + m + 1, c, CHUNK_TILES))
                            square(y_sum[:, m, :].rearrange("p (h t) -> p h t", h=2), 2 * KT + m, m % 2)

            with act.Fori(0, CHUNKS - 1) as c:
                chunk(c)
            chunk(CHUNKS - 1, last=True)
            take_root(3)
            for kg in range(KT // 4):
                for c in range(TOK):
                    o = kg * TOK + c
                    if o % 2 == 0:
                        act.wait_ge(y_turned, o + 1)
                        if o >= 8:
                            act.wait_ge(y_stored[o % 8], 16 * (o // 8))
                        r = tok_rows[c]
                        nc.scalar.activation(w_raw[0:r].rearrange("p s n -> p (s n)")[:, (o % 8) * 512:(o % 8 + 1) * 512],
                                             banks[0:r, o % 8, :], ACT.Copy).then_inc(y_copied[0], 1)

        @block.vector
        def _(dve):
            chained = [0]

            def step(ins):
                ins.then_inc(small, 1)
                chained[0] += 1
                dve.wait_ge(small, chained[0])

            def split(k, v=0):
                dve.wait_ge(hi_split, num(k + 1, v, 4))
                nc.vector.tensor_tensor(w_lo[:, k % SPLIT_SLOTS, :], w_raw[:, k % RAW_SLOTS, :],
                                        w_hi[:, k % SPLIT_SLOTS, :].bitcast(F32), ALU.subtract).then_inc(lo_split, 1)

            def row_scales(n, target):
                if n == 0:
                    dve.wait_ge(squares, TOK)
                else:
                    dve.wait_ge(sums_turned, n)
                    nc.vector.tensor_copy(ss[:, 0:TOK - 1], banks[:, 6, 0:TOK - 1])
                    step(nc.vector.tensor_copy(ss[0:ND, TOK - 1:TOK], banks[0:ND, 6, TOK - 1:TOK]))
                step(nc.vector.tensor_scalar(var[:], ss[:], 1.0 / D, EPS, ALU.mult, ALU.add))
                nc.vector.reciprocal(inv[:], var[:]).then_inc(inv_ready, 1)
                dve.wait_ge(root_ready, n + 1)
                step(nc.vector.tensor_tensor(newton[:], root[:], root[:], ALU.mult))
                step(nc.vector.tensor_tensor(newton[:], newton[:], var[:], ALU.mult))
                step(nc.vector.tensor_scalar(newton[:], newton[:], -0.5, 1.5, ALU.mult, ALU.add))
                step(nc.vector.tensor_tensor(rstd[:], root[:], newton[:], ALU.mult))
                nc.vector.tensor_tensor(diag, ident[:].unsqueeze(1).broadcast_to([P, TOK, P]),
                                        rstd[:].unsqueeze(2).broadcast_to([P, TOK, P]), ALU.mult).then_inc(diag_ready, 1)
                dve.wait_ge(spread, n + 1)
                nc.vector.tensor_copy(target[:], flat(6, T)).then_inc(scale_ready, 1)

            dve.wait_ge(vecs_turned, 1)
            step(nc.vector.tensor_copy(sink_all[:], banks[:, 1, 0:HEADS]))
            step(nc.vector.tensor_scalar(neg_sink[:], sink_all[:], -1.0, None, ALU.mult))
            step(nc.vector.tensor_copy(dec_consts[:], banks[:, 1, HEADS:HEADS + 2 * PAIRS]))
            for bg in range(2):
                step(nc.vector.tensor_copy(dec_sink[:, bg, :], dec_consts[:, 0:PAIRS]))
            step(nc.vector.tensor_scalar(neg_dec_sink[:], dec_sink[:], -1.0, None, ALU.mult))
            dve.wait_ge(consts, 5 + 2 * GQA + PAIRS)
            step(nc.vector.tensor_scalar(row_i[:, 1:2], row_i[:, 0:1], DEC_T - 1, None, ALU.bitwise_and))
            step(nc.vector.tensor_scalar(row_i[:, 2:3], row_i[:, 0:1], 5, None, ALU.logical_shift_right))
            step(nc.vector.tensor_copy(row_t[:], row_i[:, 1:3]))
            nc.vector.tensor_copy(vecs[:], banks[:, 0, 0:4 * KT + UT]).then_inc(vecs_ready, 1)

            def first_low(kt):
                dve.wait_ge(h_hi, kt + 1)
                nc.vector.scalar_tensor_tensor(out=acts_lo[:, kt, :], in0=flat(2 * (kt % 4), T), scalar=g_pre[:, kt:kt + 1],
                                               in1=acts_hi[:, kt, :].bitcast(F32), op0=ALU.mult, op1=ALU.subtract).then_inc(h_lo, 1)

            dve.wait_ge(squares, TOK)
            step(nc.vector.tensor_scalar(var[:], ss[:], 1.0 / D, EPS, ALU.mult, ALU.add))
            nc.vector.reciprocal(inv[:], var[:]).then_inc(inv_ready, 1)
            dve.wait_ge(vecs_ready, 1)
            for kt in range(KT):
                first_low(kt)
                if kt in (2, 6):
                    split(kt // 4)
            dve.wait_ge(root_ready, 1)
            step(nc.vector.tensor_tensor(newton[:], root[:], root[:], ALU.mult))
            step(nc.vector.tensor_tensor(newton[:], newton[:], var[:], ALU.mult))
            step(nc.vector.tensor_scalar(newton[:], newton[:], -0.5, 1.5, ALU.mult, ALU.add))
            step(nc.vector.tensor_tensor(rstd[:], root[:], newton[:], ALU.mult))
            nc.vector.tensor_tensor(diag, ident[:].unsqueeze(1).broadcast_to([P, TOK, P]),
                                    rstd[:].unsqueeze(2).broadcast_to([P, TOK, P]), ALU.mult).then_inc(diag_ready, 1)
            dve.wait_ge(spread, 1)
            nc.vector.tensor_copy(gemm_scale[:], flat(6, T)).then_inc(scale_ready, 1)

            def halves(ap):
                return ap.rearrange("p o (h t) -> p (o h) t", h=2)

            def pair_ready(nt, k, v, pair_k, pair_v):
                if nt == 0:
                    dve.wait_ge(first_done, num(pair_k + 1, pair_v))
                else:
                    dve.wait_ge(unit_used, num(k + K_UNITS, v, 4))

            scale2 = gemm_scale[:].rearrange("p (h t) -> p h t", h=2)
            dve.wait_ge(scale_ready, 1)

            def tile_evacuated(ins):
                ins.then_inc(tile_read, 1)

            def read_q(g, nt, src):
                return nc.vector.scalar_tensor_tensor(
                    out=qT[:, 2 * g + nt, :].rearrange("p (h t) -> p h t", h=2), in0=src, scalar=HD ** -0.5,
                    in1=scale2, op0=ALU.mult, op1=ALU.mult)

            def read_k(nt, src):
                for half in range(2):
                    rows = slice(half * HD, (half + 1) * HD)
                    for copy in range(2):
                        ins = nc.vector.tensor_tensor(
                            k_twice[copy * HD:(copy + 1) * HD, 2 * nt + half, :].rearrange("p (h t) -> p h t", h=2),
                            src[rows], scale2[rows], ALU.mult)
                        if half + copy < 2:
                            ins.then_inc(small, 1)
                            chained[0] += 1
                return ins

            def read_u(p, nt, src):
                u = uT[:, 2 * pool_order[p] + nt, :]
                n = SEQ - H
                nc.vector.tensor_tensor(u[:, PAD:PAD + H], src[:, 0, :], scale2[:, 0, :], ALU.mult).then_inc(small, 1)
                nc.vector.tensor_tensor(u[:, PAD + H:PAD + SEQ], src[:, 1, 0:n], scale2[:, 1, 0:n], ALU.mult).then_inc(small, 1)
                if p >= 2:
                    dve.wait_ge(u_turned, p - 1)
                nc.vector.tensor_tensor(u_new[:, p % 2, nt, :], src[:, 1, n:H], scale2[:, 1, n:H], ALU.mult).then_inc(small, 1)
                chained[0] += 3
                by_batch = "p (b t) -> p b t"
                return nc.vector.tensor_tensor(
                    u[:, PAD + SEQ:ROW].rearrange("p (b s) -> p b s", s=LAST)[:, :, STATE:LAST],
                    src[:, 1, n:H].rearrange(by_batch, t=DEC_T), scale2[:, 1, n:H].rearrange(by_batch, t=DEC_T), ALU.mult)

            def read_pair(pair):
                for nt in range(2):
                    pair_ready(nt, pair * K_UNITS, 0, pair, 0)
                    src = slot((pair * 2 if pair < Q_PAIR0 else 0) + nt)
                    if pair == 0:
                        ins = read_k(nt, src)
                    elif pair == 1:
                        ins = nc.vector.tensor_tensor(vT[:, nt, :].rearrange("p (h t) -> p h t", h=2), src, scale2, ALU.mult)
                    elif pair < U_PAIR0:
                        ins = read_q(pair - Q_PAIR0, nt, src)
                    else:
                        ins = read_u(pair - U_PAIR0, nt, src)
                    ins.then_inc(tile_read, 1)

            def decode_masks(bg):
                new = slice(WINDOW, NKEY)
                step(nc.vector.tensor_scalar(dec_pen[:, bg, new], dec_pen[:, 0, new], row_t[:, 1:2], 4.0 * bg,
                                             ALU.subtract, ALU.not_equal))
                step(nc.vector.tensor_scalar(dec_pen[:, bg, new], dec_pen[:, bg, new], MASKED, None, ALU.mult))
                step(nc.vector.tensor_scalar(dec_bias[:, bg, :], dec_bias[:, 0, :], row_t[:, 0:1], None, ALU.subtract))
                step(nc.vector.tensor_scalar(dec_pen[:, bg, 0:WINDOW], dec_bias[:, bg, 0:WINDOW], -float(WINDOW), MASKED,
                                             ALU.is_le, ALU.mult))
                step(nc.vector.tensor_tensor(dec_pen[:, bg, :], dec_pen[:, bg, :], dec_bias[:, bg, :], ALU.add))
                step(nc.vector.tensor_scalar(dec_bias[:, bg, new], dec_bias[:, bg, new], 0.0, MASKED, ALU.is_gt, ALU.mult))
                step(nc.vector.tensor_tensor(dec_pen[:, bg, new], dec_pen[:, bg, new], dec_bias[:, bg, new], ALU.add))

            def decode_queries():
                dve.wait_ge(q_zero, 1)
                dve.wait_ge(tile_read, 2 * U_PAIR0)
                for pair in range(PAIRS):
                    for half in range(2):
                        for odd in range(2):
                            w = GQA * DEC_T
                            dst = q_blocks[half * HD:(half + 1) * HD, :, half * w:(half + 1) * w].rearrange(
                                "d (b pair) (e odd t) -> d pair odd e b t", pair=PAIRS, odd=2, t=DEC_T)[:, pair, odd]
                            e = 4 * pair + 2 * half
                            src = qT[odd * HD:(odd + 1) * HD, e:e + 2, SEQ:T].rearrange("d e (b t) -> d e b t", t=DEC_T)
                            nc.vector.tensor_copy(dst, src).then_inc(q_ready, 1)

            def shift_scores(s):
                g, blk = divmod(s, TOK - 1)
                par, st = s % 2, s % 4
                lo = WINDOW if blk == 0 else 0
                dve.wait_ge(scores, s + 1)
                if s >= 2:
                    dve.wait_ge(probs_turned, 2 * (s - 1))
                if s >= 4:
                    dve.wait_ge(mixed_read, s - 3)
                for h in range(GQA):
                    slope = 2.0 ** (-8.0 * (g * GQA + h + 1) / HEADS)
                    nc.vector.scalar_tensor_tensor(
                        out=probs[:, par, h, lo:], in0=bias[:, lo:], scalar=slope,
                        in1=banks[:, 4 + h % 2, (h // 2) * 256 + lo:(h // 2) * 256 + 256],
                        op0=ALU.mult, op1=ALU.add).then_inc(scores_read, 1)
                dve.wait_ge(scores_read, GQA * (s + 1))
                step(nc.vector.tensor_reduce(stats[:, st, 4, :], probs[:, par, :, lo:], AX.X, ALU.max, negate=True))
                step(nc.vector.tensor_tensor(stats[:, st, 0, :], stats[:, st, 4, :],
                                             neg_sink[:, g * GQA:(g + 1) * GQA], ALU.min))
                nc.vector.tensor_tensor(stats[:, st, 1, :], sink_all[:, g * GQA:(g + 1) * GQA], stats[:, st, 0, :],
                                        ALU.add).then_inc(shift_ready, 1)

            def normalise(s):
                st = s % 4
                dve.wait_ge(exps, (GQA + 1) * (s + 1))
                step(nc.vector.tensor_tensor(stats[:, st, 5, :], stats[:, st, 2, :], stats[:, st, 3, :], ALU.add))
                step(nc.vector.reciprocal(stats[:, st, 6, :], stats[:, st, 5, :]))
                dve.wait_ge(mixed, s + 1)
                if s >= 2:
                    dve.wait_ge(rows_turned, s - 1)
                nc.vector.tensor_tensor(attn_tok[:, s % 2, :].rearrange("p (h d) -> p h d", h=GQA),
                                        banks[:, 7, 0:GQA * HD].rearrange("p (h d) -> p h d", h=GQA),
                                        stats[:, st, 6, :].unsqueeze(2).broadcast_to([P, GQA, HD]),
                                        ALU.mult).then_inc(mixed_read, 1)

            def rows_back(s):
                g, blk = divmod(s, TOK - 1)
                dve.wait_ge(rows_turned, s + 1)
                nc.vector.tensor_copy(qT[:, 2 * g:2 * g + 2, blk * P:(blk + 1) * P],
                                      banks[:, 7, 256:512].rearrange("p (a q) -> p a q", a=2)).then_inc(rows_read, 1)

            def decode_shift():
                dve.wait_ge(dec_scores, 1)
                for bg in range(2):
                    for pair in range(PAIRS):
                        step(nc.vector.scalar_tensor_tensor(
                            out=dec_probs[:, bg * PAIRS + pair, :], in0=dec_pen[:, bg, :], scalar=dec_slope[:, pair:pair + 1],
                            in1=banks[:, 4 + bg, pair * NKEY:(pair + 1) * NKEY], op0=ALU.mult, op1=ALU.add))
                step(nc.vector.tensor_reduce(dec_stats[:, 4, :], dec_probs, AX.X, ALU.max, negate=True))
                step(nc.vector.tensor_tensor(dec_stats[:, 0, :], dec_stats[:, 4, :],
                                             neg_dec_sink[:].rearrange("p b c -> p (b c)"), ALU.min))
                nc.vector.tensor_tensor(dec_stats[:, 1, :], dec_sink[:].rearrange("p b c -> p (b c)"), dec_stats[:, 0, :],
                                        ALU.add).then_inc(dec_shift, 1)

            def decode_normalise():
                dve.wait_ge(dec_exps, 5)
                step(nc.vector.tensor_tensor(dec_stats[:, 5, :], dec_stats[:, 2, :], dec_stats[:, 3, :], ALU.add))
                step(nc.vector.reciprocal(dec_stats[:, 6, :], dec_stats[:, 5, :]))
                nc.vector.tensor_tensor(dec_probs, dec_probs, dec_stats[:, 6, :].unsqueeze(2).broadcast_to([P, 4, NKEY]),
                                        ALU.mult).then_inc(dec_norm, 1)

            runs = [0]

            def pool_z(p):
                g = pool_order[p]
                w, e = POOL_WINDOWS[g], slice(2 * g, 2 * g + 2)
                run = run_bufs[g % 2]
                if g > 0:
                    runs[0] += g + 1
                    dve.wait_ge(run_ready, runs[0])
                else:
                    dve.wait_ge(z_ready, p)
                    dve.wait_ge(tile_read, 2 * IN_PAIRS)
                    step(nc.vector.tensor_tensor(run[:, :, 1:ROW], uT[:, e, 1:ROW], uT[:, e, 0:ROW - 1], ALU.add))
                dve.wait_ge(edge_ready, 1 + sum(w - 1 for w in POOL_WINDOWS))
                step(nc.vector.tensor_tensor(run[:, :, PAD:2 * PAD], run[:, :, PAD:2 * PAD],
                                             edge[:, g:g + 1, :].broadcast_to([P, 2, PAD]), ALU.mult))
                dve.wait_ge(u_turned, p + 1)
                nc.vector.scalar_tensor_tensor(out=uT[:, e, PAD:ROW], in0=run[:, :, PAD:ROW], scalar=1.0 / w,
                                               in1=uT[:, e, PAD:ROW], op0=ALU.mult, op1=ALU.subtract).then_inc(z_ready, 1)

            for j in range(IN_UNITS):
                if j % K_UNITS == K_UNITS - 1:
                    read_pair(j // K_UNITS)
                if j + 2 <= U_POOL:
                    split(j + 2)
                if j in (K_UNITS, K_UNITS + 1):
                    dve.wait_ge(bias_ready, 6)
                    decode_masks(K_UNITS + 1 - j)
                if j == 2 * K_UNITS:
                    dve.wait_ge(kv_turned, 1)
                    nc.vector.tensor_copy(kv_dec[:].rearrange("p b n -> p (b n)"), banks[0:ND, 6, :]).then_inc(kv_copied, 1)
                    nc.vector.tensor_copy(k_tok[:], banks[:, 7, 0:KVW]).then_inc(kv_copied, 1)
                    dve.wait_ge(tile_read, 2)
                    for half in range(2):
                        rows = slice(half * HD, (half + 1) * HD)
                        nc.vector.tensor_copy(k_new[rows], k_twice[rows, :, SEQ:T].rearrange(
                            "p (pair half) n -> p half pair n", half=2)[:, half]).then_inc(q_ready, 1)
                if j == 2 * K_UNITS + 2:
                    for r in range(2, 4):
                        dve.wait_ge(old_k_turned, r + 1)
                        nc.vector.tensor_copy(old_kT[:, 4 * r:4 * r + 4, :].rearrange("p a k -> p (a k)"),
                                              banks[:, 4 + r, :]).then_inc(old_k_dve, 1)
                if j == 2 * K_UNITS + 3:
                    dve.wait_ge(state_turned, 1)
                    for r in range(2):
                        nc.vector.tensor_copy(
                            decode_part(uT[:, 4 * r:4 * r + 4, :])[:, :, :, 0:STATE],
                            banks[:, 6 + r, 0:4 * DEC_B * STATE].rearrange("p (e b s) -> p e b s", e=4, b=DEC_B)
                        ).then_inc(state_copied, 1)
                s = j - MIX_AT
                if 0 <= s < steps:
                    normalise(s)
                if j == U_PAIR0 * K_UNITS:
                    decode_queries()
                if 0 <= s < steps:
                    rows_back(s)
                if 0 <= j + 1 - SCORE_AT < steps:
                    shift_scores(j + 1 - SCORE_AT)
                if j == DEC_SCORE_AT - 1:
                    decode_shift()
                if j == DEC_SCORE_AT:
                    decode_normalise()
                if j == DEC_TURN_AT - 1:
                    dve.wait_ge(dec_turned, 1)
                    nc.vector.tensor_copy(dec_PT_new.rearrange("p a r -> p (a r)"), banks[0:ND, 7, :]).then_inc(dec_copied, 1)
                for p, at in enumerate(Z_AT):
                    if j == at:
                        pool_z(p)
            pool_z(len(pool_order) - 1)

            def z_low(p):
                src, hi, lo = z_parts(pool_order[p])
                for part in range(2):
                    dve.wait_ge(z_hi, 2 * p + part + 1)
                    nc.vector.tensor_tensor(lo[part], src[part], hi[part].bitcast(F32), ALU.subtract).then_inc(z_lo, 1)

            def mix_low(p):
                for nt in range(2):
                    m = 2 * pool_order[p] + nt
                    dve.wait_ge(mix_hi, 2 * p + nt + 1)
                    shape = "p (h t) -> p h t"
                    nc.vector.scalar_tensor_tensor(
                        out=acts_lo[:, QT + m, :].rearrange(shape, h=2), in0=slot((p % 2) * 2 + nt),
                        scalar=p_scale[:, m:m + 1], in1=acts_hi[:, QT + m, :].bitcast(F32).rearrange(shape, h=2),
                        op0=ALU.mult, op1=ALU.subtract).then_inc(tile_read, 1)

            def attn_low(r):
                dve.wait_ge(attn_hi, r + 1)
                e = slice(4 * r, 4 * r + 4)
                nc.vector.tensor_tensor(acts_lo[:, e, :], qT[:, e, :], acts_hi[:, e, :].bitcast(F32),
                                        ALU.subtract).then_inc(attn_lo, 1)

            for p in range(3):
                z_low(p)
            split(U_POOL + 1)
            z_low(3)
            mix_low(0)
            attn_low(0)
            mix_low(1)
            split(U_OUT)
            attn_low(1)
            mix_low(2)
            mix_low(3)

            def out_pair(k, v, pair_k, pair_v, tile, count):
                for kq in range(K_UNITS):
                    split(k + kq + 1, v)
                for nt in range(2):
                    dve.wait_ge(sq_ready, count + nt + 1)
                    nc.vector.tensor_scalar(halves(x1T[:, tile(nt), :]), slot((pair_k % 2) * 2 + nt), 1.0, None,
                                            ALU.mult).then_inc(tile_read, 1)

            with dve.Fori(0, OUT_PAIRS // 2) as i:
                for b in range(2):
                    out_pair(U_OUT + b * K_UNITS, i * 2, P_OUT + b, i * 2,
                             lambda nt: bass.ds(i * 4 + 2 * b + nt, 1), i * 4 + 2 * b)

            row_scales(1, norm_scale)
            dve.wait_ge(scale_ready, 2)

            def second_low(kt):
                dve.wait_ge(h_hi, KT + kt + 1)
                nc.vector.scalar_tensor_tensor(out=acts_lo[:, kt, :], in0=x1T[:, kt, :], scalar=g_ffn[:, kt:kt + 1],
                                               in1=acts_hi[:, kt, :].bitcast(F32), op0=ALU.mult, op1=ALU.subtract).then_inc(h_lo, 1)

            for kt in range(KT):
                step(nc.vector.tensor_tensor(x1T[:, kt, :], x1T[:, kt, :], norm_scale[:], ALU.mult))
                dve.wait_ge(x_turned, KT + kt + 1)
                nc.vector.scalar_tensor_tensor(out=x1T[:, kt, :], in0=x1T[:, kt, :], scalar=g_post[:, kt:kt + 1],
                                               in1=flat(2 * (kt % 4), T), op0=ALU.mult, op1=ALU.add).then_inc(x1_ready, 1)
                if kt > 0:
                    second_low(kt - 1)
            second_low(KT - 1)
            row_scales(2, gemm_scale)
            dve.wait_ge(scale_ready, 3)

            dve.wait_ge(y_clear, 1)

            def chunk(c, last=False):
                v = c * (CHUNK_UNITS // 4)
                for b in range(UP_PAIRS):
                    k = U_FFN + b * K_UNITS
                    for kq in range(K_UNITS):
                        split(k + kq + 1, v)
                    for nt in range(2):
                        j = 2 * b + nt
                        pair_ready(nt, k, v, P_FFN + b, c * CHUNK_PAIRS)
                        nc.vector.scalar_tensor_tensor(
                            out=relu_buf[:].rearrange("p (h t) -> p h t", h=2), in0=slot(((P_FFN + b) % 2) * 2 + nt),
                            scalar=0.0, in1=scale2, op0=ALU.max, op1=ALU.mult).then_inc(tile_read, 1)
                        dve.wait_ge(tile_read, num(2 * P_FFN + j + 1, c, CHUNK_TILES))
                        nc.vector.tensor_tensor(sq_tmp[:, 0:T], relu_buf[:], relu_buf[:], ALU.mult).then_inc(relu_sq, 1)
                        dve.wait_ge(mlp_hi_ready, num(j + 1, c, 2 * UP_PAIRS))
                        dve.wait_ge(relu_sq, num(j + 1, c, 2 * UP_PAIRS))
                        nc.vector.tensor_tensor(mlp_lo[:, j, :], sq_tmp[:, 0:T], mlp_hi[:, j, :].bitcast(F32),
                                                ALU.subtract).then_inc(mlp_lo_ready, 1)
                for n in range(OUT_PAIRS):
                    k = U_FFN + UP_PAIRS * K_UNITS + n
                    if not last or n + 1 < OUT_PAIRS:
                        split(k + 1, v)
                    for nt in range(2):
                        m = 2 * n + nt
                        if nt == 0:
                            dve.wait_ge(first_done, num(P_FFN + UP_PAIRS + n + 1, c, CHUNK_PAIRS))
                        else:
                            dve.wait_ge(unit_used, num(k + 1, v, 4))
                        acc = y_sum[:, m, :].rearrange("p (h t) -> p h t", h=2)
                        nc.vector.tensor_tensor(acc, acc, slot(((P_FFN + UP_PAIRS + n) % 2) * 2 + nt),
                                                ALU.add).then_inc(tile_read, 1)

            with dve.Fori(0, CHUNKS - 1) as c:
                chunk(c)
            chunk(CHUNKS - 1, last=True)

            row_scales(3, norm_scale)
            dve.wait_ge(scale_ready, 4)
            o = 0
            for kg in range(KT // 4):
                for kt in range(4 * kg, 4 * kg + 4):
                    step(nc.vector.tensor_tensor(y_sum[:, kt, :], y_sum[:, kt, :], norm_scale[:], ALU.mult))
                    nc.vector.scalar_tensor_tensor(out=x1T[:, kt, :], in0=y_sum[:, kt, :], scalar=g_last[:, kt:kt + 1],
                                                   in1=x1T[:, kt, :], op0=ALU.mult, op1=ALU.add).then_inc(y_ready, 1)
                for c in range(TOK):
                    o = kg * TOK + c
                    if o % 2 == 1:
                        dve.wait_ge(y_turned, o + 1)
                        if o >= 8:
                            dve.wait_ge(y_stored[o % 8], 16 * (o // 8))
                        r = tok_rows[c]
                        nc.vector.tensor_copy(w_raw[0:r].rearrange("p s n -> p (s n)")[:, (o % 8) * 512:(o % 8 + 1) * 512],
                                              banks[0:r, o % 8, :]).then_inc(y_copied[1], 1)

        @block.tensor
        def _(pe):
            def turn_x(tok, kt, s):
                for c in range(TOK):
                    r = tok_rows[c]
                    ins = nc.tensor.transpose(flat(2 * s, T)[:, c * P:c * P + r], tok[0:r, c, kt * P:(kt + 1) * P],
                                              ident[0:r, 0:r])
                ins.then_inc(x_turned, 1)

            def spread_scales(n):
                pe.wait_ge(diag_ready, n + 1)
                for c in range(TOK):
                    r = tok_rows[c]
                    ins = nc.tensor.matmul(flat(6, T)[:, c * P:c * P + r], ones[0:r, :], diag[0:r, c, 0:r], start=True, stop=True)
                ins.then_inc(spread, 1)

            def turn_sums(n):
                pe.wait_ge(sq_added, n * KT)
                for c in range(TOK):
                    r = tok_rows[c]
                    ins = nc.tensor.matmul(banks[0:r, 6, c:c + 1], sq_sum[:, c * P:c * P + r], ones[:, 0:1], start=True, stop=True)
                ins.then_inc(sums_turned, 1)

            def product(out, s, kk, nt, hi, lo, start, stop):
                cols = slice(kk * UNIT_N + nt * P, kk * UNIT_N + (nt + 1) * P)
                wh, wl = w_hi[:, s, cols], w_lo[:, s, cols]
                terms = [(wh, hi, start, False), (wh, lo, False, False), (wl, hi, False, stop)]
                for w, x, first, last in terms:
                    for h in range(2):
                        ins = nc.tensor.matmul(out[:, h, :], w, x[:, h * H:(h + 1) * H], start=first, stop=last)
                return ins

            def pair_tiles(k, v, pair_k, pair_v, units, rows_ready=None):
                for q in range(units):
                    u = k + q
                    pe.wait_ge(lo_split, num(u + 1, v, 4))
                    if rows_ready:
                        rows_ready(q)
                    for nt in range(2):
                        if q == 0 and (pair_k >= 2 or not isinstance(pair_v, int)):
                            pe.wait_ge(tile_read, num(2 * pair_k - 3 + nt, pair_v, 2))
                        for kk in range(UNIT_KT):
                            kt = q * UNIT_KT + kk
                            ins = product(slot((pair_k % 2) * 2 + nt), u % SPLIT_SLOTS, kk, nt, acts_hi[:, kt, :],
                                          acts_lo[:, kt, :], kt == 0, kt == units * UNIT_KT - 1)
                        if q == units - 1 and nt == 0:
                            ins.then_inc(first_done, 1)
                    ins.then_inc(unit_used, 1)

            pe.wait_ge(consts, 7 + 2 * GQA + PAIRS)
            for i in range(7):
                pe.wait_ge(vec_landed[i], 16)
            n = 4 * KT + UT
            nc.tensor.transpose(banks[:, 0, 0:n], vec_rows[:], ident[0:n, 0:n])
            nc.tensor.matmul(banks[:, 1, 0:HEADS], ones[0:1, :], sink_row[:], start=True, stop=True)
            nc.tensor.matmul(banks[:, 1, HEADS:HEADS + PAIRS], head_rows[:], sink_hh[:], start=True, stop=True)
            nc.tensor.matmul(banks[:, 1, HEADS + PAIRS:HEADS + 2 * PAIRS], slope_row[:], slope_pair[:], start=True,
                             stop=True).then_inc(vecs_turned, 1)
            for c in range(TOK):
                pe.wait_ge(x_landed[c], 16)
            for kt in range(KT):
                if kt == 0:
                    pe.wait_ge(vecs_ready, 1)
                if kt >= 4:
                    pe.wait_ge(h_lo, kt - 3)
                turn_x(x_tok, kt, kt % 4)
            pe.wait_ge(h_lo, KT)
            spread_scales(0)
            pe.wait_ge(scale_ready, 1)

            def turn_new_keys():
                pe.wait_ge(tile_read, 2 * Q_PAIR0)
                for blk in range(TOK - 1):
                    for e in range(PAIRS):
                        nc.tensor.transpose(flat(4, 1024)[:, blk * KVW + e * P:blk * KVW + (e + 1) * P],
                                            vT[:, e, blk * P:(blk + 1) * P], ident[:])
                for g in range(KV_HEADS):
                    nc.tensor.transpose(banks[0:ND, 6, g * HD:(g + 1) * HD], k_twice[0:HD, g, SEQ:T], ident[0:HD, 0:HD])
                for e in range(PAIRS):
                    nc.tensor.transpose(banks[0:ND, 6, KVW + e * P:KVW + (e + 1) * P], vT[:, e, SEQ:T], ident[:])
                for g in range(KV_HEADS):
                    ins = nc.tensor.transpose(banks[:, 7, g * HD:(g + 1) * HD], k_twice[0:HD, g, SEQ - P:SEQ], ident[0:HD, 0:HD])
                ins.then_inc(kv_turned, 1)

            def turn_old_keys(r):
                for a in range(4):
                    b, pair = divmod(4 * r + a, PAIRS)
                    ins = nc.tensor.transpose(banks[:, 4 + r, a * P:(a + 1) * P], old_k[:, b, pair * P:(pair + 1) * P], ident[:])
                ins.then_inc(old_k_turned, 1)

            def turn_state():
                n = DEC_B * STATE
                pe.wait_ge(state_landed, 16)
                pe.wait_ge(old_k_dve, 2)
                for e in range(UT):
                    ins = nc.tensor.transpose(banks[:, 6 + e // 4, (e % 4) * n:(e % 4 + 1) * n],
                                              state_tok[:, e * P:(e + 1) * P], ident[0:n, 0:n])
                ins.then_inc(state_turned, 1)

            def score(s):
                g, blk = divmod(s, TOK - 1)
                lo = WINDOW if blk == 0 else 0
                keys = slice(max(blk - 1, 0) * P, (blk + 1) * P)
                if s == 0:
                    pe.wait_ge(old_k_act, 2)
                else:
                    pe.wait_ge(scores_read, GQA * s)
                pe.wait_ge(tile_read, 2 * (Q_PAIR0 + g) + 2)
                for h in range(GQA):
                    rows = slice((h % 2) * HD, (h % 2 + 1) * HD)
                    ins = nc.tensor.matmul(banks[:, 4 + h % 2, (h // 2) * 256 + lo:(h // 2) * 256 + 256],
                                           qT[rows, 2 * g + h // 2, blk * P:(blk + 1) * P], k_twice[rows, g, keys],
                                           start=True, stop=True)
                ins.then_inc(scores, 1)

            def turn_probs(s, r):
                parts = 1 if s % (TOK - 1) == 0 else 2
                if r == 0:
                    pe.wait_ge(exps, (GQA + 1) * (s + 1))
                if s == 0 and r == 0:
                    pe.wait_ge(state_copied, 2)
                else:
                    pe.wait_ge(probs_copied, 2 * s + r)
                for hh in range(2):
                    for half in range(parts):
                        at = (2 - parts + half) * WINDOW
                        i = hh * parts + half
                        ins = nc.tensor.transpose(banks[:, 6, i * P:(i + 1) * P], probs[:, s % 2, 2 * r + hh, at:at + P], ident[:])
                ins.then_inc(probs_turned, 1)

            def mix(s):
                g, blk = divmod(s, TOK - 1)
                parts = 1 if blk == 0 else 2
                pe.wait_ge(probs_copied, 2 * s + 2)
                if s > 0:
                    pe.wait_ge(rows_read, s)
                for h in range(GQA):
                    for half in range(parts):
                        i = (h % 2) * parts + half
                        ins = nc.tensor.matmul(banks[:, 7, h * HD:(h + 1) * HD], probs_T[:, h // 2, i * P:(i + 1) * P],
                                               v_tok[:, blk - parts + 1 + half, g * HD:(g + 1) * HD],
                                               start=half == 0, stop=half == parts - 1)
                ins.then_inc(mixed, 1)

            def turn_rows(s):
                pe.wait_ge(mixed_read, s + 1)
                for a in range(2):
                    ins = nc.tensor.transpose(banks[:, 7, 256 + a * P:256 + (a + 1) * P], attn_tok[:, s % 2, a * P:(a + 1) * P], ident[:])
                ins.then_inc(rows_turned, 1)

            def decode_scores():
                pe.wait_ge(q_ready, 2 + 4 * PAIRS)
                pe.wait_ge(scores_read, GQA * steps)
                for b in range(DEC_B):
                    rows = slice(32 * (b % 4), 32 * (b % 4) + 32)
                    for pair in range(PAIRS):
                        out = banks[rows, 4 + b // 4, pair * NKEY:(pair + 1) * NKEY]
                        i = b * PAIRS + pair
                        nc.tensor.matmul(out[:, 0:WINDOW], q_blocks[:, i, :], old_kT[:, i, :], start=True, stop=True)
                        ins = nc.tensor.matmul(out[:, WINDOW:NKEY], q_blocks[:, i, :], k_new[:, pair, :], start=True, stop=True)
                ins.then_inc(dec_scores, 1)

            def turn_decode_probs():
                pe.wait_ge(dec_norm, 1)
                pe.wait_ge(probs_copied, 2 * steps)
                pe.wait_ge(rows_read, steps)
                for ck in range(4):
                    nc.tensor.transpose(banks[:, 6, ck * P:(ck + 1) * P], dec_probs[:, ck, 0:WINDOW], ident[:])
                    ins = nc.tensor.transpose(banks[0:ND, 7, ck * P:(ck + 1) * P], dec_probs[:, ck, WINDOW:NKEY], ident[:])
                ins.then_inc(dec_turned, 1)

            def decode_mix():
                pe.wait_ge(dec_copied, 2)
                pe.wait_ge(cache_landed[1], 16)
                for b in range(DEC_B):
                    for pair in range(PAIRS):
                        ck = (b // 4) * PAIRS + pair
                        out = banks[:, 4, (b * PAIRS + pair) * 32:(b * PAIRS + pair + 1) * 32]
                        rows = slice(32 * (b % 4), 32 * (b % 4) + 32)
                        nc.tensor.matmul(out, old_v[:, b, pair * P:(pair + 1) * P], dec_PT[:, ck, rows], start=True, stop=False)
                        ins = nc.tensor.matmul(out, kv_dec[:, 1, pair * P:(pair + 1) * P], dec_PT_new[:, ck, rows], start=False, stop=True)
                ins.then_inc(dec_mixed, 1)

            def turn_new_rows(p):
                pe.wait_ge(tile_read, 2 * (U_PAIR0 + p) + 2)
                if p == 0:
                    pe.wait_ge(dec_shift, 1)
                else:
                    pe.wait_ge(u_copied, 2 * p)
                for i in range(2):
                    e = 2 * pool_order[p] + i
                    nc.tensor.transpose(banks[0:STATE, 5, i * P:(i + 1) * P], uT[:, e, PAD + SEQ - STATE:PAD + SEQ], ident[:])
                    ins = nc.tensor.transpose(banks[0:ND, 5, (2 + i) * P:(3 + i) * P],
                                              u_new[:, p % 2, i, :], ident[:])
                ins.then_inc(u_turned, 1)

            def mid(j):
                if 0 <= j - ROWS_AT < steps:
                    turn_rows(j - ROWS_AT)
                if 0 <= j - (TURN_AT + 1) < steps:
                    turn_probs(j - (TURN_AT + 1), 1)
                if 0 <= j - SCORE_AT < steps:
                    score(j - SCORE_AT)
                if j == DEC_SCORE_AT:
                    decode_scores()
                if j == DEC_TURN_AT:
                    turn_decode_probs()
                if j == DEC_MIX_AT:
                    decode_mix()
                for p, at in enumerate(U_TURN_AT):
                    if j == at:
                        turn_new_rows(p)

            def after(j):
                if j == 2 * K_UNITS:
                    turn_new_keys()
                if j == 2 * K_UNITS + 1:
                    pe.wait_ge(kv_copied, 3)
                    pe.wait_ge(cache_landed[0], 16)
                    turn_old_keys(0)
                    turn_old_keys(1)
                if j == 2 * K_UNITS + 2:
                    turn_old_keys(2)
                    turn_old_keys(3)
                if j == 2 * K_UNITS + 3:
                    turn_state()
                if 0 <= j - MIX_AT < steps:
                    mix(j - MIX_AT)
                if 0 <= j - TURN_AT < steps:
                    turn_probs(j - TURN_AT, 0)

            for j in range(IN_UNITS):
                pair, q = divmod(j, K_UNITS)
                pe.wait_ge(lo_split, j + 1)
                for nt in range(2):
                    if q == 0 and pair >= Q_PAIR0:
                        pe.wait_ge(tile_read, 2 * pair - 1 + nt)
                    for kk in range(UNIT_KT):
                        kt = q * UNIT_KT + kk
                        ins = product(slot((pair * 2 if pair < Q_PAIR0 else 0) + nt), j % SPLIT_SLOTS, kk, nt, acts_hi[:, kt, :],
                                      acts_lo[:, kt, :], kt == 0, kt == KT - 1)
                    if nt == 0:
                        if q == K_UNITS - 1:
                            ins.then_inc(first_done, 1)
                        mid(j)
                ins.then_inc(unit_used, 1)
                after(j)
            turn_new_rows(len(pool_order) - 1)

            for p, g in enumerate(pool_order):
                u = U_POOL + p // 2
                if p % 2 == 0:
                    pe.wait_ge(lo_split, u + 1)
                pe.wait_ge(z_lo, 2 * p + 2)
                if p == 1:
                    pe.wait_ge(u_copied, 2 * len(pool_order))
                    pe.wait_ge(dec_hi, 2 * GQA)
                for nt in range(2):
                    pe.wait_ge(tile_read, 2 * (P_POOL + p) - (1 if p == 0 else 3) + nt)
                    for kk in range(2):
                        e = QT + 2 * g + kk
                        ins = product(slot((p % 2) * 2 + nt), u % SPLIT_SLOTS, (g % 2) * 2 + kk, nt, acts_hi[:, e, :],
                                      acts_lo[:, e, :], kk == 0, kk == 1)
                    if nt == 0:
                        ins.then_inc(first_done, 1)
                ins.then_inc(even_group_done if p % 2 == 0 else unit_used, 1)

            def mixer_rows_ready(q):
                if q < 2:
                    pe.wait_ge(attn_lo, q + 1)
                else:
                    pe.wait_ge(tile_read, 2 * P_OUT)

            with pe.Fori(0, OUT_PAIRS // 2) as i:
                for b in range(2):
                    pair_tiles(U_OUT + b * K_UNITS, i * 2, P_OUT + b, i * 2, K_UNITS, mixer_rows_ready)

            pe.wait_ge(tile_read, 2 * P_FFN)
            turn_sums(1)
            spread_scales(1)
            for c in range(TOK):
                pe.wait_ge(x2_landed[c], 16)
            for kt in range(KT):
                if kt == 3:
                    pe.wait_ge(scale_ready, 2)
                if kt >= 4:
                    pe.wait_ge(x1_ready, kt - 3)
                turn_x(x_tok2, kt, kt % 4)
            pe.wait_ge(x1_ready, KT)
            turn_sums(2)
            spread_scales(2)
            pe.wait_ge(h_lo, 2 * KT)
            pe.wait_ge(scale_ready, 3)

            def chunk(c):
                v = c * (CHUNK_UNITS // 4)
                for b in range(UP_PAIRS):
                    pair_tiles(U_FFN + b * K_UNITS, v, P_FFN + b, c * CHUNK_PAIRS, K_UNITS)
                for n in range(OUT_PAIRS):
                    u = U_FFN + UP_PAIRS * K_UNITS + n
                    pair = P_FFN + UP_PAIRS + n
                    pe.wait_ge(lo_split, num(u + 1, v, 4))
                    for kk in range(UNIT_KT):
                        if n == 0:
                            pe.wait_ge(mlp_lo_ready, num(kk + 1, c, 2 * UP_PAIRS))
                        for nt in range(2):
                            if kk == 0:
                                pe.wait_ge(tile_read, num(2 * pair - 3 + nt, c, CHUNK_TILES))
                            ins = product(slot((pair % 2) * 2 + nt), u % SPLIT_SLOTS, kk, nt, mlp_hi[:, kk, :],
                                          mlp_lo[:, kk, :], kk == 0, kk == UNIT_KT - 1)
                            if kk == UNIT_KT - 1 and nt == 0:
                                ins.then_inc(first_done, 1)
                    ins.then_inc(unit_used, 1)

            with pe.Fori(0, CHUNKS) as c:
                chunk(c)

            pe.wait_ge(tile_read, 2 * (P_FFN + CHUNKS * CHUNK_PAIRS))
            turn_sums(3)
            spread_scales(3)
            pe.wait_ge(scale_ready, 4)
            for kg in range(KT // 4):
                pe.wait_ge(y_ready, 4 * kg + 4)
                for c in range(TOK):
                    o = kg * TOK + c
                    r = tok_rows[c]
                    if o >= 8:
                        pe.wait_ge(y_copied[o % 2], (o - 8) // 2 + 1)
                    for a in range(4):
                        ins = nc.tensor.transpose(banks[0:r, o % 8, a * P:(a + 1) * P], x1T[:, 4 * kg + a, c * P:c * P + r], ident[:])
                    ins.then_inc(y_turned, 1)


_INS = ['x_prompt', 'x_sample', 'cache_k', 'cache_v', 'state_pool', 'w_in', 'w_out', 'w_pool', 'pool_scale', 'attn_sinks',
        'g_pre_mix', 'g_post_mix', 'g_pre_ffn', 'g_post_ffn', 'w_up', 'w_down']


def kernel(**inputs):
    import numpy as np
    import concourse.bacc as bacc
    from concourse.bass_utils import run_bass_kernel_spmd

    nc = bacc.Bacc("TRN2", target_bir_lowering=False, num_devices=1)
    arrays, args = {}, []
    for name in _INS:
        a = np.ascontiguousarray(inputs[name])
        arrays[f"in_{name}"] = a
        args.append(nc.dram_tensor(f"in_{name}", a.shape, mybir.dt.from_np(a.dtype), kind="ExternalInput").ap())
    depth, dec_b, window, kv_heads, hd = inputs['cache_k'].shape
    _, _, state, pool_w = inputs['state_pool'].shape
    prompt = (depth, 1, window, kv_heads, hd)
    shapes = [inputs['x_prompt'].shape, inputs['x_sample'].shape, prompt, prompt, (depth, 1, state, pool_w),
              inputs['cache_k'].shape, inputs['cache_v'].shape, inputs['state_pool'].shape]
    for i, shape in enumerate(shapes):
        args.append(nc.dram_tensor(f"out_{i}", tuple(shape), F32, kind="ExternalOutput").ap())
    hybrid_decoder(nc, *args)
    r = run_bass_kernel_spmd(nc, [arrays], core_ids=[0])
    return tuple(r.results[0][f"out_{i}"] for i in range(len(shapes)))
```

```python
from contextlib import ExitStack

import concourse.bass as bass
from concourse import mybir

F32 = mybir.dt.float32
F32R = mybir.dt.float32r
I32 = mybir.dt.int32
ALU = mybir.AluOpType
ACT = mybir.ActivationFunctionType
AX = mybir.AxisListType

P = 128
EPS = 1e-6
MASKED = -1e38
RAW_SLOTS = 4
SPLIT_SLOTS = 2
UNIT_KT = 4
UNIT_N = 256
POOL_WINDOWS = (2, 4, 8, 16)


def hybrid_decoder(nc, x_prompt, x_sample, cache_k, cache_v, state_pool, w_in, w_out, w_pool, pool_scale,
                   attn_sinks, g_pre_mix, g_post_mix, g_pre_ffn, g_post_ffn, w_up, w_down,
                   y_prompt, y_sample, k_prompt, v_prompt, pool_prompt, k_sample, v_sample, pool_sample):
    _, SEQ, D = x_prompt.shape
    DEC_B, DEC_T, _ = x_sample.shape
    _, _, WINDOW, KV_HEADS, HD = cache_k.shape
    STATE = state_pool.shape[2]
    HEADS = attn_sinks.shape[1]
    GQA = HEADS // KV_HEADS
    F = w_up.shape[2]
    ND = DEC_B * DEC_T
    T = SEQ + ND
    H = T // 2
    KT = D // P
    TOK = SEQ // P + 1
    QW = HEADS * HD
    KVW = KV_HEADS * HD
    PW = w_pool.shape[1] * w_pool.shape[2]
    PAIRS = KV_HEADS // 2
    QT = QW // P
    UT = PW // P
    NKEY = WINDOW + ND
    LAST = STATE + DEC_T
    PAD = 16
    ROW = PAD + SEQ + DEC_B * LAST
    assert D == w_out.shape[1] and WINDOW == P and HD * 2 == P and T % 2 == 0 and QT + UT == KT
    assert QW // UNIT_N == KV_HEADS and KVW == UNIT_N and w_pool.shape[2] == UNIT_N and max(POOL_WINDOWS) <= PAD
    assert tuple(w_in.shape[1:]) == (D, QW + 2 * KVW + PW) and PAIRS == 2 and GQA == 4 and TOK == 5

    IN_PAIRS = w_in.shape[2] // UNIT_N
    Q_PAIR0, U_PAIR0 = 2, 2 + QW // UNIT_N
    K_UNITS = KT // UNIT_KT
    IN_UNITS = IN_PAIRS * K_UNITS
    POOL_UNITS = PW // (UNIT_KT * P)
    POOL_PAIRS = len(POOL_WINDOWS)
    OUT_PAIRS = D // UNIT_N
    CHUNK = UNIT_KT * P
    CHUNKS = F // CHUNK
    UP_PAIRS = CHUNK // UNIT_N
    CHUNK_UNITS = UP_PAIRS * K_UNITS + OUT_PAIRS
    CHUNK_PAIRS = UP_PAIRS + OUT_PAIRS
    CHUNK_TILES = 2 * CHUNK_PAIRS
    U_POOL = IN_UNITS
    U_OUT = U_POOL + POOL_UNITS
    U_FFN = U_OUT + OUT_PAIRS * K_UNITS
    P_POOL = IN_PAIRS
    P_OUT = P_POOL + POOL_PAIRS
    P_FFN = P_OUT + OUT_PAIRS

    tok_rows = [min(P, T - c * P) for c in range(TOK)]

    def units_of(w):
        return w.rearrange("(u k p) n -> u p k n", k=UNIT_KT, p=P)

    w_in_v, w_out_v, w_up_v, w_down_v = units_of(w_in[0]), units_of(w_out[0]), units_of(w_up[0]), units_of(w_down[0])
    w_pool_v = units_of(w_pool[0].rearrange("g c d -> (g c) d"))

    with ExitStack() as ctx:
        def sb(name, shape, dt=F32, scope=ctx):
            return scope.enter_context(nc.sbuf_tensor(name, shape, dt))

        def sem(name):
            return ctx.enter_context(nc.semaphore(name))

        acts_hi = sb("acts_hi", [P, KT, T], F32R)
        acts_lo = sb("acts_lo", [P, KT, T], F32R)
        w_raw = sb("w_raw", [P, RAW_SLOTS, UNIT_KT * UNIT_N])
        w_hi = sb("w_hi", [P, SPLIT_SLOTS, UNIT_KT * UNIT_N], F32R)
        w_lo = sb("w_lo", [P, SPLIT_SLOTS, UNIT_KT * UNIT_N], F32R)
        gemm_scale = sb("gemm_scale", [P, T])
        norm_scale = sb("norm_scale", [P, T])
        sq_sum = sb("sq_sum", [P, T])
        sq_tmp = sb("sq_tmp", [P, 2 * T])
        vecs = sb("vecs", [P, 4 * KT + UT])
        ident = sb("ident", [P, P])
        ones = sb("ones", [P, P])
        sink_all = sb("sink_all", [P, HEADS])
        neg_sink = sb("neg_sink", [P, HEADS])
        dec_consts = sb("dec_consts", [P, 2 * PAIRS])
        neg_dec_sink = sb("neg_dec_sink", [P, 2, PAIRS])
        dec_sink = sb("dec_sink", [P, 2, PAIRS])
        dec_slope = dec_consts[:, PAIRS:2 * PAIRS]
        row_i = sb("row_i", [P, 3], I32)
        row_t = sb("row_t", [P, 2])
        ss = sb("ss", [P, TOK])
        ss_half = sb("ss_half", [P, 2, TOK])
        var = sb("var", [P, TOK])
        inv = sb("inv", [P, TOK])
        root = sb("root", [P, TOK])
        newton = sb("newton", [P, TOK])
        rstd = sb("rstd", [P, TOK])
        g_pre, g_post = vecs[:, 0:KT], vecs[:, KT:2 * KT]
        g_ffn, g_last = vecs[:, 2 * KT:3 * KT], vecs[:, 3 * KT:4 * KT]
        p_scale = vecs[:, 4 * KT:4 * KT + UT]

        banks = ctx.enter_context(nc.psum_tensor("banks", [P, 8, 512], F32))

        def slot(s):
            return banks[:, 2 * s:2 * s + 2, 0:H]

        def flat(b, n):
            return banks[:, b:b + (n + 511) // 512, :].rearrange("p b n -> p (b n)")[:, 0:n]

        mixer = ExitStack()
        qT = sb("qT", [P, QT, T], F32, mixer)
        k_twice = sb("k_twice", [P, KV_HEADS, T], F32, mixer)
        uT = sb("uT", [P, UT, ROW], F32, mixer)
        start = ExitStack()
        x_tok = sb("x_tok", [P, TOK, D], F32, start)
        pre_rows = sb("pre_rows", [KT, P], F32, start)
        start.close()
        run_a = sb("run_a", [P, 2 * ROW], F32, mixer)
        old_k = sb("old_k", [P, DEC_B, KVW], F32, mixer)
        probs = sb("probs", [P, 2, GQA, 2 * WINDOW], F32, mixer)
        probs_T = sb("probs_T", [P, 2, 4 * P], F32, mixer)
        v_tok = sb("v_tok", [P, TOK - 1, KVW], F32, mixer)
        attn_tok = sb("attn_tok", [P, 2, GQA * HD], F32, mixer)
        kv_dec = sb("kv_dec", [ND, 2, KVW], F32, mixer)
        k_tok = sb("k_tok", [P, KVW], F32, mixer)
        k_new = sb("k_new", [P, PAIRS, ND], F32, mixer)
        q_blocks = sb("q_blocks", [P, DEC_B * PAIRS, 2 * GQA * DEC_T], F32, mixer)
        u_new = sb("u_new", [P, 2, 2, ND], F32, mixer)
        bias = sb("bias", [P, 2 * WINDOW], F32, mixer)
        dec_bias = sb("dec_bias", [P, 2, NKEY], F32, mixer)
        dec_pen = sb("dec_pen", [P, 2, NKEY], F32, mixer)
        edge = sb("edge", [P, len(POOL_WINDOWS), PAD], F32, mixer)
        stats = sb("stats", [P, 4, 7, GQA], F32, mixer)
        dec_stats = sb("dec_stats", [P, 7, 4], F32, mixer)
        vec_rows = norm_scale[0:3 * KT + UT, 0:P]
        head_rows = norm_scale[0:2 * GQA, P:2 * P]
        slope_row = norm_scale[0:1, 2 * P:3 * P]
        sink_row = norm_scale[0:1, 3 * P:3 * P + HEADS]
        sink_hh = norm_scale[0:2 * GQA, 3 * P + HEADS:3 * P + HEADS + PAIRS]
        slope_pair = norm_scale[0:1, 3 * P + HEADS + PAIRS:3 * P + HEADS + 2 * PAIRS]
        vT = run_a[:, 0:PAIRS * T].rearrange("p (e t) -> p e t", e=PAIRS)
        old_k_flat = old_k[:].rearrange("p b n -> p (b n)")
        old_kT = old_k_flat.rearrange("p (i w) -> p i w", w=P)
        run_bufs = [run_a[:].rearrange("p (e n) -> p e n", e=2), old_k_flat[:, 0:2 * ROW].rearrange("p (e n) -> p e n", e=2)]
        probs_flat = probs[:].rearrange("p a h k -> p (a h k)")
        state_tok = probs_flat[0:DEC_B * STATE, 0:PW]
        old_v = probs_flat.rearrange("p (b n) -> p b n", b=DEC_B)
        u_tok = v_tok[:].rearrange("p c n -> p (c n)")
        dec_PT = probs_T[:, 0, :].rearrange("p (c r) -> p c r", c=4)
        dec_PT_new = probs_T[0:ND, 1, :].rearrange("p (c r) -> p c r", c=4)
        dec_probs = sq_tmp[:, 0:4 * NKEY].rearrange("p (c k) -> p c k", c=4)
        mixer.close()
        x1T = sb("x1T", [P, KT, T])
        relu_buf = sb("relu_buf", [P, T])
        again = ExitStack()
        x_tok2 = sb("x_tok2", [P, TOK, D], F32, again)
        again.close()
        y_sum = sb("y_sum", [P, KT, T])
        mlp_hi = sb("mlp_hi", [P, UNIT_KT, T], F32R)
        mlp_lo = sb("mlp_lo", [P, UNIT_KT, T], F32R)

        vec_landed = [sem(f"vec_landed{i}") for i in range(7)]
        x_landed = [[sem(f"x_landed{i}_{c}") for c in range(TOK)] for i in range(2)]
        x2_landed = [sem(f"x2_landed{i}") for i in range(TOK)]
        w_landed = [sem(f"w_landed{i}") for i in range(RAW_SLOTS)]
        state_landed = sem("state_landed")
        pads_clear = sem("pads_clear")
        cache_landed = [sem(f"cache_landed{i}") for i in range(2)]
        hi_split = sem("hi_split")
        lo_split = sem("lo_split")
        unit_used = sem("unit_used")
        first_done = sem("first_done")
        even_group_done = sem("even_group_done")
        tile_read = sem("tile_read")
        consts = sem("consts")
        vecs_turned = sem("vecs_turned")
        vecs_ready = sem("vecs_ready")
        pre_turned = sem("pre_turned")
        pre_ready = sem("pre_ready")
        small = sem("small")
        squares = sem("squares")
        x_turned = sem("x_turned")
        h_hi = sem("h_hi")
        h_lo = sem("h_lo")
        inv_ready = sem("inv_ready")
        root_ready = sem("root_ready")
        rstd_ready = sem("rstd_ready")
        spread = sem("spread")
        scale_ready = sem("scale_ready")
        sums_turned = sem("sums_turned")
        sq_ready = sem("sq_ready")
        sq_added = sem("sq_added")
        sum_clear = sem("sum_clear")
        state_turned = sem("state_turned")
        u_turned = sem("u_turned")
        u_copied = sem("u_copied")
        state_copied = sem("state_copied")
        run_ready = sem("run_ready")
        z_ready = sem("z_ready")
        z_hi = sem("z_hi")
        z_lo = sem("z_lo")
        mix_hi = sem("mix_hi")
        edge_ready = sem("edge_ready")
        bias_ready = sem("bias_ready")
        kv_turned = sem("kv_turned")
        kv_copied = sem("kv_copied")
        scores = sem("scores")
        scores_read = sem("scores_read")
        shift_ready = sem("shift_ready")
        exps = sem("exps")
        probs_turned = sem("probs_turned")
        probs_copied = sem("probs_copied")
        mixed = sem("mixed")
        mixed_read = sem("mixed_read")
        rows_turned = sem("rows_turned")
        rows_read = sem("rows_read")
        attn_hi = sem("attn_hi")
        attn_lo = sem("attn_lo")
        old_k_turned = sem("old_k_turned")
        old_k_act = sem("old_k_act")
        old_k_dve = sem("old_k_dve")
        q_zero = sem("q_zero")
        q_ready = sem("q_ready")
        dec_scores = sem("dec_scores")
        dec_shift = sem("dec_shift")
        dec_exps = sem("dec_exps")
        dec_norm = sem("dec_norm")
        dec_turned = sem("dec_turned")
        dec_copied = sem("dec_copied")
        dec_mixed = sem("dec_mixed")
        dec_hi = sem("dec_hi")
        x1_ready = sem("x1_ready")
        normed = sem("normed")
        y_clear = sem("y_clear")
        relu_sq = sem("relu_sq")
        mlp_hi_ready = sem("mlp_hi_ready")
        mlp_lo_ready = sem("mlp_lo_ready")
        y_ready = sem("y_ready")
        y_turned = sem("y_turned")
        y_copied = [sem("y_copied_act"), sem("y_copied_dve")]
        y_stored = [sem(f"y_stored{i}") for i in range(8)]
        kept = sem("kept")
        u_stored = sem("u_stored")
        stored = sem("stored")

        N_STORED = 4

        def num(k, v, per=1):
            return k + v * per if not isinstance(v, int) or v else k

        def dec_out(half, h):
            src = banks[half * HD:(half + 1) * HD, 4, :].rearrange("d (b pair c) -> d pair b c", b=DEC_B, pair=PAIRS)[
                :, :, :, half * GQA * DEC_T + h * DEC_T:half * GQA * DEC_T + (h + 1) * DEC_T]
            r = slice((h % 2) * HD, (h % 2 + 1) * HD)
            e = half * 2 + h // 2
            return src, qT[r, 0:QT, SEQ:T].rearrange("d (pair e) (b t) -> d e pair b t", pair=PAIRS, t=DEC_T)[:, e]

        def x_slot(kt):
            return kt if kt < 2 else 2 + kt % 2

        START_SPLITS = {0: 0, 5: 1, 7: 2, 11: 3}

        def scale_chunk(c):
            return banks[:, c, H:H + P] if c < TOK - 1 else banks[:, 0, H + P:H + P + ND]
        SUMS_AT = H + P + ND

        OWN_NORMED = (0, 3, 7, 11, 14)

        def copier(o):
            late = (KT // 4 - 1) * TOK
            if o < late:
                return 0, o + 1
            return (1, (o - late) // 2 + 1) if (o - late) % 2 == 0 else (0, late + (o - late + 1) // 2)

        pool_order = [3, 2, 1, 0]

        def decode_part(ap):
            return ap[:, :, PAD + SEQ:ROW].rearrange("p e (b s) -> p e b s", s=LAST)

        def z_parts(g):
            e = slice(2 * g, 2 * g + 2)
            out = slice(QT + 2 * g, QT + 2 * g + 2)

            def parts(t):
                return t[:, out, 0:SEQ], t[:, out, SEQ:T].rearrange("p e (b t) -> p e b t", t=DEC_T)
            return (uT[:, e, PAD:PAD + SEQ], decode_part(uT[:, e, :])[:, :, :, STATE:LAST]), parts(acts_hi), parts(acts_lo)

        steps = (TOK - 1) * KV_HEADS

        SCORE_AT = (Q_PAIR0 + 1) * K_UNITS
        TURN_AT = SCORE_AT + 1
        MIX_AT = TURN_AT + 1
        ROWS_AT = MIX_AT + 1
        DEC_SCORE_AT = ROWS_AT + steps - 1
        DEC_TURN_AT = DEC_SCORE_AT + 2
        DEC_MIX_AT = DEC_TURN_AT + 1
        U_TURN_AT = [DEC_SCORE_AT + 1, DEC_SCORE_AT + 3, IN_UNITS - 3]
        Z_AT = [DEC_TURN_AT + 1, IN_UNITS - 5, IN_UNITS - 2]

        block = ctx.enter_context(nc.Block())

        @block.sync
        def _(sp):
            def load(k, v, src):
                if k >= RAW_SLOTS or not isinstance(v, int):
                    sp.wait_ge(lo_split, num(k - RAW_SLOTS + 1, v, 4))
                s = k % RAW_SLOTS
                sp.dma_start(w_raw[:, s, :].rearrange("p (k n) -> p k n", k=UNIT_KT), src).then_inc(w_landed[s], 16)

            def load_x(half):
                cols = slice(half * (D // 2), (half + 1) * (D // 2))
                for c in range(TOK - 1):
                    sp.dma_start(x_tok[:, c, cols], x_prompt[0, c * P:(c + 1) * P, cols]).then_inc(x_landed[half][c], 16)
                sp.dma_start(x_tok[0:ND, TOK - 1, cols], x_sample.rearrange("b t d -> (b t) d")[:, cols]
                             ).then_inc(x_landed[half][TOK - 1], 16)

            sp.dma_start(pre_rows[:], g_pre_mix[0].rearrange("(k p) -> k p", p=P)).then_inc(vec_landed[0], 16)
            load_x(0)
            columns = [QW, QW + KVW] + [g * UNIT_N for g in range(KV_HEADS)] + [QW + 2 * KVW + g * UNIT_N for g in pool_order]
            for pair, n0 in enumerate(columns):
                for kq in range(K_UNITS):
                    load(pair * K_UNITS + kq, 0, w_in_v[kq, :, :, n0:n0 + UNIT_N])
                    if pair + kq == 0:
                        load_x(1)
            for j in range(POOL_UNITS):
                load(U_POOL + j, 0, w_pool_v[pool_order[2 * j] // 2])
            with sp.Fori(0, OUT_PAIRS) as pair:
                for kq in range(K_UNITS):
                    load(U_OUT + kq, pair, w_out_v[kq, :, :, bass.ts(pair, UNIT_N)])
            with sp.Fori(0, CHUNKS) as c:
                for b in range(UP_PAIRS):
                    for kq in range(K_UNITS):
                        load(U_FFN + b * K_UNITS + kq, c * (CHUNK_UNITS // 4),
                             w_up_v[kq, :, :, bass.ds(c * CHUNK + b * UNIT_N, UNIT_N)])
                for n in range(OUT_PAIRS):
                    load(U_FFN + UP_PAIRS * K_UNITS + n, c * (CHUNK_UNITS // 4),
                         w_down_v[bass.ds(c, 1), :, :, n * UNIT_N:(n + 1) * UNIT_N].rearrange("o p k n -> (o p) k n"))

            for kg in range(KT // 4):
                for c in range(TOK):
                    o = kg * TOK + c
                    who, count = copier(o)
                    sp.wait_ge(y_copied[who], count)
                    dst = (y_prompt[0, c * P:(c + 1) * P, :] if c < TOK - 1 else y_sample.rearrange("b t d -> (b t) d"))
                    sp.dma_start(dst[:, kg * 512:(kg + 1) * 512],
                                 w_raw[0:tok_rows[c], :, :].rearrange("p s n -> p (s n)")[:, (o % 8) * 512:(o % 8 + 1) * 512]
                                 ).then_inc(y_stored[o % 8], 16)
            for i in range(8):
                sp.wait_ge(y_stored[i], 16 * len(range(i, TOK * KT // 4, 8)))
            sp.wait_ge(kept, 16 * 3)
            sp.wait_ge(u_stored, 16 * 2)
            sp.wait_ge(stored, 16 * N_STORED)

        @block.gpsimd
        def _(gp):
            nc.gpsimd.memset(ident[:], 0.0).then_inc(consts, 1)
            nc.gpsimd.memset(ones[:], 1.0).then_inc(consts, 1)
            nc.gpsimd.memset(ss_half[:], 1.0).then_inc(consts, 1)
            nc.gpsimd.memset(head_rows, 1.0).then_inc(consts, 1)
            for hh in range(2 * GQA):
                nc.gpsimd.memset(slope_row.rearrange("o (b hh t) -> o b hh t", b=4, t=DEC_T)[:, :, hh, :],
                                 2.0 ** (-8.0 * (hh + 1) / HEADS)).then_inc(consts, 1)
            for pair in range(PAIRS):
                nc.gpsimd.memset(slope_pair[:, pair:pair + 1], 2.0 ** (-8.0 * 2 * GQA * pair / HEADS)).then_inc(consts, 1)
            nc.gpsimd.iota(row_i[:, 0:1], pattern=[[0, 1]], base=0, channel_multiplier=1).then_inc(consts, 1)
            n = 5 + 2 * GQA + PAIRS
            gp.wait_ge(consts, n)
            nc.gpsimd.affine_select(out=ident[:], in_=ident[:], compare_op=ALU.not_equal, fill=1.0, base=0,
                                    pattern=[[-1, P]], channel_multiplier=1).then_inc(consts, 1)
            hr = head_rows.rearrange("h (b hh t) -> h b hh t", b=4, t=DEC_T)
            nc.gpsimd.affine_select(out=hr, in_=hr, compare_op=ALU.is_equal, fill=0.0, base=0,
                                    pattern=[[0, 4], [1, 2 * GQA], [0, DEC_T]], channel_multiplier=-1).then_inc(consts, 1)

            gp.wait_ge(x_turned, KT)
            gp.wait_ge(squares, 2 * TOK)
            nc.gpsimd.memset(uT[:, :, 0:PAD], 0.0).then_inc(pads_clear, 1)
            nc.gpsimd.memset(edge[:], 1.0).then_inc(edge_ready, 1)
            gp.wait_ge(edge_ready, 1)
            n_edge = 1
            for g, w in enumerate(POOL_WINDOWS):
                for t in range(w - 1):
                    nc.gpsimd.memset(edge[:, g, t:t + 1], float(w) / (t + 1)).then_inc(edge_ready, 1)
                    n_edge += 1

            nc.gpsimd.iota(bias[:], pattern=[[1, 2 * WINDOW]], base=-WINDOW, channel_multiplier=-1,
                           allow_small_or_imprecise_dtypes=True).then_inc(bias_ready, 1)
            gp.wait_ge(bias_ready, 1)
            nc.gpsimd.affine_select(out=bias[:], in_=bias[:], compare_op=ALU.is_ge, fill=MASKED, base=WINDOW,
                                    pattern=[[-1, 2 * WINDOW]], channel_multiplier=1).then_inc(bias_ready, 1)
            gp.wait_ge(bias_ready, 2)
            nc.gpsimd.affine_select(out=bias[:], in_=bias[:], compare_op=ALU.is_gt, fill=MASKED, base=0,
                                    pattern=[[1, 2 * WINDOW]], channel_multiplier=-1).then_inc(bias_ready, 1)
            nc.gpsimd.iota(dec_bias[:, 0, 0:WINDOW], pattern=[[1, WINDOW]], base=-WINDOW, channel_multiplier=0,
                           allow_small_or_imprecise_dtypes=True).then_inc(bias_ready, 1)
            nc.gpsimd.iota(dec_bias[:, 0, WINDOW:NKEY], pattern=[[0, DEC_B], [1, DEC_T]], base=0, channel_multiplier=0,
                           allow_small_or_imprecise_dtypes=True).then_inc(bias_ready, 1)
            nc.gpsimd.iota(dec_pen[:, 0, WINDOW:NKEY], pattern=[[1, DEC_B], [0, DEC_T]], base=0, channel_multiplier=0,
                           allow_small_or_imprecise_dtypes=True).then_inc(bias_ready, 1)
            nc.gpsimd.memset(q_blocks[:], 0.0).then_inc(q_zero, 1)

            gp.wait_ge(pads_clear, 1)
            gp.wait_ge(state_copied, 2)
            gp.wait_ge(kv_turned, 1)
            gp.wait_ge(dec_scores, 1)
            n_run = 0
            for p, g in enumerate(pool_order[:-1]):
                gp.wait_ge(tile_read, 2 * (U_PAIR0 + p) + 2)
                if p > 0:
                    gp.wait_ge(z_ready, p)
                src = uT[:, 2 * g:2 * g + 2, :]
                for level in range(g + 1):
                    half = 1 << level
                    dst = run_bufs[level % 2]
                    if level > 0:
                        gp.wait_ge(run_ready, n_run)
                    nc.gpsimd.tensor_tensor(dst[:, :, 2 * half - 1:ROW], src[:, :, 2 * half - 1:ROW],
                                            src[:, :, half - 1:ROW - half], ALU.add).then_inc(run_ready, 1)
                    n_run += 1
                    src = dst

            for r in range(2):
                gp.wait_ge(attn_hi, r + 1)
                e = slice(4 * r, 4 * r + 4)
                nc.gpsimd.tensor_tensor(acts_lo[:, e, :], qT[:, e, :], acts_hi[:, e, :].bitcast(F32),
                                        ALU.subtract).then_inc(attn_lo, 1)

            def clear_sum(n):
                if n > 0:
                    gp.wait_ge(sums_turned, n)
                nc.gpsimd.memset(sq_sum[:], 0.0).then_inc(sum_clear, 1)
                gp.wait_ge(sum_clear, n + 1)

            def add(group, kt):
                count = group * (KT - 1) + kt
                gp.wait_ge(sq_ready, group * KT + kt + 1)
                if count:
                    gp.wait_ge(sq_added, count)
                par = kt % 2
                nc.gpsimd.tensor_tensor(sq_sum[:], sq_sum[:], sq_tmp[:, par * T:(par + 1) * T], ALU.add).then_inc(sq_added, 1)

            clear_sum(0)
            for kt in range(KT - 1):
                add(0, kt)
            clear_sum(1)
            def normalise_tile(tile):
                nc.gpsimd.tensor_tensor(tile, tile, norm_scale[:], ALU.mult).then_inc(normed, 1)

            gp.wait_ge(scale_ready, 2)
            for kt in (1, 3):
                normalise_tile(x1T[:, kt, :])
            for kt in range(KT):
                if kt < KT - 1:
                    add(1, kt)
                if kt % 2 == 1 and kt + 4 < KT:
                    normalise_tile(x1T[:, kt + 4, :])
            gp.wait_ge(x_turned, 2 * KT)
            nc.gpsimd.memset(y_sum[:], 0.0).then_inc(y_clear, 1)
            clear_sum(2)
            for kt in range(KT - 1):
                add(2, kt)
            gp.wait_ge(scale_ready, 4)
            for kt in range(KT):
                if kt not in OWN_NORMED:
                    normalise_tile(y_sum[:, kt, :])

        @block.scalar
        def _(act):
            def split(k, v=0):
                act.wait_ge(w_landed[k % RAW_SLOTS], num(16 * (k // RAW_SLOTS + 1), v, 16))
                if k >= SPLIT_SLOTS or not isinstance(v, int):
                    act.wait_ge(unit_used, num(k - SPLIT_SLOTS + 1, v, 4))
                nc.scalar.activation(w_hi[:, k % SPLIT_SLOTS, :], w_raw[:, k % RAW_SLOTS, :], ACT.Copy).then_inc(hi_split, 1)

            def take_root(n):
                act.wait_ge(inv_ready, n + 1)
                nc.scalar.activation(root[:], inv[:], ACT.Sqrt).then_inc(root_ready, 1)

            act.wait_ge(pre_turned, 1)
            nc.scalar.activation(g_pre, banks[:, 0, 0:KT], ACT.Copy).then_inc(pre_ready, 1)
            act.wait_ge(pre_ready, 1)
            act.wait_ge(consts, 3)
            for kt in range(KT):
                act.wait_ge(x_turned, kt + 1)
                nc.scalar.activation(acts_hi[:, kt, :], flat(2 * x_slot(kt), T), ACT.Copy, scale=g_pre[:, kt:kt + 1]).then_inc(h_hi, 1)
                if kt in START_SPLITS:
                    split(START_SPLITS[kt])
                n = kt - (KT - 2 * TOK)
                if n >= 0:
                    half, c = divmod(n, TOK)
                    r = tok_rows[c]
                    act.wait_ge(x_landed[half][c], 16)
                    if n > 0:
                        act.wait_ge(squares, n)
                    nc.scalar.activation(uT[0:r].rearrange("p e n -> p (e n)")[:, 0:D // 2],
                                         x_tok[0:r, c, half * (D // 2):(half + 1) * (D // 2)], ACT.Square,
                                         accum_out=ss_half[0:r, half, c:c + 1]).then_inc(squares, 1)
            take_root(0)
            split(4)
            act.wait_ge(x_turned, KT)
            act.wait_ge(squares, 2 * TOK)
            act.dma_start(state_tok, state_pool[0].rearrange("b s c -> (b s) c")).then_inc(state_landed, 16)
            rows = [(g_post_mix, 0, KT), (g_pre_ffn, KT, KT), (g_post_ffn, 2 * KT, KT), (pool_scale, 3 * KT, UT)]
            for i, (vec, at, n) in enumerate(rows):
                act.dma_start(vec_rows[at:at + n, :], vec[0].rearrange("(k p) -> k p", p=P)).then_inc(vec_landed[i + 1], 16)
            act.wait_ge(consts, 4 + 2 * GQA + PAIRS)
            act.dma_start(sink_row, attn_sinks).then_inc(vec_landed[5], 16)
            with nc.allow_non_contiguous_dma("16 sinks, by head within a pair of groups"):
                act.dma_start(sink_hh, attn_sinks[0].rearrange("(pair hh) -> hh pair", pair=PAIRS)).then_inc(vec_landed[6], 16)
            act.dma_start(k_sample[0, :, 0:WINDOW - DEC_T].rearrange("b w h d -> b (w h d)"),
                          cache_k[0, :, DEC_T:WINDOW].rearrange("b w h d -> b (w h d)")).then_inc(kept, 16)
            act.dma_start(v_sample[0, :, 0:WINDOW - DEC_T].rearrange("b w h d -> b (w h d)"),
                          cache_v[0, :, DEC_T:WINDOW].rearrange("b w h d -> b (w h d)")).then_inc(kept, 16)
            act.dma_start(pool_sample[0, :, 0:STATE - DEC_T].rearrange("b s c -> b (s c)"),
                          state_pool[0, :, DEC_T:STATE].rearrange("b s c -> b (s c)")).then_inc(kept, 16)
            act.dma_start(old_k[:], cache_k[0].rearrange("b w h d -> w b (h d)")).then_inc(cache_landed[0], 16)

            def exponentials(s):
                blk = s % (TOK - 1)
                lo = WINDOW if blk == 0 else 0
                act.wait_ge(shift_ready, s + 1)
                if s >= 4:
                    act.wait_ge(mixed_read, s - 3)
                for h in range(GQA):
                    nc.scalar.activation(probs[:, s % 2, h, lo:], probs[:, s % 2, h, lo:], ACT.Exp,
                                         bias=stats[:, s % 4, 0, h:h + 1], accum_out=stats[:, s % 4, 2, h:h + 1]).then_inc(exps, 1)
                nc.scalar.activation(stats[:, s % 4, 3, :], stats[:, s % 4, 1, :], ACT.Exp).then_inc(exps, 1)

            def copy_turned(s, r):
                n = 2 * P if s % (TOK - 1) == 0 else 4 * P
                act.wait_ge(probs_turned, 2 * s + r + 1)
                if s > 0:
                    act.wait_ge(mixed, s)
                nc.scalar.activation(probs_T[:, r, 0:n], banks[:, 6, 0:n], ACT.Copy).then_inc(probs_copied, 1)

            def new_rows(p):
                act.wait_ge(u_turned, p + 1)
                if p == 0:
                    act.wait_ge(mixed, steps)
                    act.wait_ge(stored, 16 * N_STORED)
                cols = slice(pool_order[p] * UNIT_N, (pool_order[p] + 1) * UNIT_N)
                nc.scalar.activation(u_tok[0:STATE, cols], banks[0:STATE, 5, 0:UNIT_N], ACT.Copy).then_inc(u_copied, 1)
                nc.scalar.activation(u_tok[ND:2 * ND, cols], banks[0:ND, 5, UNIT_N:2 * UNIT_N], ACT.Copy).then_inc(u_copied, 1)

            for j in range(IN_UNITS):
                if 4 < j + 2 <= U_POOL:
                    split(j + 2)
                if j == 2 * K_UNITS:
                    act.wait_ge(kv_turned, 1)
                    nc.scalar.activation(v_tok[:].rearrange("p b n -> p (b n)"), flat(4, (TOK - 1) * KVW), ACT.Copy).then_inc(kv_copied, 1)
                    act.wait_ge(kv_copied, 3)
                    act.dma_start(k_prompt[0, 0].rearrange("w h d -> w (h d)"), k_tok[:]).then_inc(stored, 16)
                    for i, dst in enumerate((k_sample, v_sample)):
                        act.dma_start(dst[0, :, WINDOW - DEC_T:WINDOW].rearrange("b t h d -> b t (h d)"), kv_dec[:, i, :]).then_inc(stored, 16)
                    act.dma_start(v_prompt[0, 0].rearrange("w h d -> w (h d)"), v_tok[:, TOK - 2, :]).then_inc(stored, 16)
                if j == 2 * K_UNITS + 1:
                    for r in range(2):
                        act.wait_ge(old_k_turned, r + 1)
                        nc.scalar.activation(old_kT[:, 4 * r:4 * r + 4, :].rearrange("p a k -> p (a k)"), banks[:, 4 + r, :],
                                             ACT.Copy).then_inc(old_k_act, 1)
                s = j - TURN_AT
                if 0 <= s < steps:
                    copy_turned(s, 0)
                if 0 <= s + 1 < steps:
                    exponentials(s + 1)
                if 0 <= s < steps:
                    copy_turned(s, 1)
                if s == steps:
                    act.wait_ge(probs_turned, 2 * steps)
                    act.dma_start(old_v, cache_v[0].rearrange("b w h d -> w b (h d)")).then_inc(cache_landed[1], 16)
                if j == DEC_SCORE_AT:
                    act.wait_ge(dec_shift, 1)
                    for ck in range(4):
                        nc.scalar.activation(dec_probs[:, ck, :], dec_probs[:, ck, :], ACT.Exp, bias=dec_stats[:, 0, ck:ck + 1],
                                             accum_out=dec_stats[:, 2, ck:ck + 1]).then_inc(dec_exps, 1)
                    nc.scalar.activation(dec_stats[:, 3, :], dec_stats[:, 1, :], ACT.Exp).then_inc(dec_exps, 1)
                if j == DEC_TURN_AT - 1:
                    act.wait_ge(dec_turned, 1)
                    nc.scalar.activation(dec_PT.rearrange("p a r -> p (a r)"), banks[:, 6, :], ACT.Copy).then_inc(dec_copied, 1)
                if j == DEC_MIX_AT:
                    act.wait_ge(dec_mixed, 1)
                    for half in range(2):
                        for h in range(GQA):
                            src, dst = dec_out(half, h)
                            nc.scalar.activation(dst, src, ACT.Copy).then_inc(dec_hi, 1)
                for p, at in enumerate(U_TURN_AT):
                    if j == at:
                        new_rows(p)

            def z_high(p):
                act.wait_ge(z_ready, p + 1)
                src, hi, _ = z_parts(pool_order[p])
                for part in range(2):
                    nc.scalar.activation(hi[part], src[part], ACT.Copy).then_inc(z_hi, 1)

            def mix_high(p):
                if p % 2 == 0:
                    act.wait_ge(even_group_done, p // 2 + 1)
                else:
                    act.wait_ge(unit_used, U_POOL + p // 2 + 1)
                for nt in range(2):
                    m = 2 * pool_order[p] + nt
                    out = acts_hi[:, QT + m, :].rearrange("p (h t) -> p h t", h=2)
                    nc.scalar.activation(out, slot((p % 2) * 2 + nt), ACT.Copy, scale=p_scale[:, m:m + 1]).then_inc(mix_hi, 1)

            def attn_high(r):
                act.wait_ge(rows_read, steps)
                act.wait_ge(dec_hi, 2 * GQA)
                nc.scalar.activation(acts_hi[:, 4 * r:4 * r + 4, :], qT[:, 4 * r:4 * r + 4, :], ACT.Copy).then_inc(attn_hi, 1)

            act.wait_ge(unit_used, IN_UNITS)
            z_high(0)
            new_rows(len(pool_order) - 1)
            z_high(1)
            split(U_POOL + 1)
            z_high(2)
            z_high(3)
            mix_high(0)
            attn_high(0)
            mix_high(1)
            split(U_OUT)
            attn_high(1)
            mix_high(2)
            mix_high(3)
            act.wait_ge(u_copied, 2 * len(pool_order))
            act.dma_start(pool_prompt[0, 0], u_tok[0:STATE, :]).then_inc(u_stored, 16)
            act.dma_start(pool_sample[0, :, STATE - DEC_T:STATE], u_tok[ND:2 * ND, :]).then_inc(u_stored, 16)

            def square(src, count, par):
                group = 0 if not isinstance(count, int) else count // KT
                if isinstance(count, int) and count % KT < 2:
                    if group:
                        act.wait_ge(sums_turned, group)
                else:
                    act.wait_ge(sq_added, count - 1 - group)
                nc.scalar.activation(sq_tmp[:, par * T:(par + 1) * T].rearrange("p (h t) -> p h t", h=2), src,
                                     ACT.Square).then_inc(sq_ready, 1)

            def out_pair(k, v, pair_k, pair_v, count):
                for kq in range(K_UNITS):
                    split(k + kq + 1, v)
                for nt in range(2):
                    if nt == 0:
                        act.wait_ge(first_done, num(pair_k + 1, pair_v))
                    else:
                        act.wait_ge(unit_used, num(k + K_UNITS, v, 4))
                    square(slot((pair_k % 2) * 2 + nt), count + nt, nt)

            out_pair(U_OUT, 0, P_OUT, 0, 0)
            act.wait_ge(attn_lo, 2)
            act.wait_ge(z_lo, 2 * len(pool_order))
            act.wait_ge(stored, 16 * N_STORED)
            act.wait_ge(u_stored, 32)
            for c in range(TOK - 1):
                act.dma_start(x_tok2[:, c, :], x_prompt[0, c * P:(c + 1) * P, :]).then_inc(x2_landed[c], 16)
            act.dma_start(x_tok2[0:ND, TOK - 1, :], x_sample.rearrange("b t d -> (b t) d")).then_inc(x2_landed[TOK - 1], 16)
            out_pair(U_OUT + K_UNITS, 0, P_OUT + 1, 0, 2)
            with act.Fori(1, OUT_PAIRS // 2) as i:
                for b in range(2):
                    out_pair(U_OUT + b * K_UNITS, i * 2, P_OUT + b, i * 2, i * 4 + 2 * b)

            take_root(1)
            for kt in range(KT):
                act.wait_ge(x1_ready, kt + 1)
                nc.scalar.activation(acts_hi[:, kt, :], x1T[:, kt, :], ACT.Copy, scale=g_ffn[:, kt:kt + 1]).then_inc(h_hi, 1)
                square(x1T[:, kt, :].rearrange("p (h t) -> p h t", h=2), KT + kt, kt % 2)
                if kt % UNIT_KT == UNIT_KT - 1:
                    split(U_FFN + kt // UNIT_KT + 1)
            split(U_FFN + 5)
            take_root(2)
            split(U_FFN + 6)

            def chunk(c, first=False, last=False):
                v = c * (CHUNK_UNITS // 4)
                for b in range(UP_PAIRS):
                    for kq in range(K_UNITS):
                        if not first or b * K_UNITS + kq + 1 > 6:
                            split(U_FFN + b * K_UNITS + kq + 1, v)
                    for nt in range(2):
                        j = 2 * b + nt
                        act.wait_ge(tile_read, num(2 * P_FFN + j + 1, c, CHUNK_TILES))
                        nc.scalar.activation(mlp_hi[:, j, :], relu_buf[:], ACT.Square).then_inc(mlp_hi_ready, 1)
                for n in range(OUT_PAIRS):
                    k = U_FFN + UP_PAIRS * K_UNITS + n + 1
                    if not last or n + 1 < OUT_PAIRS:
                        split(k, v)
                    if last:
                        for nt in range(2):
                            m = 2 * n + nt
                            act.wait_ge(tile_read, num(2 * P_FFN + 2 * UP_PAIRS + m + 1, c, CHUNK_TILES))
                            square(y_sum[:, m, :].rearrange("p (h t) -> p h t", h=2), 2 * KT + m, m % 2)

            chunk(0, first=True)
            with act.Fori(1, CHUNKS - 1) as c:
                chunk(c)
            chunk(CHUNKS - 1, last=True)
            take_root(3)
            for kg in range(KT // 4):
                for c in range(TOK):
                    o = kg * TOK + c
                    if copier(o)[0] == 0:
                        act.wait_ge(y_turned, o + 1)
                        if o >= 8:
                            act.wait_ge(y_stored[o % 8], 16 * (o // 8))
                        r = tok_rows[c]
                        nc.scalar.activation(w_raw[0:r].rearrange("p s n -> p (s n)")[:, (o % 8) * 512:(o % 8 + 1) * 512],
                                             banks[0:r, o % 8, :], ACT.Copy).then_inc(y_copied[0], 1)

        @block.vector
        def _(dve):
            chained = [0]

            def step(ins):
                ins.then_inc(small, 1)
                chained[0] += 1
                dve.wait_ge(small, chained[0])

            def split(k, v=0):
                dve.wait_ge(hi_split, num(k + 1, v, 4))
                nc.vector.tensor_tensor(w_lo[:, k % SPLIT_SLOTS, :], w_raw[:, k % RAW_SLOTS, :],
                                        w_hi[:, k % SPLIT_SLOTS, :].bitcast(F32), ALU.subtract).then_inc(lo_split, 1)

            def row_roots(n):
                step(nc.vector.tensor_scalar(var[:], ss[:], 1.0 / D, EPS, ALU.mult, ALU.add))
                nc.vector.reciprocal(inv[:], var[:]).then_inc(inv_ready, 1)
                dve.wait_ge(root_ready, n + 1)
                step(nc.vector.tensor_tensor(newton[:], root[:], root[:], ALU.mult))
                step(nc.vector.tensor_tensor(newton[:], newton[:], var[:], ALU.mult))
                step(nc.vector.tensor_scalar(newton[:], newton[:], -0.5, 1.5, ALU.mult, ALU.add))
                nc.vector.tensor_tensor(rstd[:], root[:], newton[:], ALU.mult).then_inc(rstd_ready, 1)

            def sums_by_token(n, at):
                dve.wait_ge(sums_turned, n)
                nc.vector.tensor_copy(ss[:, 0:TOK - 1], at[:, 0:TOK - 1])
                step(nc.vector.tensor_copy(ss[0:ND, TOK - 1:TOK], at[0:ND, TOK - 1:TOK]))

            def row_scales(n, target):
                sums_by_token(n, banks[:, 6, :])
                row_roots(n)
                dve.wait_ge(spread, n + 1)
                nc.vector.tensor_copy(target[:], flat(6, T)).then_inc(scale_ready, 1)

            dve.wait_ge(pre_ready, 1)
            for kt in range(KT):
                dve.wait_ge(h_hi, kt + 1)
                nc.vector.scalar_tensor_tensor(out=acts_lo[:, kt, :], in0=flat(2 * x_slot(kt), T), scalar=g_pre[:, kt:kt + 1],
                                               in1=acts_hi[:, kt, :].bitcast(F32), op0=ALU.mult, op1=ALU.subtract).then_inc(h_lo, 1)
                if kt in START_SPLITS:
                    split(START_SPLITS[kt])
            dve.wait_ge(squares, 2 * TOK)
            step(nc.vector.tensor_tensor(ss[:], ss_half[:, 0, :], ss_half[:, 1, :], ALU.add))
            row_roots(0)
            split(4)
            dve.wait_ge(spread, 1)
            nc.vector.tensor_copy(gemm_scale[:], flat(6, T)).then_inc(scale_ready, 1)

            def halves(ap):
                return ap.rearrange("p o (h t) -> p (o h) t", h=2)

            def pair_ready(nt, k, v, pair_k, pair_v):
                if nt == 0:
                    dve.wait_ge(first_done, num(pair_k + 1, pair_v))
                else:
                    dve.wait_ge(unit_used, num(k + K_UNITS, v, 4))

            scale2 = gemm_scale[:].rearrange("p (h t) -> p h t", h=2)
            dve.wait_ge(scale_ready, 1)

            def read_q(g, nt, src):
                return nc.vector.scalar_tensor_tensor(
                    out=qT[:, 2 * g + nt, :].rearrange("p (h t) -> p h t", h=2), in0=src, scalar=HD ** -0.5,
                    in1=scale2, op0=ALU.mult, op1=ALU.mult)

            def read_k(nt, src):
                for half in range(2):
                    rows = slice(half * HD, (half + 1) * HD)
                    for copy in range(2):
                        ins = nc.vector.tensor_tensor(
                            k_twice[copy * HD:(copy + 1) * HD, 2 * nt + half, :].rearrange("p (h t) -> p h t", h=2),
                            src[rows], scale2[rows], ALU.mult)
                        if half + copy < 2:
                            ins.then_inc(small, 1)
                            chained[0] += 1
                return ins

            def read_u(p, nt, src):
                u = uT[:, 2 * pool_order[p] + nt, :]
                n = SEQ - H
                nc.vector.tensor_tensor(u[:, PAD:PAD + H], src[:, 0, :], scale2[:, 0, :], ALU.mult).then_inc(small, 1)
                nc.vector.tensor_tensor(u[:, PAD + H:PAD + SEQ], src[:, 1, 0:n], scale2[:, 1, 0:n], ALU.mult).then_inc(small, 1)
                if p >= 2:
                    dve.wait_ge(u_turned, p - 1)
                nc.vector.tensor_tensor(u_new[:, p % 2, nt, :], src[:, 1, n:H], scale2[:, 1, n:H], ALU.mult).then_inc(small, 1)
                chained[0] += 3
                by_batch = "p (b t) -> p b t"
                return nc.vector.tensor_tensor(
                    u[:, PAD + SEQ:ROW].rearrange("p (b s) -> p b s", s=LAST)[:, :, STATE:LAST],
                    src[:, 1, n:H].rearrange(by_batch, t=DEC_T), scale2[:, 1, n:H].rearrange(by_batch, t=DEC_T), ALU.mult)

            def read_pair(pair):
                for nt in range(2):
                    pair_ready(nt, pair * K_UNITS, 0, pair, 0)
                    src = slot((pair * 2 if pair < Q_PAIR0 else 0) + nt)
                    if pair == 0:
                        ins = read_k(nt, src)
                    elif pair == 1:
                        ins = nc.vector.tensor_tensor(vT[:, nt, :].rearrange("p (h t) -> p h t", h=2), src, scale2, ALU.mult)
                    elif pair < U_PAIR0:
                        ins = read_q(pair - Q_PAIR0, nt, src)
                    else:
                        ins = read_u(pair - U_PAIR0, nt, src)
                    ins.then_inc(tile_read, 1)

            def vectors():
                dve.wait_ge(vecs_turned, 1)
                step(nc.vector.tensor_copy(sink_all[:], banks[:, 5, 0:HEADS]))
                step(nc.vector.tensor_scalar(neg_sink[:], sink_all[:], -1.0, None, ALU.mult))
                step(nc.vector.tensor_copy(dec_consts[:], banks[:, 5, HEADS:HEADS + 2 * PAIRS]))
                for bg in range(2):
                    step(nc.vector.tensor_copy(dec_sink[:, bg, :], dec_consts[:, 0:PAIRS]))
                step(nc.vector.tensor_scalar(neg_dec_sink[:], dec_sink[:], -1.0, None, ALU.mult))
                nc.vector.tensor_copy(vecs[:, KT:4 * KT + UT], banks[:, 4, 0:3 * KT + UT]).then_inc(vecs_ready, 1)
                dve.wait_ge(vecs_ready, 1)

            def decode_masks(bg):
                new = slice(WINDOW, NKEY)
                step(nc.vector.tensor_scalar(dec_pen[:, bg, new], dec_pen[:, 0, new], row_t[:, 1:2], 4.0 * bg,
                                             ALU.subtract, ALU.not_equal))
                step(nc.vector.tensor_scalar(dec_pen[:, bg, new], dec_pen[:, bg, new], MASKED, None, ALU.mult))
                step(nc.vector.tensor_scalar(dec_bias[:, bg, :], dec_bias[:, 0, :], row_t[:, 0:1], None, ALU.subtract))
                step(nc.vector.tensor_scalar(dec_pen[:, bg, 0:WINDOW], dec_bias[:, bg, 0:WINDOW], -float(WINDOW), MASKED,
                                             ALU.is_le, ALU.mult))
                step(nc.vector.tensor_tensor(dec_pen[:, bg, :], dec_pen[:, bg, :], dec_bias[:, bg, :], ALU.add))
                step(nc.vector.tensor_scalar(dec_bias[:, bg, new], dec_bias[:, bg, new], 0.0, MASKED, ALU.is_gt, ALU.mult))
                step(nc.vector.tensor_tensor(dec_pen[:, bg, new], dec_pen[:, bg, new], dec_bias[:, bg, new], ALU.add))

            def decode_queries():
                dve.wait_ge(q_zero, 1)
                dve.wait_ge(tile_read, 2 * U_PAIR0)
                for pair in range(PAIRS):
                    for half in range(2):
                        for odd in range(2):
                            w = GQA * DEC_T
                            dst = q_blocks[half * HD:(half + 1) * HD, :, half * w:(half + 1) * w].rearrange(
                                "d (b pair) (e odd t) -> d pair odd e b t", pair=PAIRS, odd=2, t=DEC_T)[:, pair, odd]
                            e = 4 * pair + 2 * half
                            src = qT[odd * HD:(odd + 1) * HD, e:e + 2, SEQ:T].rearrange("d e (b t) -> d e b t", t=DEC_T)
                            nc.vector.tensor_copy(dst, src).then_inc(q_ready, 1)

            def shift_scores(s):
                g, blk = divmod(s, TOK - 1)
                par, st = s % 2, s % 4
                lo = WINDOW if blk == 0 else 0
                dve.wait_ge(scores, s + 1)
                if s >= 2:
                    dve.wait_ge(probs_turned, 2 * (s - 1))
                if s >= 4:
                    dve.wait_ge(mixed_read, s - 3)
                for h in range(GQA):
                    slope = 2.0 ** (-8.0 * (g * GQA + h + 1) / HEADS)
                    nc.vector.scalar_tensor_tensor(
                        out=probs[:, par, h, lo:], in0=bias[:, lo:], scalar=slope,
                        in1=banks[:, 4 + h % 2, (h // 2) * 256 + lo:(h // 2) * 256 + 256],
                        op0=ALU.mult, op1=ALU.add).then_inc(scores_read, 1)
                dve.wait_ge(scores_read, GQA * (s + 1))
                step(nc.vector.tensor_reduce(stats[:, st, 4, :], probs[:, par, :, lo:], AX.X, ALU.max, negate=True))
                step(nc.vector.tensor_tensor(stats[:, st, 0, :], stats[:, st, 4, :],
                                             neg_sink[:, g * GQA:(g + 1) * GQA], ALU.min))
                nc.vector.tensor_tensor(stats[:, st, 1, :], sink_all[:, g * GQA:(g + 1) * GQA], stats[:, st, 0, :],
                                        ALU.add).then_inc(shift_ready, 1)

            def normalise(s):
                st = s % 4
                dve.wait_ge(exps, (GQA + 1) * (s + 1))
                step(nc.vector.tensor_tensor(stats[:, st, 5, :], stats[:, st, 2, :], stats[:, st, 3, :], ALU.add))
                step(nc.vector.reciprocal(stats[:, st, 6, :], stats[:, st, 5, :]))
                dve.wait_ge(mixed, s + 1)
                if s >= 2:
                    dve.wait_ge(rows_turned, s - 1)
                nc.vector.tensor_tensor(attn_tok[:, s % 2, :].rearrange("p (h d) -> p h d", h=GQA),
                                        banks[:, 7, 0:GQA * HD].rearrange("p (h d) -> p h d", h=GQA),
                                        stats[:, st, 6, :].unsqueeze(2).broadcast_to([P, GQA, HD]),
                                        ALU.mult).then_inc(mixed_read, 1)

            def rows_back(s):
                g, blk = divmod(s, TOK - 1)
                dve.wait_ge(rows_turned, s + 1)
                nc.vector.tensor_copy(qT[:, 2 * g:2 * g + 2, blk * P:(blk + 1) * P],
                                      banks[:, 7, 256:512].rearrange("p (a q) -> p a q", a=2)).then_inc(rows_read, 1)

            def decode_shift():
                dve.wait_ge(dec_scores, 1)
                for bg in range(2):
                    for pair in range(PAIRS):
                        step(nc.vector.scalar_tensor_tensor(
                            out=dec_probs[:, bg * PAIRS + pair, :], in0=dec_pen[:, bg, :], scalar=dec_slope[:, pair:pair + 1],
                            in1=banks[:, 4 + bg, pair * NKEY:(pair + 1) * NKEY], op0=ALU.mult, op1=ALU.add))
                step(nc.vector.tensor_reduce(dec_stats[:, 4, :], dec_probs, AX.X, ALU.max, negate=True))
                step(nc.vector.tensor_tensor(dec_stats[:, 0, :], dec_stats[:, 4, :],
                                             neg_dec_sink[:].rearrange("p b c -> p (b c)"), ALU.min))
                nc.vector.tensor_tensor(dec_stats[:, 1, :], dec_sink[:].rearrange("p b c -> p (b c)"), dec_stats[:, 0, :],
                                        ALU.add).then_inc(dec_shift, 1)

            def decode_normalise():
                dve.wait_ge(dec_exps, 5)
                step(nc.vector.tensor_tensor(dec_stats[:, 5, :], dec_stats[:, 2, :], dec_stats[:, 3, :], ALU.add))
                step(nc.vector.reciprocal(dec_stats[:, 6, :], dec_stats[:, 5, :]))
                nc.vector.tensor_tensor(dec_probs, dec_probs, dec_stats[:, 6, :].unsqueeze(2).broadcast_to([P, 4, NKEY]),
                                        ALU.mult).then_inc(dec_norm, 1)

            runs = [0]

            def pool_z(p):
                g = pool_order[p]
                w, e = POOL_WINDOWS[g], slice(2 * g, 2 * g + 2)
                run = run_bufs[g % 2]
                if g > 0:
                    runs[0] += g + 1
                    dve.wait_ge(run_ready, runs[0])
                else:
                    dve.wait_ge(z_ready, p)
                    dve.wait_ge(tile_read, 2 * IN_PAIRS)
                    step(nc.vector.tensor_tensor(run[:, :, 1:ROW], uT[:, e, 1:ROW], uT[:, e, 0:ROW - 1], ALU.add))
                dve.wait_ge(edge_ready, 1 + sum(w - 1 for w in POOL_WINDOWS))
                step(nc.vector.tensor_tensor(run[:, :, PAD:2 * PAD], run[:, :, PAD:2 * PAD],
                                             edge[:, g:g + 1, :].broadcast_to([P, 2, PAD]), ALU.mult))
                dve.wait_ge(u_turned, p + 1)
                nc.vector.scalar_tensor_tensor(out=uT[:, e, PAD:ROW], in0=run[:, :, PAD:ROW], scalar=1.0 / w,
                                               in1=uT[:, e, PAD:ROW], op0=ALU.mult, op1=ALU.subtract).then_inc(z_ready, 1)

            for j in range(IN_UNITS):
                if j % K_UNITS == K_UNITS - 1:
                    read_pair(j // K_UNITS)
                if 4 < j + 2 <= U_POOL:
                    split(j + 2)
                if j == K_UNITS:
                    dve.wait_ge(consts, 5 + 2 * GQA + PAIRS)
                    step(nc.vector.tensor_scalar(row_i[:, 1:2], row_i[:, 0:1], DEC_T - 1, None, ALU.bitwise_and))
                    step(nc.vector.tensor_scalar(row_i[:, 2:3], row_i[:, 0:1], 5, None, ALU.logical_shift_right))
                    step(nc.vector.tensor_copy(row_t[:], row_i[:, 1:3]))
                if j in (K_UNITS, K_UNITS + 1):
                    dve.wait_ge(bias_ready, 6)
                    decode_masks(K_UNITS + 1 - j)
                if j == 2 * K_UNITS:
                    dve.wait_ge(kv_turned, 1)
                    nc.vector.tensor_copy(kv_dec[:].rearrange("p b n -> p (b n)"), banks[0:ND, 6, :]).then_inc(kv_copied, 1)
                    nc.vector.tensor_copy(k_tok[:], banks[:, 7, 0:KVW]).then_inc(kv_copied, 1)
                    dve.wait_ge(tile_read, 2)
                    for half in range(2):
                        rows = slice(half * HD, (half + 1) * HD)
                        nc.vector.tensor_copy(k_new[rows], k_twice[rows, :, SEQ:T].rearrange(
                            "p (pair half) n -> p half pair n", half=2)[:, half]).then_inc(q_ready, 1)
                if j == 2 * K_UNITS + 2:
                    for r in range(2, 4):
                        dve.wait_ge(old_k_turned, r + 1)
                        nc.vector.tensor_copy(old_kT[:, 4 * r:4 * r + 4, :].rearrange("p a k -> p (a k)"),
                                              banks[:, 4 + r, :]).then_inc(old_k_dve, 1)
                    vectors()
                if j == 2 * K_UNITS + 3:
                    dve.wait_ge(state_turned, 1)
                    for r in range(2):
                        nc.vector.tensor_copy(
                            decode_part(uT[:, 4 * r:4 * r + 4, :])[:, :, :, 0:STATE],
                            banks[:, 6 + r, 0:4 * DEC_B * STATE].rearrange("p (e b s) -> p e b s", e=4, b=DEC_B)
                        ).then_inc(state_copied, 1)
                s = j - MIX_AT
                if 0 <= s < steps:
                    normalise(s)
                if j == U_PAIR0 * K_UNITS:
                    decode_queries()
                if 0 <= s < steps:
                    rows_back(s)
                if 0 <= j + 1 - SCORE_AT < steps:
                    shift_scores(j + 1 - SCORE_AT)
                if j == DEC_SCORE_AT - 1:
                    decode_shift()
                if j == DEC_SCORE_AT:
                    decode_normalise()
                if j == DEC_TURN_AT - 1:
                    dve.wait_ge(dec_turned, 1)
                    nc.vector.tensor_copy(dec_PT_new.rearrange("p a r -> p (a r)"), banks[0:ND, 7, :]).then_inc(dec_copied, 1)
                for p, at in enumerate(Z_AT):
                    if j == at:
                        pool_z(p)

            def z_low(p):
                src, hi, lo = z_parts(pool_order[p])
                for part in range(2):
                    dve.wait_ge(z_hi, 2 * p + part + 1)
                    nc.vector.tensor_tensor(lo[part], src[part], hi[part].bitcast(F32), ALU.subtract).then_inc(z_lo, 1)

            def mix_low(p):
                for nt in range(2):
                    m = 2 * pool_order[p] + nt
                    dve.wait_ge(mix_hi, 2 * p + nt + 1)
                    shape = "p (h t) -> p h t"
                    nc.vector.scalar_tensor_tensor(
                        out=acts_lo[:, QT + m, :].rearrange(shape, h=2), in0=slot((p % 2) * 2 + nt),
                        scalar=p_scale[:, m:m + 1], in1=acts_hi[:, QT + m, :].bitcast(F32).rearrange(shape, h=2),
                        op0=ALU.mult, op1=ALU.subtract).then_inc(tile_read, 1)

            z_low(0)
            z_low(1)
            split(U_POOL + 1)
            pool_z(len(pool_order) - 1)
            z_low(2)
            z_low(3)
            mix_low(0)
            mix_low(1)
            split(U_OUT)
            mix_low(2)
            mix_low(3)

            def out_pair(k, v, pair_k, pair_v, tile, count):
                for kq in range(K_UNITS):
                    split(k + kq + 1, v)
                for nt in range(2):
                    dve.wait_ge(sq_ready, count + nt + 1)
                    nc.vector.tensor_scalar(halves(x1T[:, tile(nt), :]), slot((pair_k % 2) * 2 + nt), 1.0, None,
                                            ALU.mult).then_inc(tile_read, 1)

            with dve.Fori(0, OUT_PAIRS // 2) as i:
                for b in range(2):
                    out_pair(U_OUT + b * K_UNITS, i * 2, P_OUT + b, i * 2,
                             lambda nt: bass.ds(i * 4 + 2 * b + nt, 1), i * 4 + 2 * b)

            row_scales(1, norm_scale)
            dve.wait_ge(scale_ready, 2)

            def second_low(kt):
                dve.wait_ge(h_hi, KT + kt + 1)
                nc.vector.scalar_tensor_tensor(out=acts_lo[:, kt, :], in0=x1T[:, kt, :], scalar=g_ffn[:, kt:kt + 1],
                                               in1=acts_hi[:, kt, :].bitcast(F32), op0=ALU.mult, op1=ALU.subtract).then_inc(h_lo, 1)

            for kt in range(KT):
                if kt % 2 == 0:
                    step(nc.vector.tensor_tensor(x1T[:, kt, :], x1T[:, kt, :], norm_scale[:], ALU.mult))
                else:
                    dve.wait_ge(normed, kt // 2 + 1)
                dve.wait_ge(x_turned, KT + kt + 1)
                nc.vector.scalar_tensor_tensor(out=x1T[:, kt, :], in0=x1T[:, kt, :], scalar=g_post[:, kt:kt + 1],
                                               in1=flat(2 * x_slot(kt), T), op0=ALU.mult, op1=ALU.add).then_inc(x1_ready, 1)
                if kt % UNIT_KT > 0:
                    second_low(kt - 1)
                if kt % UNIT_KT == UNIT_KT - 1:
                    second_low(kt)
                    split(U_FFN + kt // UNIT_KT + 1)
            split(U_FFN + 5)
            sums_by_token(2, banks[:, 0, SUMS_AT:])
            row_roots(2)
            split(U_FFN + 6)
            dve.wait_ge(spread, 3)
            nc.vector.tensor_copy(gemm_scale[:, 0:SEQ].rearrange("p (c t) -> p c t", c=TOK - 1), banks[:, 0:TOK - 1, H:H + P])
            nc.vector.tensor_copy(gemm_scale[:, SEQ:T], banks[:, 0, H + P:H + P + ND]).then_inc(scale_ready, 1)
            dve.wait_ge(scale_ready, 3)

            dve.wait_ge(y_clear, 1)

            def chunk(c, first=False, last=False):
                v = c * (CHUNK_UNITS // 4)
                for b in range(UP_PAIRS):
                    k = U_FFN + b * K_UNITS
                    for kq in range(K_UNITS):
                        if not first or b * K_UNITS + kq + 1 > 6:
                            split(k + kq + 1, v)
                    for nt in range(2):
                        j = 2 * b + nt
                        pair_ready(nt, k, v, P_FFN + b, c * CHUNK_PAIRS)
                        nc.vector.scalar_tensor_tensor(
                            out=relu_buf[:].rearrange("p (h t) -> p h t", h=2), in0=slot(((P_FFN + b) % 2) * 2 + nt),
                            scalar=0.0, in1=scale2, op0=ALU.max, op1=ALU.mult).then_inc(tile_read, 1)
                        dve.wait_ge(tile_read, num(2 * P_FFN + j + 1, c, CHUNK_TILES))
                        nc.vector.tensor_tensor(sq_tmp[:, 0:T], relu_buf[:], relu_buf[:], ALU.mult).then_inc(relu_sq, 1)
                        dve.wait_ge(mlp_hi_ready, num(j + 1, c, 2 * UP_PAIRS))
                        dve.wait_ge(relu_sq, num(j + 1, c, 2 * UP_PAIRS))
                        nc.vector.tensor_tensor(mlp_lo[:, j, :], sq_tmp[:, 0:T], mlp_hi[:, j, :].bitcast(F32),
                                                ALU.subtract).then_inc(mlp_lo_ready, 1)
                for n in range(OUT_PAIRS):
                    k = U_FFN + UP_PAIRS * K_UNITS + n
                    if not last or n + 1 < OUT_PAIRS:
                        split(k + 1, v)
                    for nt in range(2):
                        m = 2 * n + nt
                        if nt == 0:
                            dve.wait_ge(first_done, num(P_FFN + UP_PAIRS + n + 1, c, CHUNK_PAIRS))
                        else:
                            dve.wait_ge(unit_used, num(k + 1, v, 4))
                        acc = y_sum[:, m, :].rearrange("p (h t) -> p h t", h=2)
                        nc.vector.tensor_tensor(acc, acc, slot(((P_FFN + UP_PAIRS + n) % 2) * 2 + nt),
                                                ALU.add).then_inc(tile_read, 1)

            chunk(0, first=True)
            with dve.Fori(1, CHUNKS - 1) as c:
                chunk(c)
            chunk(CHUNKS - 1, last=True)

            row_scales(3, norm_scale)
            dve.wait_ge(scale_ready, 4)
            def finish_tiles(kg):
                for kt in range(4 * kg, 4 * kg + 4):
                    if kt in OWN_NORMED:
                        step(nc.vector.tensor_tensor(y_sum[:, kt, :], y_sum[:, kt, :], norm_scale[:], ALU.mult))
                    else:
                        dve.wait_ge(normed, KT // 2 + sum(i not in OWN_NORMED for i in range(kt + 1)))
                    nc.vector.scalar_tensor_tensor(out=x1T[:, kt, :], in0=y_sum[:, kt, :], scalar=g_last[:, kt:kt + 1],
                                                   in1=x1T[:, kt, :], op0=ALU.mult, op1=ALU.add).then_inc(y_ready, 1)

            def copy_out(kg):
                for o in range(kg * TOK, (kg + 1) * TOK):
                    if copier(o)[0] == 1:
                        dve.wait_ge(y_turned, o + 1)
                        if o >= 8:
                            dve.wait_ge(y_stored[o % 8], 16 * (o // 8))
                        r = tok_rows[o % TOK]
                        nc.vector.tensor_copy(w_raw[0:r].rearrange("p s n -> p (s n)")[:, (o % 8) * 512:(o % 8 + 1) * 512],
                                              banks[0:r, o % 8, :]).then_inc(y_copied[1], 1)

            for kg in range(KT // 4):
                finish_tiles(kg)
            copy_out(KT // 4 - 1)

        @block.tensor
        def _(pe):
            def turn_x(tok, kt, s):
                for c in range(TOK):
                    r = tok_rows[c]
                    ins = nc.tensor.transpose(flat(2 * s, T)[:, c * P:c * P + r], tok[0:r, c, kt * P:(kt + 1) * P],
                                              ident[0:r, 0:r])
                ins.then_inc(x_turned, 1)

            def spread_chunks(n, chunks):
                pe.wait_ge(rstd_ready, n + 1)
                for c in range(TOK):
                    r = tok_rows[c]
                    ins = nc.tensor.matmul(chunks(c)[:, 0:r], rstd[0:r, c:c + 1].broadcast_to([r, P]), ident[0:r, 0:r],
                                           start=True, stop=True)
                ins.then_inc(spread, 1)

            def spread_scales(n):
                spread_chunks(n, lambda c: flat(6, T)[:, c * P:c * P + tok_rows[c]])

            def turn_sums(n, at=banks[:, 6, :]):
                pe.wait_ge(sq_added, n * (KT - 1))
                pe.wait_ge(sq_ready, n * KT)
                last = sq_tmp[:, ((KT - 1) % 2) * T:((KT - 1) % 2 + 1) * T]
                for c in range(TOK):
                    r = tok_rows[c]
                    nc.tensor.matmul(at[0:r, c:c + 1], sq_sum[:, c * P:c * P + r], ones[:, 0:1], start=True, stop=False)
                    ins = nc.tensor.matmul(at[0:r, c:c + 1], last[:, c * P:c * P + r], ones[:, 0:1], start=False, stop=True)
                ins.then_inc(sums_turned, 1)

            def product(out, s, kk, nt, hi, lo, start, stop):
                cols = slice(kk * UNIT_N + nt * P, kk * UNIT_N + (nt + 1) * P)
                wh, wl = w_hi[:, s, cols], w_lo[:, s, cols]
                terms = [(wh, hi, start, False), (wh, lo, False, False), (wl, hi, False, stop)]
                for w, x, first, last in terms:
                    for h in range(2):
                        ins = nc.tensor.matmul(out[:, h, :], w, x[:, h * H:(h + 1) * H], start=first, stop=last)
                return ins

            def pair_tiles(k, v, pair_k, pair_v, units, rows_ready=None, between=None):
                for q in range(units):
                    u = k + q
                    pe.wait_ge(lo_split, num(u + 1, v, 4))
                    if rows_ready:
                        rows_ready(q)
                    for nt in range(2):
                        if q == 0 and (pair_k >= 2 or not isinstance(pair_v, int)):
                            pe.wait_ge(tile_read, num(2 * pair_k - 3 + nt, pair_v, 2))
                        for kk in range(UNIT_KT):
                            kt = q * UNIT_KT + kk
                            ins = product(slot((pair_k % 2) * 2 + nt), u % SPLIT_SLOTS, kk, nt, acts_hi[:, kt, :],
                                          acts_lo[:, kt, :], kt == 0, kt == units * UNIT_KT - 1)
                        if nt == 0:
                            if q == units - 1:
                                ins.then_inc(first_done, 1)
                            if between:
                                between(q, 0)
                    ins.then_inc(unit_used, 1)
                    if between:
                        between(q, 1)

            def tile_by_tile(u, pair, rows, q, half_way):
                for kk in range(UNIT_KT):
                    kt = q * UNIT_KT + kk
                    pe.wait_ge(h_lo, rows + kt + 1)
                    for nt in range(2):
                        if kt == 0 and nt == 1:
                            pe.wait_ge(h_lo, rows + 2)
                        if kt == 0 and pair >= 2:
                            pe.wait_ge(tile_read, 2 * pair - 3 + nt)
                        ins = product(slot((pair % 2) * 2 + nt), u % SPLIT_SLOTS, kk, nt, acts_hi[:, kt, :],
                                      acts_lo[:, kt, :], kt == 0, kt == KT - 1)
                        if nt == 0 and kt == KT - 1:
                            ins.then_inc(first_done, 1)
                    if kk == 1:
                        half_way(u)
                ins.then_inc(unit_used, 1)

            pe.wait_ge(consts, 6 + 2 * GQA + PAIRS)
            pe.wait_ge(vec_landed[0], 16)
            nc.tensor.transpose(banks[:, 0, 0:KT], pre_rows[:], ident[0:KT, 0:KT]).then_inc(pre_turned, 1)
            pe.wait_ge(pre_ready, 1)

            def first_turn(kt):
                if kt in (0, KT // 2):
                    for c in range(TOK):
                        pe.wait_ge(x_landed[kt // (KT // 2)][c], 16)
                if kt >= 4:
                    pe.wait_ge(h_lo, kt - 1)
                turn_x(x_tok, kt, x_slot(kt))

            for kt in range(UNIT_KT):
                first_turn(kt)

            def turn_new_keys():
                pe.wait_ge(tile_read, 2 * Q_PAIR0)
                for blk in range(TOK - 1):
                    for e in range(PAIRS):
                        nc.tensor.transpose(flat(4, 1024)[:, blk * KVW + e * P:blk * KVW + (e + 1) * P],
                                            vT[:, e, blk * P:(blk + 1) * P], ident[:])
                for g in range(KV_HEADS):
                    nc.tensor.transpose(banks[0:ND, 6, g * HD:(g + 1) * HD], k_twice[0:HD, g, SEQ:T], ident[0:HD, 0:HD])
                for e in range(PAIRS):
                    nc.tensor.transpose(banks[0:ND, 6, KVW + e * P:KVW + (e + 1) * P], vT[:, e, SEQ:T], ident[:])
                for g in range(KV_HEADS):
                    ins = nc.tensor.transpose(banks[:, 7, g * HD:(g + 1) * HD], k_twice[0:HD, g, SEQ - P:SEQ], ident[0:HD, 0:HD])
                ins.then_inc(kv_turned, 1)

            def turn_old_keys(r):
                for a in range(4):
                    b, pair = divmod(4 * r + a, PAIRS)
                    ins = nc.tensor.transpose(banks[:, 4 + r, a * P:(a + 1) * P], old_k[:, b, pair * P:(pair + 1) * P], ident[:])
                ins.then_inc(old_k_turned, 1)

            def turn_vectors():
                pe.wait_ge(consts, 7 + 2 * GQA + PAIRS)
                for i in range(1, 7):
                    pe.wait_ge(vec_landed[i], 16)
                pe.wait_ge(old_k_act, 2)
                n = 3 * KT + UT
                nc.tensor.transpose(banks[:, 4, 0:n], vec_rows, ident[0:n, 0:n])
                nc.tensor.matmul(banks[:, 5, 0:HEADS], ones[0:1, :], sink_row, start=True, stop=True)
                nc.tensor.matmul(banks[:, 5, HEADS:HEADS + PAIRS], head_rows, sink_hh, start=True, stop=True)
                nc.tensor.matmul(banks[:, 5, HEADS + PAIRS:HEADS + 2 * PAIRS], slope_row, slope_pair, start=True,
                                 stop=True).then_inc(vecs_turned, 1)

            def turn_state():
                n = DEC_B * STATE
                pe.wait_ge(state_landed, 16)
                pe.wait_ge(old_k_dve, 2)
                for e in range(UT):
                    ins = nc.tensor.transpose(banks[:, 6 + e // 4, (e % 4) * n:(e % 4 + 1) * n],
                                              state_tok[:, e * P:(e + 1) * P], ident[0:n, 0:n])
                ins.then_inc(state_turned, 1)

            def score(s):
                g, blk = divmod(s, TOK - 1)
                lo = WINDOW if blk == 0 else 0
                keys = slice(max(blk - 1, 0) * P, (blk + 1) * P)
                if s == 0:
                    pe.wait_ge(vecs_ready, 1)
                else:
                    pe.wait_ge(scores_read, GQA * s)
                pe.wait_ge(tile_read, 2 * (Q_PAIR0 + g) + 2)
                for h in range(GQA):
                    rows = slice((h % 2) * HD, (h % 2 + 1) * HD)
                    ins = nc.tensor.matmul(banks[:, 4 + h % 2, (h // 2) * 256 + lo:(h // 2) * 256 + 256],
                                           qT[rows, 2 * g + h // 2, blk * P:(blk + 1) * P], k_twice[rows, g, keys],
                                           start=True, stop=True)
                ins.then_inc(scores, 1)

            def turn_probs(s, r):
                parts = 1 if s % (TOK - 1) == 0 else 2
                if r == 0:
                    pe.wait_ge(exps, (GQA + 1) * (s + 1))
                if s == 0 and r == 0:
                    pe.wait_ge(state_copied, 2)
                else:
                    pe.wait_ge(probs_copied, 2 * s + r)
                for hh in range(2):
                    for half in range(parts):
                        at = (2 - parts + half) * WINDOW
                        i = hh * parts + half
                        ins = nc.tensor.transpose(banks[:, 6, i * P:(i + 1) * P], probs[:, s % 2, 2 * r + hh, at:at + P], ident[:])
                ins.then_inc(probs_turned, 1)

            def mix(s):
                g, blk = divmod(s, TOK - 1)
                parts = 1 if blk == 0 else 2
                pe.wait_ge(probs_copied, 2 * s + 2)
                if s > 0:
                    pe.wait_ge(rows_read, s)
                for h in range(GQA):
                    for half in range(parts):
                        i = (h % 2) * parts + half
                        ins = nc.tensor.matmul(banks[:, 7, h * HD:(h + 1) * HD], probs_T[:, h // 2, i * P:(i + 1) * P],
                                               v_tok[:, blk - parts + 1 + half, g * HD:(g + 1) * HD],
                                               start=half == 0, stop=half == parts - 1)
                ins.then_inc(mixed, 1)

            def turn_rows(s):
                pe.wait_ge(mixed_read, s + 1)
                for a in range(2):
                    ins = nc.tensor.transpose(banks[:, 7, 256 + a * P:256 + (a + 1) * P], attn_tok[:, s % 2, a * P:(a + 1) * P], ident[:])
                ins.then_inc(rows_turned, 1)

            def decode_scores():
                pe.wait_ge(q_ready, 2 + 4 * PAIRS)
                pe.wait_ge(scores_read, GQA * steps)
                for b in range(DEC_B):
                    rows = slice(32 * (b % 4), 32 * (b % 4) + 32)
                    for pair in range(PAIRS):
                        out = banks[rows, 4 + b // 4, pair * NKEY:(pair + 1) * NKEY]
                        i = b * PAIRS + pair
                        nc.tensor.matmul(out[:, 0:WINDOW], q_blocks[:, i, :], old_kT[:, i, :], start=True, stop=True)
                        ins = nc.tensor.matmul(out[:, WINDOW:NKEY], q_blocks[:, i, :], k_new[:, pair, :], start=True, stop=True)
                ins.then_inc(dec_scores, 1)

            def turn_decode_probs():
                pe.wait_ge(dec_norm, 1)
                pe.wait_ge(probs_copied, 2 * steps)
                pe.wait_ge(rows_read, steps)
                for ck in range(4):
                    nc.tensor.transpose(banks[:, 6, ck * P:(ck + 1) * P], dec_probs[:, ck, 0:WINDOW], ident[:])
                    ins = nc.tensor.transpose(banks[0:ND, 7, ck * P:(ck + 1) * P], dec_probs[:, ck, WINDOW:NKEY], ident[:])
                ins.then_inc(dec_turned, 1)

            def decode_mix():
                pe.wait_ge(dec_copied, 2)
                pe.wait_ge(cache_landed[1], 16)
                for b in range(DEC_B):
                    for pair in range(PAIRS):
                        ck = (b // 4) * PAIRS + pair
                        out = banks[:, 4, (b * PAIRS + pair) * 32:(b * PAIRS + pair + 1) * 32]
                        rows = slice(32 * (b % 4), 32 * (b % 4) + 32)
                        nc.tensor.matmul(out, old_v[:, b, pair * P:(pair + 1) * P], dec_PT[:, ck, rows], start=True, stop=False)
                        ins = nc.tensor.matmul(out, kv_dec[:, 1, pair * P:(pair + 1) * P], dec_PT_new[:, ck, rows], start=False, stop=True)
                ins.then_inc(dec_mixed, 1)

            def turn_new_rows(p):
                pe.wait_ge(tile_read, 2 * (U_PAIR0 + p) + 2)
                if p == 0:
                    pe.wait_ge(dec_shift, 1)
                else:
                    pe.wait_ge(u_copied, 2 * p)
                for i in range(2):
                    e = 2 * pool_order[p] + i
                    nc.tensor.transpose(banks[0:STATE, 5, i * P:(i + 1) * P], uT[:, e, PAD + SEQ - STATE:PAD + SEQ], ident[:])
                    ins = nc.tensor.transpose(banks[0:ND, 5, (2 + i) * P:(3 + i) * P],
                                              u_new[:, p % 2, i, :], ident[:])
                ins.then_inc(u_turned, 1)

            def mid(j):
                if j + 1 < K_UNITS:
                    first_turn(4 + 4 * j)
                    first_turn(5 + 4 * j)
                if 0 <= j - ROWS_AT < steps:
                    turn_rows(j - ROWS_AT)
                if 0 <= j - (TURN_AT + 1) < steps:
                    turn_probs(j - (TURN_AT + 1), 1)
                if 0 <= j - SCORE_AT < steps:
                    score(j - SCORE_AT)
                if j == DEC_SCORE_AT:
                    decode_scores()
                if j == DEC_TURN_AT:
                    turn_decode_probs()
                if j == DEC_MIX_AT:
                    decode_mix()
                for p, at in enumerate(U_TURN_AT):
                    if j == at:
                        turn_new_rows(p)

            def after(j):
                if j + 1 < K_UNITS:
                    first_turn(6 + 4 * j)
                    first_turn(7 + 4 * j)
                if j == K_UNITS - 1:
                    spread_scales(0)
                if j == 2 * K_UNITS:
                    turn_new_keys()
                if j == 2 * K_UNITS + 1:
                    pe.wait_ge(kv_copied, 3)
                    pe.wait_ge(cache_landed[0], 16)
                    turn_old_keys(0)
                    turn_old_keys(1)
                if j == 2 * K_UNITS + 2:
                    turn_old_keys(2)
                    turn_old_keys(3)
                    turn_vectors()
                if j == 2 * K_UNITS + 3:
                    turn_state()
                if 0 <= j - MIX_AT < steps:
                    mix(j - MIX_AT)
                if 0 <= j - TURN_AT < steps:
                    turn_probs(j - TURN_AT, 0)

            for j in range(IN_UNITS):
                pair, q = divmod(j, K_UNITS)
                pe.wait_ge(lo_split, j + 1)
                if pair == 0:
                    tile_by_tile(j, 0, 0, q, mid)
                    after(j)
                    continue
                for nt in range(2):
                    if j == K_UNITS and nt == 1:
                        pe.wait_ge(scale_ready, 1)
                    if q == 0 and pair >= Q_PAIR0:
                        pe.wait_ge(tile_read, 2 * pair - 1 + nt)
                    for kk in range(UNIT_KT):
                        kt = q * UNIT_KT + kk
                        ins = product(slot((pair * 2 if pair < Q_PAIR0 else 0) + nt), j % SPLIT_SLOTS, kk, nt, acts_hi[:, kt, :],
                                      acts_lo[:, kt, :], kt == 0, kt == KT - 1)
                    if nt == 0:
                        if q == K_UNITS - 1:
                            ins.then_inc(first_done, 1)
                        mid(j)
                ins.then_inc(unit_used, 1)
                after(j)
            turn_new_rows(len(pool_order) - 1)

            for p, g in enumerate(pool_order):
                u = U_POOL + p // 2
                if p % 2 == 0:
                    pe.wait_ge(lo_split, u + 1)
                pe.wait_ge(z_lo, 2 * p + 2)
                if p == 1:
                    pe.wait_ge(u_copied, 2 * len(pool_order))
                    pe.wait_ge(dec_hi, 2 * GQA)
                for nt in range(2):
                    pe.wait_ge(tile_read, 2 * (P_POOL + p) - (1 if p == 0 else 3) + nt)
                    for kk in range(2):
                        e = QT + 2 * g + kk
                        ins = product(slot((p % 2) * 2 + nt), u % SPLIT_SLOTS, (g % 2) * 2 + kk, nt, acts_hi[:, e, :],
                                      acts_lo[:, e, :], kk == 0, kk == 1)
                    if nt == 0:
                        ins.then_inc(first_done, 1)
                ins.then_inc(even_group_done if p % 2 == 0 else unit_used, 1)

            def mixer_rows_ready(q):
                if q < 2:
                    pe.wait_ge(attn_lo, q + 1)
                else:
                    pe.wait_ge(tile_read, 2 * P_OUT)

            with pe.Fori(0, OUT_PAIRS // 2) as i:
                for b in range(2):
                    pair_tiles(U_OUT + b * K_UNITS, i * 2, P_OUT + b, i * 2, K_UNITS, mixer_rows_ready)

            for c in range(TOK):
                pe.wait_ge(x2_landed[c], 16)
            for kt in range(3):
                pe.wait_ge(tile_read, 2 * P_FFN - 3 + kt)
                turn_x(x_tok2, kt, x_slot(kt))
            pe.wait_ge(tile_read, 2 * P_FFN)
            turn_sums(1)
            spread_scales(1)

            def second_turn(kt):
                if kt == 3:
                    pe.wait_ge(scale_ready, 2)
                if kt >= 4:
                    pe.wait_ge(x1_ready, kt - 1)
                turn_x(x_tok2, kt, x_slot(kt))

            second_turn(3)

            def down(c, v):
                for n in range(OUT_PAIRS):
                    u = U_FFN + UP_PAIRS * K_UNITS + n
                    pair = P_FFN + UP_PAIRS + n
                    pe.wait_ge(lo_split, num(u + 1, v, 4))
                    order = [(kk, nt) for kk in range(UNIT_KT) for nt in range(2)] if n == 0 else [
                        (kk, nt) for nt in range(2) for kk in range(UNIT_KT)]
                    for kk, nt in order:
                        if n == 0 and nt == 0:
                            pe.wait_ge(mlp_lo_ready, num(kk + 1, c, 2 * UP_PAIRS))
                        if kk == 0:
                            pe.wait_ge(tile_read, num(2 * pair - 3 + nt, c, CHUNK_TILES))
                        ins = product(slot((pair % 2) * 2 + nt), u % SPLIT_SLOTS, kk, nt, mlp_hi[:, kk, :],
                                      mlp_lo[:, kk, :], kk == 0, kk == UNIT_KT - 1)
                        if kk == UNIT_KT - 1 and nt == 0:
                            ins.then_inc(first_done, 1)
                    ins.then_inc(unit_used, 1)

            def turn_half(q, half):
                kt = 4 + 4 * q + 2 * half
                if kt < KT:
                    second_turn(kt)
                    second_turn(kt + 1)

            def scales_between(q, nt):
                if q == 0 and nt == 1:
                    spread_chunks(2, scale_chunk)

            for q in range(K_UNITS):
                pe.wait_ge(lo_split, U_FFN + q + 1)
                tile_by_tile(U_FFN + q, P_FFN, KT, q, lambda u: turn_half(q, 0))
                turn_half(q, 1)
            turn_sums(2, banks[:, 0, SUMS_AT:])
            pair_tiles(U_FFN + K_UNITS, 0, P_FFN + 1, 0, K_UNITS, None, scales_between)
            down(0, 0)
            with pe.Fori(1, CHUNKS) as c:
                v = c * (CHUNK_UNITS // 4)
                for b in range(UP_PAIRS):
                    pair_tiles(U_FFN + b * K_UNITS, v, P_FFN + b, c * CHUNK_PAIRS, K_UNITS)
                down(c, v)

            pe.wait_ge(tile_read, 2 * (P_FFN + CHUNKS * CHUNK_PAIRS))
            turn_sums(3)
            spread_scales(3)
            pe.wait_ge(scale_ready, 4)
            for kg in range(KT // 4):
                for a in range(4):
                    pe.wait_ge(y_ready, 4 * kg + a + 1)
                    for c in range(TOK):
                        o = kg * TOK + c
                        r = tok_rows[c]
                        if o >= 8 and a == 0:
                            who, count = copier(o - 8)
                            pe.wait_ge(y_copied[who], count)
                        ins = nc.tensor.transpose(banks[0:r, o % 8, a * P:(a + 1) * P], x1T[:, 4 * kg + a, c * P:c * P + r], ident[:])
                        if a == 3:
                            ins.then_inc(y_turned, 1)


_INS = ['x_prompt', 'x_sample', 'cache_k', 'cache_v', 'state_pool', 'w_in', 'w_out', 'w_pool', 'pool_scale', 'attn_sinks',
        'g_pre_mix', 'g_post_mix', 'g_pre_ffn', 'g_post_ffn', 'w_up', 'w_down']


def kernel(**inputs):
    import numpy as np
    import concourse.bacc as bacc
    from concourse.bass_utils import run_bass_kernel_spmd

    nc = bacc.Bacc("TRN2", target_bir_lowering=False, num_devices=1)
    arrays, args = {}, []
    for name in _INS:
        a = np.ascontiguousarray(inputs[name])
        arrays[f"in_{name}"] = a
        args.append(nc.dram_tensor(f"in_{name}", a.shape, mybir.dt.from_np(a.dtype), kind="ExternalInput").ap())
    depth, dec_b, window, kv_heads, hd = inputs['cache_k'].shape
    _, _, state, pool_w = inputs['state_pool'].shape
    prompt = (depth, 1, window, kv_heads, hd)
    shapes = [inputs['x_prompt'].shape, inputs['x_sample'].shape, prompt, prompt, (depth, 1, state, pool_w),
              inputs['cache_k'].shape, inputs['cache_v'].shape, inputs['state_pool'].shape]
    for i, shape in enumerate(shapes):
        args.append(nc.dram_tensor(f"out_{i}", tuple(shape), F32, kind="ExternalOutput").ap())
    hybrid_decoder(nc, *args)
    r = run_bass_kernel_spmd(nc, [arrays], core_ids=[0])
    return tuple(r.results[0][f"out_{i}"] for i in range(len(shapes)))
```
